# Optimizing a Trainium2 kernel written in Bass

```python
import jax, jax.numpy as jnp
from jax import lax
import numpy as np

D_MODEL = 1024
BATCH = 1
SEQ = 512
DEPTH = 2

CHUNK = 64
D_FF = 2816
SSD_WIDTH = D_MODEL // 2
SSD_HEAD_DIM = 64
SSD_HEADS = SSD_WIDTH // SSD_HEAD_DIM
SSD_GROUPS = 2
SSD_STATE = 64
SSD_CONV = 4
SSD_CONV_DIM = SSD_WIDTH + 2 * SSD_GROUPS * SSD_STATE
HG_WIDTH = D_MODEL - SSD_WIDTH
HG_HEADS = 8
HG_VAL_HEAD = HG_WIDTH // HG_HEADS
HG_KEY_HEAD = 64
HG_KEY_DIM = HG_HEADS * HG_KEY_HEAD
HG_CHUNK = 16
D_MIX = SSD_WIDTH + HG_WIDTH
D_PROJ = SSD_WIDTH + SSD_CONV_DIM + SSD_HEADS + 2 * HG_KEY_DIM + 2 * HG_WIDTH
NORM_EPS = 1e-6

kernel_name = "hymba_ssd_hgrn2_macaron_trunk"

def rmsnorm(x, w):
    xf = x.astype(jnp.float32)
    xf = xf * lax.rsqrt(jnp.mean(xf * xf, axis=-1, keepdims=True) + NORM_EPS)
    return (xf * w.astype(jnp.float32)).astype(x.dtype)

def swiglu(h, w_gate, w_up, w_down):
    return (jax.nn.silu(h @ w_gate) * (h @ w_up)) @ w_down

def chunk_state_scan(decay, contrib):
    decay_t = jnp.moveaxis(decay, 1, 0)
    contrib_t = jnp.moveaxis(contrib, 1, 0)

    def step(state, inp):
        d, c = inp
        return d * state + c, state

    _, prev = lax.scan(step, jnp.zeros_like(contrib_t[0]), (decay_t, contrib_t))
    return jnp.moveaxis(prev, 0, 1)

def causal_depthwise_conv(u, w, b):
    L = u.shape[1]
    upad = jnp.pad(u, ((0, 0), (SSD_CONV - 1, 0), (0, 0)))
    out = sum(upad[:, k:k + L] * w[k] for k in range(SSD_CONV))
    return out + b

def ssd_mixer(z, xbc_raw, dt_raw, conv_w, conv_b, dt_bias, a_log, d_skip, norm_w):
    Bsz, L, _ = z.shape
    nc = L // CHUNK
    R = SSD_HEADS // SSD_GROUPS
    xbc = jax.nn.silu(causal_depthwise_conv(xbc_raw, conv_w, conv_b))
    xs, Bm, Cm = jnp.split(xbc, [SSD_WIDTH, SSD_WIDTH + SSD_GROUPS * SSD_STATE], axis=-1)
    dt = jax.nn.softplus(dt_raw + dt_bias)
    A = -jnp.exp(a_log).reshape(SSD_GROUPS, R)
    xs = xs.reshape(Bsz, nc, CHUNK, SSD_GROUPS, R, SSD_HEAD_DIM)
    Bm = Bm.reshape(Bsz, nc, CHUNK, SSD_GROUPS, SSD_STATE)
    Cm = Cm.reshape(Bsz, nc, CHUNK, SSD_GROUPS, SSD_STATE)
    dt = dt.reshape(Bsz, nc, CHUNK, SSD_GROUPS, R)
    x_dt = xs * dt[..., None]
    a_cum = jnp.cumsum(dt * A, axis=2)
    causal = jnp.tril(jnp.ones((CHUNK, CHUNK), dtype=bool))[None, None, :, :, None, None]
    seg = a_cum[:, :, :, None] - a_cum[:, :, None, :]
    decay_ts = jnp.where(causal, jnp.exp(jnp.where(causal, seg, 0.0)), 0.0)
    cb = jnp.einsum('bctgn,bcsgn->bctsg', Cm, Bm)
    y_intra = jnp.einsum('bctsg,bctsgr,bcsgrp->bctgrp', cb, decay_ts, x_dt)
    decay_end = jnp.exp(a_cum[:, :, -1:] - a_cum)
    contrib = jnp.einsum('bcsgn,bcsgr,bcsgrp->bcgrpn', Bm, decay_end, x_dt)
    chunk_decay = jnp.exp(a_cum[:, :, -1])[..., None, None]
    s_prev = chunk_state_scan(chunk_decay, contrib)
    y_inter = jnp.einsum('bctgn,bcgrpn,bctgr->bctgrp', Cm, s_prev, jnp.exp(a_cum))
    y = y_intra + y_inter + d_skip.reshape(SSD_GROUPS, R)[:, :, None] * xs
    y = y.reshape(Bsz, L, SSD_WIDTH) * jax.nn.silu(z)
    yg = y.reshape(Bsz, L, SSD_GROUPS, SSD_WIDTH // SSD_GROUPS)
    yg = yg * lax.rsqrt(jnp.mean(yg * yg, axis=-1, keepdims=True) + NORM_EPS)
    return yg.reshape(Bsz, L, SSD_WIDTH) * norm_w

def hgrn2_mixer(q_raw, f_raw, i_raw, g_raw, lb, norm_w):
    Bsz, L, _ = q_raw.shape
    nc = L // HG_CHUNK
    kshp = (Bsz, nc, HG_CHUNK, HG_HEADS, HG_KEY_HEAD)
    lbh = lb.reshape(HG_HEADS, HG_KEY_HEAD)
    a = f_raw.reshape(kshp)
    q = jax.nn.silu(q_raw).reshape(kshp)
    f = lbh + (1.0 - lbh) * jax.nn.sigmoid(a)
    logf = jnp.log(f)
    k = (1.0 - lbh) * jax.nn.sigmoid(-a)
    v = i_raw.reshape(Bsz, nc, HG_CHUNK, HG_HEADS, HG_VAL_HEAD)
    b = jnp.cumsum(logf, axis=2)
    b_last = b[:, :, -1:]
    b_ref = b[:, :, HG_CHUNK // 2 - 1:HG_CHUNK // 2]
    qe_rel = q * jnp.exp(b - b_ref)
    ke_rel = k * jnp.exp(b_ref - b)
    kd = k * jnp.exp(b_last - b)
    mask = jnp.tril(jnp.ones((HG_CHUNK, HG_CHUNK), dtype=bool))
    scores = jnp.einsum('bcthd,bcshd->bchts', qe_rel, ke_rel)
    scores = jnp.where(mask, scores, 0.0)
    o_intra = jnp.einsum('bchts,bcshv->bcthv', scores, v)
    contrib = jnp.einsum('bcshd,bcshv->bchdv', kd, v)
    decay = jnp.exp(b_last[:, :, 0])[..., None]
    s_prev = chunk_state_scan(decay, contrib)
    o_inter = jnp.einsum('bcthd,bchdv->bcthv', q * jnp.exp(b), s_prev)
    o = (o_intra + o_inter).reshape(Bsz, L, HG_HEADS, HG_VAL_HEAD)
    o = o * lax.rsqrt(jnp.mean(o * o, axis=-1, keepdims=True) + NORM_EPS) * norm_w
    o = o * jax.nn.silu(g_raw.reshape(Bsz, L, HG_HEADS, HG_VAL_HEAD))
    return o.reshape(Bsz, L, HG_WIDTH)

def setup_inputs(seed: int = 0) -> dict:
    key = jax.random.key(seed)
    ks = jax.random.split(key, 24)
    f32 = jnp.float32

    def nrm(k, shape, fan_in):
        return jax.random.normal(k, shape, f32) * (fan_in ** -0.5)

    def gain(k, shape):
        return 1.0 + 0.05 * jax.random.normal(k, shape, f32)

    u = jax.random.uniform(ks[11], (DEPTH, SSD_HEADS), f32)
    dt0 = jnp.exp(u * (jnp.log(0.1) - jnp.log(0.001)) + jnp.log(0.001))
    dt_bias = dt0 + jnp.log(-jnp.expm1(-dt0))
    return {
        "x": jax.random.normal(ks[0], (BATCH, SEQ, D_MODEL), f32),
        "ffn1_norm": gain(ks[1], (DEPTH, D_MODEL)),
        "ffn1_w_gate": nrm(ks[2], (DEPTH, D_MODEL, D_FF), D_MODEL),
        "ffn1_w_up": nrm(ks[3], (DEPTH, D_MODEL, D_FF), D_MODEL),
        "ffn1_w_down": nrm(ks[4], (DEPTH, D_FF, D_MODEL), D_FF),
        "mix_norm": gain(ks[5], (DEPTH, D_MODEL)),
        "w_in": nrm(ks[6], (DEPTH, D_MODEL, D_PROJ), D_MODEL),
        "ssd_conv_w": nrm(ks[7], (DEPTH, SSD_CONV, SSD_CONV_DIM), SSD_CONV),
        "ssd_conv_b": 0.02 * jax.random.normal(ks[8], (DEPTH, SSD_CONV_DIM), f32),
        "ssd_dt_bias": dt_bias,
        "ssd_a_log": jnp.log(jax.random.uniform(ks[9], (DEPTH, SSD_HEADS), f32, 1.0, 16.0)),
        "ssd_d": gain(ks[10], (DEPTH, SSD_HEADS)),
        "ssd_norm_w": gain(ks[12], (DEPTH, SSD_WIDTH)),
        "hg_lb_logits": 0.5 * jax.random.normal(ks[13], (DEPTH, HG_KEY_DIM), f32),
        "hg_norm_w": gain(ks[14], (DEPTH, HG_VAL_HEAD)),
        "w_out": nrm(ks[15], (DEPTH, D_MIX, D_MODEL), D_MIX),
        "ffn2_norm": gain(ks[16], (DEPTH, D_MODEL)),
        "ffn2_w_gate": nrm(ks[17], (DEPTH, D_MODEL, D_FF), D_MODEL),
        "ffn2_w_up": nrm(ks[18], (DEPTH, D_MODEL, D_FF), D_MODEL),
        "ffn2_w_down": nrm(ks[19], (DEPTH, D_FF, D_MODEL), D_FF),
        "final_norm": gain(ks[20], (D_MODEL,)),
    }

def reference(x, ffn1_norm, ffn1_w_gate, ffn1_w_up, ffn1_w_down, mix_norm, w_in,
              ssd_conv_w, ssd_conv_b, ssd_dt_bias, ssd_a_log, ssd_d, ssd_norm_w,
              hg_lb_logits, hg_norm_w, w_out, ffn2_norm, ffn2_w_gate, ffn2_w_up,
              ffn2_w_down, final_norm):
    f32 = jnp.float32
    lb_p = jax.nn.softmax(hg_lb_logits.astype(f32), axis=0)
    lower_bounds = jnp.cumsum(lb_p, axis=0) - lb_p[0]
    split_idx = list(np.cumsum([SSD_WIDTH, SSD_CONV_DIM, SSD_HEADS,
                                HG_KEY_DIM, HG_KEY_DIM, HG_WIDTH])[:])
    for l in range(DEPTH):
        x = x + 0.5 * swiglu(rmsnorm(x, ffn1_norm[l]), ffn1_w_gate[l], ffn1_w_up[l], ffn1_w_down[l])
        h = rmsnorm(x, mix_norm[l])
        proj = (h @ w_in[l]).astype(f32)
        z, xbc, dt_raw, q_raw, f_raw, i_raw, g_raw = jnp.split(proj, split_idx, axis=-1)
        y_ssd = ssd_mixer(z, xbc, dt_raw, ssd_conv_w[l].astype(f32), ssd_conv_b[l].astype(f32),
                          ssd_dt_bias[l].astype(f32), ssd_a_log[l].astype(f32),
                          ssd_d[l].astype(f32), ssd_norm_w[l].astype(f32))
        y_hg = hgrn2_mixer(q_raw, f_raw, i_raw, g_raw, lower_bounds[l], hg_norm_w[l].astype(f32))
        y = jnp.concatenate([y_ssd, y_hg], axis=-1).astype(x.dtype)
        x = x + y @ w_out[l]
        x = x + 0.5 * swiglu(rmsnorm(x, ffn2_norm[l]), ffn2_w_gate[l], ffn2_w_up[l], ffn2_w_down[l])
    return rmsnorm(x, final_norm)


_drawn_inputs = setup_inputs


def setup_inputs(seed=0):
    import zlib

    import numpy as np

    out = dict(_drawn_inputs(seed))
    spreads = {}
    factors = {'ssd_conv_b': 2.851}
    for name, (base, spread) in spreads.items():
        noise = np.random.default_rng([zlib.crc32(name.encode()), seed]).standard_normal(out[name].shape)
        drawn = base * np.exp(spread * noise) if base else spread * noise
        out[name] = __import__('jax').numpy.asarray(drawn.astype(out[name].dtype))
    for name, factor in factors.items():
        out[name] = (out[name] * factor).astype(out[name].dtype)
    return out
```

```python
import numpy as np
import concourse.bass as bass
from concourse import mybir
from concourse.alu_op_type import AluOpType as ALU
from contextlib import ExitStack

F32 = mybir.dt.float32
F32R = mybir.dt.float32r
I32 = mybir.dt.int32
ACT = mybir.ActivationFunctionType
AX = mybir.AxisListType

P = 128
DEPTH = 2
T = 512
TC = T // P
D = 1024
KD = D // P
FF = 2816
NJ = FF // P
SSD_W = 512
GN = 128
NP = 4
HALF = 64
CH = 16
NCC = T // CH
CREF = CH // 2 - 1
EPS = 1e-6
BIG = 1e38
MAGIC = float(0x5F3759DF)

NS = 4
BW = KD * P
UP_BLOCKS = 2 * NJ
DN_PIECES = [(0, 8), (8, 15), (15, 22)]
DN_BLOCKS = KD * len(DN_PIECES)
PROJ = ([("f", p) for p in range(NP)] + [("dt", 0), ("B", 0), ("C", 0)]
        + [(k, p) for p in range(NP) for k in ("q", "i")]
        + [("g", 0), ("g", 1)]
        + [(k, p) for p in range(NP) for k in ("xs", "z")]
        + [("g", 2), ("g", 3)])
NPROJ = len(PROJ)
AT = {kp: n for n, kp in enumerate(PROJ)}
PBLOCKS = []
for _n, (_kind, _) in enumerate(PROJ):
    PBLOCKS += [(_n, 0, 4), (_n, 4, 8)] if _kind == "B" else [(_n, 0, 8)]
MIX0 = UP_BLOCKS + DN_BLOCKS
OUT0 = MIX0 + len(PBLOCKS)
FFN2 = OUT0 + KD
W = FFN2 + UP_BLOCKS + DN_BLOCKS
assert W % NS == 0 and MIX0 % NS == 0 and FFN2 % NS == 0
LAST_BLOCK = {n: MIX0 + i for i, (n, _, _) in enumerate(PBLOCKS)}

WN = 0
CW = WN + 3 * KD
CB = CW + 6 * 4
SN = CB + 6
DC = SN + NP
HN = DC + NP
DTB = HN + 1
ALOG = DTB + 1
NIN = ALOG + 1
LB = NIN
OLB = LB + NP
NEGA = OLB + NP
NCOL = NEGA + 1
CONV_B, CONV_C = 4, 5

TANHS = ([("cv", "B"), ("cv", "C")] + [("q", p) for p in range(NP)] + [("g", 0), ("g", 1)]
         + [x for p in range(NP) for x in (("cv", p), ("z", p))] + [("g", 2), ("g", 3)])
DVE_STEPS = 150
CONVS = ["B", "C", 0, 1, 2, 3]


class Event:

    def __init__(self, sem, per=0, before=0, credit=0):
        self.sem, self.per, self.first = sem, per, before + credit + 1

    def upto(self, l, k):
        return l * self.per + (k + self.first)


class Steps:

    def __init__(self, eng, sem):
        self.eng, self.sem, self.base, self.n = eng, sem, 0, 0

    def did(self, ins):
        ins.then_inc(self.sem, 1)
        self.n += 1

    def settle(self):
        self.eng.wait_ge(self.sem, self.base + self.n)


def trunk_kernel(nc, x_in, cols, first_norm, logits, up1, dn1, mix, dtw, up2, dn2, out):
    ctx = ExitStack()
    with ctx:
        def sb(name, shape, dt=F32, at=ctx):
            return at.enter_context(nc.sbuf_tensor(name, shape, dt))

        def ev(name, per=0, before=0, credit=0):
            return Event(ctx.enter_context(nc.semaphore(name)), per, before, credit)

        x = sb("x", [P, KD, T])
        hhi = sb("hhi", [P, KD, T], F32R)
        hlo = sb("hlo", [P, KD, T], F32R)
        raw = sb("raw", [P, NS, BW])
        whi = sb("whi", [P, NS, BW], F32R)
        wlo = sb("wlo", [P, NS, BW], F32R)
        r = sb("r", [P, T])
        t1 = sb("t1", [P, T])
        acc = sb("acc", [P, T])
        sq = sb("sq", [P, T])
        g2 = sb("g2", [P, 2, T])
        u2 = sb("u2", [P, 2, T])
        par = sb("par", [P, NCOL])
        par_all = sb("par_all", [P, DEPTH, NCOL])
        first = sb("first", [P, KD])
        lg = sb("lg", [P, DEPTH, NP])
        lt = sb("lt", [P, 3, NP])
        spare = sb("spare", [1, 1])
        ident = sb("ident", [P, P])
        ones = sb("ones", [P, P])
        causal = sb("causal", [P, P])
        block16 = sb("block16", [P, P])
        keep16 = sb("keep16", [P, T])
        parity = sb("parity", [P, 2])
        par8 = sb("par8", [P, 2, 4])
        headsum = sb("headsum", [P, NP * 8])

        REGION = 27 * 1024 + 256 + 62 * 1024
        arena = sb("arena", [P, REGION // 4])
        base = nc.sbuf_base - REGION

        def place(name, shape, kib, dt=F32, start=0):
            assert start + kib * 1024 + 4 * int(np.prod(shape[1:])) <= REGION, name
            return nc.alloc_sbuf_tensor_at(name, shape, dt, offset=base + start + int(kib * 1024))

        ahi = place("ahi", [P, NJ, T], 0, F32R)
        alo = place("alo", [P, NJ, T], 44, F32R)
        stage = place("stage", [P, TC, D], 0)
        ont = place("ont", [P, KD, T], 16)
        b = place("b", [P, NP, T], 0)
        cf = place("cf", [P, T], 8)
        bt = place("bt", [P, TC, P], 10)
        cbm = place("cbm", [P, 2, TC, P], 12)
        acb = place("acb", [8, T], 16)
        dts = place("dts", [P, 2, TC, 8], 18)
        wend = place("wend", [P, TC, 8], 18.5)
        xr = place("xr", [P, 2, T + 3], 19)
        th = place("th", [P, 2, T], 23.25)
        S0 = 27 * 1024 + 256

        def put(name, shape, kib, dt=F32):
            return place(name, shape, kib, dt, S0)

        bf = put("bf", [P, T], 0)
        dtb = put("dtb", [8, T], 2)
        km = put("km", [P, NP, T], 4)
        e1 = put("e1", [P, T], 12)
        e2 = put("e2", [P, T], 14)
        e4 = put("e4", [P, T], 16)
        vf = put("vf", [P, T], 18)
        kdt = put("kdt", [P, TC, P], 20)
        vm = put("vm", [P, TC, 2, P], 22)
        vt = put("vt", [P, 2, TC, P], 26)
        e3 = put("e3", [P, 2, T], 30)
        sm = put("sm", [P, 2, 2, T], 34)
        dec = put("dec", [P, HALF, NCC + 1], 42)
        ctr = put("ctr", [P, HALF, NCC + 1], 50.25)
        xdt = put("xdt", [P, TC, P], 0)
        xde = put("xde", [P, TC, P], 2)
        gs = put("gs", [P, 2, T], 12)
        xs = put("xs", [P, 2, T], 16)
        zs = put("zs", [P, 2, T], 20)
        lm = put("lm", [P, 2, T], 24)
        cx = put("cx", [P, 2, T], 28)
        st = put("st", [P, TC, P], 32)
        y2 = put("y2", [P, 3, T], 34)
        sqb = put("sqb", [P, T], 58)
        rh = put("rh", [8, T], 60)
        shi = put("shi", [P, NP, T], 42, F32R)
        slo = put("slo", [P, NP, T], 50, F32R)
        ohi = put("ohi", [P, NP, T], 4, F32R)
        olo = [put(f"olo{p}", [P, T], kib, F32R) for p, kib in enumerate((40, 2, 60, 58))]
        eh = u2
        rg = g2[:, 1, :]

        ps = ctx.enter_context(nc.psum_tensor("ps", [P, 8, T], F32))

        def bank(i):
            return ps[:, i, :]

        def in_tiles(ap):
            return ap.rearrange("p (c t) -> p c t", c=TC)

        DOWN, NORM = 4, 6

        loaded = ev("loaded")
        stored = ev("stored")
        consts = ev("consts")
        full = [ev(f"raw_full{s}") for s in range(NS)]
        high = ev("high", W)
        split = ev("split", W, credit=NS)
        blk = ev("blk", W, credit=NS)
        par_set = ev("par_set", 1)
        par_made = ev("par_made")
        lg_max = ev("lg_max")
        lg_exp = ev("lg_exp")
        x_turned = ev("x_turned")
        x_tile = ev("x_tile", 3 * KD, KD, 2)
        x_high = ev("x_high", 3 * KD, KD)
        x_low = ev("x_low", 3 * KD, KD)
        x_sq = ev("x_sq", 3 * KD, KD)
        x_sum = ev("x_sum", 3 * KD, KD)
        norm_sum = ev("norm_sum", 3)
        g_out = ev("g_out", 2 * NJ, credit=2)
        u_out = ev("u_out", 2 * NJ, credit=2)
        silu_g = ev("silu_g", 2 * NJ)
        hid = ev("hid", 2 * NJ)
        hid_high = ev("hid_high", 2 * NJ)
        hid_low = ev("hid_low", 2 * NJ)
        dve_step = ctx.enter_context(nc.semaphore("dve_step"))
        proj_out = ev("proj_out", NPROJ, credit=3)
        tanh = ev("tanh", len(TANHS))
        tanh_used = ev("tanh_used", len(TANHS), credit=2)
        f_exp = ev("f_exp", NP)
        f_gate = ev("f_gate", NP)
        f_log = ev("f_log", NP)
        f_sum = ev("f_sum", NP)
        dt_abs = ev("dt_abs", 1)
        dt_exp = ev("dt_exp", 1)
        dt_log = ev("dt_log", 1)
        dt_sum = ev("dt_sum", 1)
        conv = ev("conv", 6)
        conv_silu = ev("conv_silu", 6)
        b_turned = ev("b_turned", 1)
        b_tok = ev("b_tok", 1)
        cb = ev("cb", 2)
        cb_masked = ev("cb_masked", 2)
        dt_turned = ev("dt_turned", 1)
        dt_tok = ev("dt_tok", 1)
        dist = ev("dist", 2 * NP)
        hexp = ev("hexp", 4 * NP)
        hmul = ev("hmul", 4 * NP)
        turned = ev("turned", 2 * NP)
        score = ev("score", 2 * NP)
        score_masked = ev("score_masked", 2 * NP)
        kd_tok = ev("kd_tok", NP)
        v_tok = ev("v_tok", 3 * NP)
        contrib = ev("contrib", 4 * NP)
        contrib_out = ev("contrib_out", 4 * NP)
        decay = ev("decay", NP)
        state = ev("state", NP)
        o_done = ev("o_done", NP)
        o_out = ev("o_out", 2 * NP)
        head_sum = ev("head_sum", 1)
        head_norm = ev("head_norm", 1)
        head_rms = ev("head_rms", NP)
        head_used = ev("head_used", NP)
        hg_y = ev("hg_y", NP)
        hg_high = ev("hg_high", NP)
        hg_low = ev("hg_low", NP)
        x_tok = ev("x_tok", NP)
        sums = ev("sums", 2 * NP)
        sums_exp = ev("sums_exp", 2 * NP)
        to_end = ev("to_end", 2 * NP)
        to_end_exp = ev("to_end_exp", 2 * NP)
        seg = ev("seg", 2 * NP)
        seg_exp = ev("seg_exp", 2 * NP)
        xdt_made = ev("xdt_made", NP)
        xde_made = ev("xde_made", NP)
        lm_made = ev("lm_made", 2 * NP)
        cx_made = ev("cx_made", 2 * NP)
        s_contrib = ev("s_contrib", NP)
        s_state = ev("s_state", NP)
        y_done = ev("y_done", NP)
        y_gated = ev("y_gated", NP)
        y_sq = ev("y_sq", NP)
        group_sum = ev("group_sum", 2)
        group_read = ev("group_read", 2)
        ssd_y = ev("ssd_y", NP)
        ssd_high = ev("ssd_high", NP)
        ssd_low = ev("ssd_low", NP)
        out_made = ev("out_made")
        out_turned = ev("out_turned")
        out_tok = ev("out_tok")

        block = ctx.enter_context(nc.Block())

        @block.sync
        def _(sp):
            sp.dma_start(stage[:], x_in.rearrange("b (c p) d -> p (b c) d", p=P)).then_inc(loaded.sem, 16)
            sp.dma_start(par_all[:, :, 0:NIN], cols).then_inc(loaded.sem, 16)
            sp.dma_start(first[:], first_norm).then_inc(loaded.sem, 16)
            sp.dma_start(lg[:], logits).then_inc(loaded.sem, 16)
            with sp.Fori(0, DEPTH) as l:
                def load(w, q, dst, src):
                    sp.wait_ge(split.sem, split.upto(l, w - NS))
                    sp.dma_start(dst, src).then_inc(full[q].sem, 16)

                def ffn(wb, up, dn):
                    with sp.Fori(0, UP_BLOCKS // NS) as i:
                        for q in range(NS):
                            load(wb + NS * i + q, q, raw[:, q, :], up[l, NS * i + q])
                    for m in range(KD):
                        for s, (j0, j1) in enumerate(DN_PIECES):
                            w = wb + UP_BLOCKS + 3 * m + s
                            load(w, w % NS, raw[:, w % NS, 0:(j1 - j0) * P], dn[l, m, :, j0 * P:j1 * P])

                ffn(0, up1, dn1)
                for i, (n, k0, k1) in enumerate(PBLOCKS):
                    w = MIX0 + i
                    if PROJ[n][0] == "dt":
                        load(w, w % NS, raw[:, w % NS, :].rearrange("p (k m) -> p k m", k=KD)[:, :, 0:8],
                             dtw[l])
                    else:
                        load(w, w % NS, raw[:, w % NS, 0:(k1 - k0) * P],
                             mix[l, n - (n > AT["dt", 0]), :, k0 * P:k1 * P])
                for m in range(KD):
                    w = OUT0 + m
                    load(w, w % NS, raw[:, w % NS, :], mix[l, NPROJ - 1 + m])
                ffn(FFN2, up2, dn2)
            sp.wait_ge(out_tok.sem, KD)
            sp.dma_start(out.rearrange("b (c p) d -> p (b c) d", p=P), stage[:]).then_inc(stored.sem, 16)
            sp.wait_ge(stored.sem, 16)

        @block.gpsimd
        def _(pool):
            def made(ins, n):
                ins.then_inc(consts.sem, 1)
                pool.wait_ge(consts.sem, n)

            made(pool.memset(ident[:], 0.0), 1)
            made(pool.affine_select(out=ident[:], in_=ident[:], compare_op=ALU.not_equal, fill=1.0, base=0,
                                    pattern=[[-1, P]], channel_multiplier=1), 2)
            made(pool.memset(ones[:], 1.0), 3)
            made(pool.memset(causal[:], 1.0), 4)
            made(pool.affine_select(out=causal[:], in_=causal[:], compare_op=ALU.is_ge, fill=0.0, base=0,
                                    pattern=[[1, P]], channel_multiplier=-1), 5)
            made(pool.affine_select(out=block16[:].rearrange("p (c i) -> p c i", i=CH),
                                    in_=causal[:].rearrange("p (c i) -> p c i", i=CH),
                                    compare_op=ALU.is_ge, fill=0.0, base=0,
                                    pattern=[[-CH, P // CH], [0, CH]], channel_multiplier=1), 6)
            made(pool.memset(keep16[:], 1.0), 7)
            made(pool.memset(keep16[:, 0:T:CH], 0.0), 8)
            made(pool.memset(par8[:], 1.0), 9)
            made(pool.affine_select(out=par8[:], in_=par8[:], compare_op=ALU.is_ge, fill=0.0, base=0,
                                    pattern=[[-CH, 2], [-2 * CH, 4]], channel_multiplier=1), 10)
            made(pool.affine_select(out=par8[:], in_=par8[:], compare_op=ALU.is_ge, fill=0.0, base=CH - 1,
                                    pattern=[[CH, 2], [2 * CH, 4]], channel_multiplier=-1), 11)
            made(pool.memset(headsum[:], 0.0), 12)
            made(pool.memset(headsum[0:HALF, 0:31:10], 1.0), 13)
            made(pool.memset(headsum[HALF:P, 1:32:10], 1.0), 14)
            for q in range(NS):
                pool.sem_inc(split.sem, 1)
            with pool.Fori(0, DEPTH * W // NS) as i:
                for q in range(NS):
                    pool.wait_ge(high.sem, NS * i + (q + 1))
                    pool.tensor_tensor(wlo[:, q, :], raw[:, q, :], whi[:, q, :].bitcast(F32),
                                       ALU.subtract).then_inc(split.sem, 1)

        @block.scalar
        def _(act):
            act.wait_ge(lg_max.sem, 1)
            act.activation(lg[:], lg[:], ACT.Exp).then_inc(lg_exp.sem, 1)
            act.activation(par_all[:, :, NEGA:NEGA + 1], par_all[:, :, ALOG:ALOG + 1], ACT.Exp)\
               .then_inc(lg_exp.sem, 1)

            def residual(l, k, gain):
                m = k % KD
                act.wait_ge(x_tile.sem, x_tile.upto(l, k))
                act.activation(hhi[:, m, :], x[:, m, :], ACT.Copy, scale=gain).then_inc(x_high.sem, 1)
                if not (isinstance(l, int) and l == 0 and k == -KD):
                    act.wait_ge(x_sum.sem, x_sum.upto(l, k - 1))
                act.activation(sq[:], x[:, m, :], ACT.Square).then_inc(x_sq.sem, 1)

            for m in range(KD):
                residual(0, m - KD, first[:, m:m + 1])

            with act.Fori(0, DEPTH) as l:
                def hi(w, q=None):
                    q = w % NS if q is None else q
                    act.wait_ge(full[q].sem, 16 * ((w - q) // NS + l * (W // NS)) + 16)
                    act.wait_ge(blk.sem, blk.upto(l, w - NS))
                    act.activation(whi[:, q, :], raw[:, q, :], ACT.Copy).then_inc(high.sem, 1)

                def hi_i(wb, i, q):
                    act.wait_ge(full[q].sem, 16 * (wb // NS + 1) + 16 * i + l * (16 * W // NS))
                    act.wait_ge(blk.sem, blk.upto(l, wb + q - NS) + NS * i)
                    act.activation(whi[:, q, :], raw[:, q, :], ACT.Copy).then_inc(high.sem, 1)

                for q in range(NS):
                    hi(q)

                def ffn(c, wb, k0, gain0):
                    with act.Fori(0, NJ // 2) as i:
                        for jj in range(2):
                            k = NJ * c + jj
                            act.wait_ge(g_out.sem, g_out.upto(l, k) + 2 * i)
                            act.activation(g2[:, jj, :], g2[:, jj, :], ACT.Silu).then_inc(silu_g.sem, 1)
                            hi_i(wb + NS, i, 2 * jj)
                            act.wait_ge(hid.sem, hid.upto(l, k) + 2 * i)
                            act.activation(ahi[:, 2 * i + jj, :], u2[:, jj, :], ACT.Copy).then_inc(hid_high.sem, 1)
                            hi_i(wb + NS, i, 2 * jj + 1)
                    for m in range(KD):
                        for s in range(3):
                            w = wb + UP_BLOCKS + 3 * m + s
                            if w + NS < W:
                                hi(w + NS)
                        residual(l, k0 + m, par[:, gain0 + m:gain0 + m + 1])

                act.wait_ge(par_set.sem, par_set.upto(l, 0))
                ffn(0, 0, 0, WN)

                def ready(e, k=0):
                    act.wait_ge(e.sem, e.upto(l, k))

                def do(e, out, in_, f, **kw):
                    act.activation(out, in_, f, **kw).then_inc(e.sem, 1)

                def do_tanh(kind, src):
                    i = TANHS.index(kind)
                    ready(tanh_used, i - 2)
                    do(tanh, th[:, i % 2, :], src, ACT.Tanh)

                def conv_src(t):
                    return {"B": bf[:], "C": cf[:]}[t] if isinstance(t, str) else xs[:, t % 2, :]

                def conv_tanh(t):
                    ready(conv, CONVS.index(t))
                    do_tanh(("cv", t), conv_src(t))

                def plain_tanh(kind, p):
                    ready(proj_out, AT[kind, p])
                    do_tanh((kind, p), g2[:, 0, :])

                def hg_exps(p):
                    ready(dist, 2 * p)
                    do(hexp, e2[:], e1[:], ACT.Exp, scale=-1.0)
                    do(hexp, e1[:], e1[:], ACT.Exp)
                    if p >= 2:
                        ready(o_done, p - 2)
                    do(hexp, e3[:, p % 2, :], b[:, p, :], ACT.Exp)
                    ready(dist, 2 * p + 1)
                    do(hexp, e4[:], e4[:], ACT.Exp)

                def hg_copies(p):
                    ready(turned, 2 * p)
                    do(kd_tok, kdt[:].rearrange("p c n -> p (c n)"), bank(3), ACT.Copy)
                    ready(turned, 2 * p + 1)
                    if p >= 2:
                        ready(o_done, p - 2)
                    do(v_tok, vt[:, p % 2, :, :].rearrange("p c n -> p (c n)"), bank(4), ACT.Copy)
                    for j in range(2):
                        do(v_tok, vm[:, :, j, :], in_tiles(bank(4)), ACT.Copy, scale=parity[:, j:j + 1])

                def hg_contrib(p):
                    if p >= 1:
                        ready(state, p - 1)
                    else:
                        ready(f_sum, NP - 1)
                    do(decay, dec[:, :, 1:NCC + 1],
                       b[:, p, CH - 1:T:CH].unsqueeze(1).to_broadcast([P, HALF, NCC]), ACT.Exp)
                    for rr in range(4):
                        ready(contrib, 4 * p + rr)
                        do(contrib_out,
                           ctr[:, :, 1:NCC + 1].rearrange("p v (c r q) -> p r c q v", r=4, q=2)[:, rr],
                           bank(3 + rr).rearrange("p (c q v) -> p c q v", c=TC, q=2), ACT.Copy)

                def hg_out(p):
                    ready(o_done, p)
                    do(o_out, km[:, p, :], bank(7), ACT.Square)
                    do(o_out, b[:, p, :], bank(7), ACT.Copy)

                def ssd_exps(p):
                    for h in range(2):
                        k = 2 * p + h
                        ready(sums, k)
                        if p >= 1:
                            ready(s_state, p - 1)
                        do(sums_exp, eh[:, h, :], bank(4 + h), ACT.Exp)
                    for h in range(2):
                        k = 2 * p + h
                        ready(to_end, k)
                        do(to_end_exp, wend[:, :, k], wend[:, :, k], ACT.Exp)
                        ready(seg, k)
                        do(seg_exp, lm[:, h, :], lm[:, h, :], ACT.Exp)

                def ssd_sq(p):
                    ready(y_gated, p)
                    if p == 2:
                        ready(group_sum, 0)
                    do(y_sq, sqb[:] if p % 2 else sq[:], y2[:, p % 3, :], ACT.Square)

                def ssd_hi(p):
                    ready(ssd_y, p)
                    do(ssd_high, shi[:, p, :], y2[:, p % 3, :], ACT.Copy)

                def hg_hi(p):
                    ready(hg_y, p)
                    do(hg_high, ohi[:, p, :], b[:, p, :], ACT.Copy)

                for n, (kind, pr) in enumerate(PROJ):
                    for i, (nn, _, _) in enumerate(PBLOCKS):
                        if nn == n:
                            hi(MIX0 + i + NS)
                    if kind == "f":
                        ready(proj_out, n)
                        do(f_exp, km[:, pr, :], g2[:, pr % 2, :], ACT.Exp, scale=-1.0)
                    if kind == "dt":
                        ready(dt_abs)
                        do(dt_exp, acb[:], acb[:], ACT.Exp)
                        for p in range(NP):
                            ready(f_gate, p)
                            do(f_log, b[:, p, :], b[:, p, :], ACT.Ln)
                        ready(dt_exp)
                        do(dt_log, acb[:], acb[:], ACT.Ln, bias=1.0)
                    if kind == "C":
                        conv_tanh("B")
                    if n == 7:
                        conv_tanh("C")
                        plain_tanh("q", 0)
                        hg_exps(0)
                    if n == 8:
                        ready(b_turned)
                        do(b_tok, bt[:].rearrange("p c n -> p (c n)"), bank(3), ACT.Copy)
                    if n in (9, 11, 13):
                        p = (n - 9) // 2
                        plain_tanh("q", p + 1)
                        hg_copies(p)
                        hg_exps(p + 1)
                    if n in (15, 16):
                        plain_tanh("g", n - 15)
                    if n == 15:
                        hg_copies(3)
                    if n in (10, 12, 14, 16):
                        hg_contrib((n - 10) // 2)
                    if n in (12, 14, 16, 18):
                        hg_out((n - 12) // 2)
                    if kind == "z":
                        plain_tanh("z", pr)
                    if n in (19, 21, 23, 25):
                        ssd_exps((n - 19) // 2)
                    if n in (21, 23, 25):
                        ssd_sq((n - 21) // 2)
                    if kind == "xs":
                        conv_tanh(pr)
                    if n in (25, 26):
                        plain_tanh("g", n - 23)
                    if n in (22, 24):
                        hg_hi((n - 22) // 2)
                for p in (0, 1):
                    ssd_hi(p)
                for p in (2, 3):
                    hg_hi(p)
                ssd_sq(3)
                for p in (2, 3):
                    ssd_hi(p)
                for m in range(KD):
                    hi(OUT0 + m + NS)
                    residual(l, KD + m, par[:, WN + KD + m:WN + KD + m + 1])
                ffn(1, FFN2, 2 * KD, WN + 2 * KD)

        @block.vector
        def _(dve):
            own = Steps(dve, dve_step)
            did, settle = own.did, own.settle
            tt, ts, stt = dve.tensor_tensor, dve.tensor_scalar, dve.scalar_tensor_tensor

            def rsqrt(dst, src, scale, read=None):
                n = dst.shape[0]
                ms, tmp = t1[0:n, :], acc[0:n, :]
                if read is None:
                    did(ts(ms, src, scale, EPS, ALU.mult, ALU.add))
                    settle()
                did(ts(dst.bitcast(I32), ms.bitcast(I32), -0.5, MAGIC, ALU.mult, ALU.add))
                settle()
                for _ in range(3):
                    did(stt(tmp, dst, -0.5, dst, ALU.mult, ALU.mult))
                    settle()
                    did(tt(tmp, tmp, ms, ALU.mult))
                    settle()
                    did(stt(dst, tmp, 1.5, dst, ALU.add, ALU.mult))
                    settle()

            def residual(l, k, gain, update):
                m = k % KD
                update(m).then_inc(x_tile.sem, 1)
                dve.wait_ge(x_high.sem, x_high.upto(l, k))
                stt(hlo[:, m, :], x[:, m, :], gain, hhi[:, m, :].bitcast(F32), ALU.mult, ALU.subtract)\
                    .then_inc(x_low.sem, 1)
                dve.wait_ge(x_sq.sem, x_sq.upto(l, k))
                if m == 0:
                    dve.tensor_copy(acc[:], sq[:]).then_inc(x_sum.sem, 1)
                else:
                    dve.wait_ge(x_sum.sem, x_sum.upto(l, k - 1))
                    tt(acc[:], acc[:], sq[:], ALU.add).then_inc(x_sum.sem, 1)

            def norm(l, ph):
                dve.wait_ge(norm_sum.sem, norm_sum.upto(l, ph))
                rsqrt(r[:], bank(NORM), 1.0 / D)

            for e, n in ((g_out, 2), (u_out, 2), (proj_out, 3), (x_tile, 2), (tanh_used, 2)):
                for _ in range(n):
                    dve.sem_inc(e.sem, 1)

            dve.wait_ge(loaded.sem, 64)
            did(dve.tensor_copy(lt[:, 0, :], lg[:, 0, :]))
            for d in range(1, DEPTH):
                settle()
                did(tt(lt[:, 0, :], lt[:, 0, :], lg[:, d, :], ALU.max))
            settle()
            tt(lg[:], lg[:], lt[:, 0:1, :].to_broadcast([P, DEPTH, NP]), ALU.subtract).then_inc(lg_max.sem, 1)
            did(ts(par_all[:, :, CW:SN], par_all[:, :, CW:SN], 0.5, None, ALU.mult))
            dve.wait_ge(lg_exp.sem, 2)
            did(ts(par_all[:, :, NEGA:NEGA + 1], par_all[:, :, NEGA:NEGA + 1], -1.0, None, ALU.mult))
            did(dve.tensor_copy(lt[:, 0, :], lg[:, 0, :]))
            for d in range(1, DEPTH):
                settle()
                did(tt(lt[:, 0, :], lt[:, 0, :], lg[:, d, :], ALU.add))
            settle()
            did(dve.reciprocal(lt[:, 1, :], lt[:, 0, :]))
            settle()
            did(tt(lg[:], lg[:], lt[:, 1:2, :].to_broadcast([P, DEPTH, NP]), ALU.mult))
            settle()
            did(dve.tensor_copy(lt[:, 2, :], lg[:, 0, :]))
            for d in range(DEPTH):
                settle()
                if d:
                    did(tt(lt[:, 2, :], lt[:, 2, :], lg[:, d, :], ALU.add))
                    settle()
                did(tt(par_all[:, d, LB:LB + NP], lt[:, 2, :], lg[:, 0, :], ALU.subtract))
            settle()
            did(ts(par_all[:, :, OLB:OLB + NP], par_all[:, :, LB:LB + NP], -1.0, 1.0, ALU.mult, ALU.add))
            dve.wait_ge(consts.sem, 14)
            dve.reduce_sum(parity[:], par8[:], AX.X).then_inc(par_made.sem, 1)

            for m in range(KD):
                def turned_in(m):
                    dve.wait_ge(x_turned.sem, m + 1)
                    return dve.tensor_copy(x[:, m, :], bank(DOWN + m % 2))
                residual(0, m - KD, first[:, m:m + 1], turned_in)
            ahead = own.n

            with dve.Fori(0, DEPTH) as l:
                own.base, own.n = l * DVE_STEPS + ahead, 0
                dve.wait_ge(dve_step, own.base)
                dve.wait_ge(x_low.sem, x_low.upto(l, -1))
                dve.tensor_copy(par[:], par_all[:, l, :]).then_inc(par_set.sem, 1)
                dve.wait_ge(par_set.sem, par_set.upto(l, 0))

                def ready(e, k=0):
                    dve.wait_ge(e.sem, e.upto(l, k))

                def made(e, ins):
                    ins.then_inc(e.sem, 1)

                def alone():
                    settle()
                    did(dve.memset(spare[:], 0.0))

                def col(c):
                    return par[:, c:c + 1]

                def ffn(c, wb, k0, gain0):
                    norm(l, 2 * c)
                    alone()
                    with dve.Fori(0, NJ // 2) as i:
                        for jj in range(2):
                            k = NJ * c + jj
                            dve.wait_ge(blk.sem, blk.upto(l, wb + 2 * jj) + NS * i)
                            made(g_out, tt(g2[:, jj, :], bank(jj), r[:], ALU.mult))
                            dve.wait_ge(blk.sem, blk.upto(l, wb + 2 * jj + 1) + NS * i)
                            made(u_out, tt(u2[:, jj, :], bank(2 + jj), r[:], ALU.mult))
                            dve.wait_ge(u_out.sem, u_out.upto(l, k) + 2 * i)
                            dve.wait_ge(silu_g.sem, silu_g.upto(l, k) + 2 * i)
                            made(hid, tt(u2[:, jj, :], g2[:, jj, :], u2[:, jj, :], ALU.mult))
                            dve.wait_ge(hid_high.sem, hid_high.upto(l, k) + 2 * i)
                            made(hid_low, tt(alo[:, 2 * i + jj, :], u2[:, jj, :],
                                             ahi[:, 2 * i + jj, :].bitcast(F32), ALU.subtract))
                    for m in range(KD):
                        def down(m):
                            ready(blk, wb + UP_BLOCKS + 3 * m + 2)
                            return stt(x[:, m, :], bank(DOWN + m % 2), 0.5, x[:, m, :], ALU.mult, ALU.add)
                        residual(l, k0 + m, col(gain0 + m), down)

                ffn(0, 0, 0, WN)

                norm(l, 1)
                settle()

                def evac(n):
                    kind, p = PROJ[n]
                    ready(blk, LAST_BLOCK[n])
                    src = bank(n % 3)
                    if kind == "f":
                        made(proj_out, tt(g2[:, p % 2, :], src, r[:], ALU.mult))
                    elif kind == "dt":
                        made(proj_out, tt(dtb[:], src[0:8, :], r[0:8, :], ALU.mult))
                    elif kind in ("B", "C", "xs"):
                        made(proj_out, tt(xr[:, n % 2, 3:T + 3], src, r[:], ALU.mult))
                    elif kind == "i":
                        made(proj_out, tt(vf[:], src, r[:], ALU.mult))
                    else:
                        before = [t for t in TANHS[:TANHS.index((kind, p))] if t[0] != "cv"]
                        if before:
                            ready(tanh_used, TANHS.index(before[-1]))
                        made(proj_out, stt(g2[:, 0, :], src, 0.5, r[:], ALU.mult, ALU.mult))

                def silu(kind, half, dst, e=None):
                    i = TANHS.index(kind)
                    ready(tanh, i)
                    made(tanh_used, stt(dst, th[:, i % 2, :], 1.0, half, ALU.add, ALU.mult))

                def gate_f(p):
                    ready(f_exp, p)
                    did(ts(t1[:], km[:, p, :], BIG, 1.0, ALU.min, ALU.add))
                    settle()
                    did(dve.reciprocal(acc[:], t1[:]))
                    settle()
                    did(stt(km[:, p, :], km[:, p, :], BIG, acc[:], ALU.min, ALU.mult))
                    made(f_gate, ts(b[:, p, :], acc[:], col(OLB + p), col(LB + p), ALU.mult, ALU.add))

                def scan_f(p):
                    ready(f_log, p)
                    made(f_sum, dve.tensor_tensor_scan(b[:, p, :], keep16[:], b[:, p, :], 0.0,
                                                       ALU.mult, ALU.add))

                def dt_first():
                    ready(proj_out, AT["dt", 0])
                    did(ts(dtb[:], dtb[:], par[0:8, DTB:DTB + 1], None, ALU.add))
                    settle()
                    made(dt_abs, stt(acb[:], dtb[:], -1.0, dtb[:], ALU.mult, ALU.min))

                def dt_rest():
                    ready(dt_log)
                    did(stt(dtb[:], dtb[:], 0.0, acb[:], ALU.max, ALU.add))
                    settle()
                    did(ts(acb[:], dtb[:], par[0:8, NEGA:NEGA + 1], None, ALU.mult))
                    settle()
                    for c in range(TC):
                        a = acb[:, c * P:(c + 1) * P]
                        ins = dve.tensor_tensor_scan(a, ones[0:8, :], a, 0.0, ALU.mult, ALU.add)
                        if c < TC - 1:
                            did(ins)
                        else:
                            made(dt_sum, ins)

                def convolve(t, n):
                    dst = {"B": bf[:], "C": cf[:]}[t] if isinstance(t, str) else xs[:, t % 2, :]
                    i = {"B": CONV_B, "C": CONV_C}.get(t, t)
                    ready(proj_out, n)
                    did(ts(dst, xr[:, n % 2, 0:T], col(CW + 4 * i), col(CB + i), ALU.mult, ALU.add))
                    for k in range(1, 4):
                        settle()
                        ins = stt(dst, xr[:, n % 2, k:T + k], col(CW + 4 * i + k), dst, ALU.mult, ALU.add)
                        if k < 3:
                            did(ins)
                        else:
                            made(conv, ins)
                    ready(conv, CONVS.index(t))

                def conv_out(t):
                    dst = {"B": bf[:], "C": cf[:]}[t] if isinstance(t, str) else xs[:, t % 2, :]
                    silu(("cv", t), dst, dst)

                def hg_dist(p):
                    if p >= 1:
                        ready(score, 2 * p - 1)
                    ready(f_sum, p)
                    bb = b[:, p, :].rearrange("p (c i) -> p c i", i=CH)
                    made(dist, tt(e1[:].rearrange("p (c i) -> p c i", i=CH), bb,
                                  bb[:, :, CREF:CREF + 1].to_broadcast([P, NCC, CH]), ALU.subtract))
                    made(dist, tt(e4[:].rearrange("p (c i) -> p c i", i=CH),
                                  bb[:, :, CH - 1:CH].to_broadcast([P, NCC, CH]), bb, ALU.subtract))

                def hg_q(p):
                    ready(proj_out, AT["q", p])
                    silu(("q", p), g2[:, 0, :], g2[:, 1, :])
                    ready(tanh_used, TANHS.index(("q", p)))
                    ready(hexp, 4 * p + 1)
                    made(hmul, tt(e1[:], g2[:, 1, :], e1[:], ALU.mult))
                    ready(hexp, 4 * p + 2)
                    made(hmul, tt(e3[:, p % 2, :], g2[:, 1, :], e3[:, p % 2, :], ALU.mult))

                def hg_k(p):
                    made(hmul, stt(e2[:], km[:, p, :], col(OLB + p), e2[:], ALU.mult, ALU.mult))
                    ready(hexp, 4 * p + 3)
                    made(hmul, stt(e4[:], km[:, p, :], col(OLB + p), e4[:], ALU.mult, ALU.mult))

                def hg_mask(p):
                    if p >= 2:
                        ready(o_done, p - 2)
                    for h in range(2):
                        ready(score, 2 * p + h)
                        alone()
                        made(score_masked, dve.copy_predicated(
                            in_tiles(sm[:, p % 2, h, :]),
                            block16[:].bitcast(I32).unsqueeze(1).to_broadcast([P, TC, P]),
                            in_tiles(bank(5 + h))))

                def hg_scan(p):
                    ready(decay, p)
                    ready(contrib_out, 4 * p + 3)
                    made(state, dve.tensor_tensor_scan(
                        ctr[:].rearrange("p v c -> p (v c)"), dec[:].rearrange("p v c -> p (v c)"),
                        ctr[:].rearrange("p v c -> p (v c)"), 0.0, ALU.mult, ALU.add))

                def ssd_common():
                    for g in range(2):
                        ready(cb, g)
                        made(cb_masked, tt(cbm[:, g], in_tiles(bank(4 + g)),
                                           causal[:].unsqueeze(1).to_broadcast([P, TC, P]), ALU.mult))
                    ready(dt_turned)
                    made(dt_tok, dve.tensor_copy(dts[:].rearrange("p a c h -> p (a c h)"),
                                                 bank(6)[:, 0:2 * TC * 8]))

                def by_head(ap, p):
                    return ap[:, :, 2 * p:2 * p + 2].unsqueeze(3).to_broadcast([P, TC, 2, HALF])

                def ssd_main(p):
                    g = p // 2
                    gg = slice(HALF * g, HALF * g + HALF)
                    xtok = bank(3).rearrange("p (c h n) -> p c h n", c=TC, h=2)
                    ready(x_tok, p)
                    ready(dt_tok)
                    if p:
                        ready(y_done, p - 1)
                    made(xdt_made, tt(xdt[:].rearrange("p c (h n) -> p c h n", h=2), xtok,
                                      by_head(dts[:, 0], p), ALU.mult))
                    for h in range(2):
                        k = 2 * p + h
                        ready(sums_exp, k)
                        acc_t = in_tiles(bank(4 + h))
                        ac_s = dts[:, 1, :, k]
                        made(to_end, tt(wend[:, :, k], acc_t[:, :, P - 1], ac_s, ALU.subtract))
                        did(tt(in_tiles(lm[:, h, :]), acc_t,
                               ac_s.unsqueeze(2).to_broadcast([P, TC, P]), ALU.subtract))
                        settle()
                        made(seg, ts(lm[:, h, :], lm[:, h, :], 0.0, None, ALU.min))
                    for h in range(2):
                        k = 2 * p + h
                        ready(to_end_exp, k)
                        did(tt(wend[:, :, k], wend[:, :, k], dts[:, 0, :, k], ALU.mult))
                    settle()
                    made(xde_made, tt(xde[:].rearrange("p c (h n) -> p c h n", h=2), xtok,
                                      by_head(wend[:], p), ALU.mult))
                    for h in range(2):
                        k = 2 * p + h
                        made(cx_made, tt(cx[gg, h, :], cf[gg, :], eh[gg, h, :], ALU.mult))
                        ready(seg_exp, k)
                        made(lm_made, tt(in_tiles(lm[:, h, :]), in_tiles(lm[:, h, :]), cbm[:, g], ALU.mult))

                def ssd_states(p):
                    g = p // 2
                    gg = slice(HALF * g, HALF * g + HALF)
                    ready(s_contrib, p)
                    did(dve.tensor_copy(st[gg, 1, :], bank(6)[gg, 0:P]))
                    for c in range(2, TC):
                        for h in range(2):
                            hh = slice(HALF * h, HALF * h + HALF)
                            if h == 0:
                                settle()
                            ins = stt(st[gg, c, hh], st[gg, c - 1, hh], eh[gg, h, c * P - P + P - 1:c * P - P + P],
                                      bank(6)[gg, (c - 1) * P + HALF * h:(c - 1) * P + HALF * h + HALF],
                                      ALU.mult, ALU.add)
                            if c == TC - 1 and h == 1:
                                made(s_state, ins)
                            else:
                                did(ins)

                def ssd_gate(p):
                    ready(y_done, p)
                    if p == 3:
                        ready(ssd_low, 0)
                    did(stt(y2[:, p % 3, :], xs[:, p % 2, :], col(DC + p), bank(7), ALU.mult, ALU.add))
                    settle()
                    made(y_gated, tt(y2[:, p % 3, :], y2[:, p % 3, :], zs[:, p % 2, :], ALU.mult))

                def group_mean(g, bk):
                    ready(group_sum, g)
                    made(group_read, ts(t1[:], bank(bk), 1.0 / (SSD_W // 2), EPS, ALU.mult, ALU.add))
                    ready(group_read, g)

                def ssd_norm(p):
                    made(ssd_y, stt(y2[:, p % 3, :], y2[:, p % 3, :], col(SN + p), rg, ALU.mult, ALU.mult))

                def ssd_lo(p):
                    ready(ssd_high, p)
                    made(ssd_low, tt(slo[:, p, :], y2[:, p % 3, :], shi[:, p, :].bitcast(F32), ALU.subtract))

                def hg_norm(p, bk):
                    ready(head_rms, p)
                    made(head_used, stt(b[:, p, :], b[:, p, :], col(HN), bank(bk), ALU.mult, ALU.mult))
                    ready(head_used, p)

                def hg_gate(p):
                    made(hg_y, tt(b[:, p, :], b[:, p, :], gs[:, p % 2, :], ALU.mult))

                def hg_lo(p):
                    ready(hg_high, p)
                    if p == 3:
                        ready(group_sum, 1)
                    made(hg_low, tt(olo[p][:], b[:, p, :], ohi[:, p, :].bitcast(F32), ALU.subtract))

                did(dve.memset(xr[:, :, 0:3], 0.0))
                did(dve.memset(dec[:, :, 0:1], 0.0))
                did(dve.memset(ctr[:, :, 0:1], 0.0))
                did(dve.memset(sm[:].rearrange("p a h t -> p (a h t)"), 0.0))
                settle()
                for n, (kind, pr) in enumerate(PROJ):
                    evac(n)
                    if kind == "f":
                        gate_f(pr)
                    if kind == "dt":
                        dt_first()
                    if n == 5:
                        dt_rest()
                        scan_f(0)
                        scan_f(1)
                    if n == 6:
                        convolve("B", 5)
                        scan_f(2)
                        scan_f(3)
                        conv_out("B")
                    if n == 7:
                        convolve("C", 6)
                        hg_dist(0)
                        conv_out("C")
                        hg_q(0)
                    if n == 8:
                        hg_k(0)
                        ssd_common()
                    if n in (9, 11, 13):
                        p = (n - 9) // 2
                        hg_mask(p)
                        hg_dist(p + 1)
                        hg_q(p + 1)
                    if n in (10, 12, 14):
                        p = (n - 10) // 2
                        hg_k(p + 1)
                        hg_scan(p)
                    if n == 15:
                        hg_mask(3)
                    if kind == "g" and pr < 2:
                        ready(proj_out, n)
                        silu(("g", pr), g2[:, 0, :], gs[:, pr, :])
                    if n == 16:
                        hg_scan(3)
                    if n in (21, 23, 25):
                        ssd_gate((n - 21) // 2)
                    if n in (19, 21, 23, 25):
                        ssd_main((n - 19) // 2)
                    if kind == "xs":
                        convolve(pr, n)
                        conv_out(pr)
                    if kind == "z":
                        if pr:
                            ssd_states(pr - 1)
                        ready(proj_out, n)
                        silu(("z", pr), g2[:, 0, :], zs[:, pr % 2, :])
                    if n == 20:
                        ready(head_sum)
                        rsqrt(rh[:], bank(7)[0:8, :], 1.0 / HALF)
                        made(head_norm, dve.tensor_copy(rh[:], rh[:]))
                    if n in (22, 24):
                        p = (n - 22) // 2
                        hg_norm(p, 3)
                        hg_gate(p)
                        if p == 0:
                            hg_lo(p)
                    if n in (25, 26):
                        ready(proj_out, n)
                        silu(("g", pr), g2[:, 0, :], gs[:, pr % 2, :])
                group_mean(0, 7)
                ssd_states(3)
                hg_lo(1)
                rsqrt(rg, None, None, read=True)
                ssd_norm(0)
                ssd_norm(1)
                hg_norm(2, 3)
                hg_gate(2)
                hg_norm(3, 4)
                hg_gate(3)
                ssd_lo(0)
                ssd_lo(1)
                ssd_gate(3)
                hg_lo(2)
                group_mean(1, 6)
                rsqrt(rg, None, None, read=True)
                ssd_norm(2)
                ssd_norm(3)
                hg_lo(3)
                ssd_lo(2)
                ssd_lo(3)
                for m in range(KD):
                    def mixed(m):
                        ready(blk, OUT0 + m)
                        return stt(x[:, m, :], bank(DOWN + m % 2), 1.0, x[:, m, :], ALU.mult, ALU.add)
                    residual(l, KD + m, col(WN + KD + m), mixed)
                ffn(1, FFN2, 2 * KD, WN + 2 * KD)
                assert own.n == DVE_STEPS, own.n

            own.base, own.n = ahead + DEPTH * DVE_STEPS, 0
            norm(DEPTH, 0)
            for m in range(KD):
                stt(ont[:, m, :], x[:, m, :], par[:, WN + 2 * KD + m:WN + 2 * KD + m + 1], r[:],
                    ALU.mult, ALU.mult).then_inc(out_made.sem, 1)
            for m in range(KD):
                dve.wait_ge(out_turned.sem, m + 1)
                dve.tensor_copy(stage[:, :, m * P:(m + 1) * P], in_tiles(bank(m))).then_inc(out_tok.sem, 1)

        @block.tensor
        def _(pe):
            mm = pe.matmul
            for _ in range(NS):
                pe.sem_inc(blk.sem, 1)
            pe.wait_ge(consts.sem, 14)
            pe.wait_ge(loaded.sem, 64)
            for m in range(KD):
                pe.wait_ge(x_tile.sem, x_tile.upto(0, m - KD - 2))
                for c in range(TC):
                    last = pe.transpose(bank(DOWN + m % 2)[:, c * P:(c + 1) * P], stage[:, c, m * P:(m + 1) * P],
                                        ident[:])
                last.then_inc(x_turned.sem, 1)

            def products(dst, q, piece, moving, start, stop):
                s = slice(piece * P, piece * P + P)
                mh, ml = moving
                mm(dst, whi[:, q, s], mh, start=start, stop=False)
                mm(dst, whi[:, q, s], ml, start=False, stop=False)
                return mm(dst, wlo[:, q, s], mh, start=False, stop=stop)

            def norm_products(l, ph):
                pe.wait_ge(x_sum.sem, x_sum.upto(l, KD * ph - 1))
                mm(bank(NORM), ones[:], acc[:], start=True, stop=True).then_inc(norm_sum.sem, 1)

            def h_tile(k):
                return hhi[:, k, :], hlo[:, k, :]

            with pe.Fori(0, DEPTH) as l:
                def ready(e, k=0):
                    pe.wait_ge(e.sem, e.upto(l, k))

                def h_ready(ph, k):
                    if k in (0, KD - 1):
                        ready(x_low, KD * ph - KD + (KD - 2 if k == 0 else KD - 1))

                def ffn(c, wb):
                    ph = 2 * c

                    def up(i, peeled):
                        for jj in range(2):
                            for kind in range(2):
                                q = 2 * jj + kind
                                free = (g_out, u_out)[kind]
                                pe.wait_ge(free.sem, free.upto(l, NJ * c + jj - 2) + 2 * i)
                                pe.wait_ge(split.sem, split.upto(l, wb + q) + NS * i)
                                for k in range(KD):
                                    if peeled and q == 0:
                                        h_ready(ph, k)
                                    last = products(bank(2 * kind + jj), q, k, h_tile(k), k == 0, k == KD - 1)
                                last.then_inc(blk.sem, 1)
                                if peeled and q == 0:
                                    norm_products(l, ph)

                    up(0, True)
                    with pe.Fori(1, NJ // 2) as i:
                        up(i, False)
                    with pe.Fori(0, 2) as i:
                        for mm4 in range(4):
                            pe.wait_ge(x_tile.sem, x_tile.upto(l, KD * ph + mm4 - 2) + 4 * i)
                            for s, (j0, j1) in enumerate(DN_PIECES):
                                w = wb + UP_BLOCKS + 3 * mm4 + s
                                ready(hid_low, NJ * c + j1 - 1)
                                pe.wait_ge(split.sem, split.upto(l, w) + 12 * i)
                                for j in range(j0, j1):
                                    last = products(bank(DOWN + mm4 % 2), w % NS, j - j0,
                                                    (ahi[:, j, :], alo[:, j, :]), j == 0, j == NJ - 1)
                                last.then_inc(blk.sem, 1)

                ffn(0, 0)

                def cols_of(c):
                    return slice(c * P, (c + 1) * P)

                def common():
                    ready(dt_sum)
                    ready(conv_silu_b, TANHS.index(("cv", "B")))
                    for c in range(TC):
                        last = pe.transpose(bank(3)[:, cols_of(c)], bf[:, cols_of(c)], ident[:])
                    last.then_inc(b_turned.sem, 1)
                    for a, src in enumerate((dtb, acb)):
                        for c in range(TC):
                            last = pe.transpose(bank(6)[:, a * 32 + c * 8:a * 32 + c * 8 + 8],
                                                src[:, cols_of(c)], ident[0:8, 0:8])
                    last.then_inc(dt_turned.sem, 1)
                    ready(conv_silu_b, TANHS.index(("cv", "C")))
                    for g in range(2):
                        gg = slice(HALF * g, HALF * g + HALF)
                        for c in range(TC):
                            last = mm(bank(4 + g)[:, cols_of(c)], bf[gg, cols_of(c)], cf[gg, cols_of(c)],
                                      start=True, stop=True)
                        last.then_inc(cb.sem, 1)

                conv_silu_b = tanh_used

                def hg_turn(p):
                    ready(hmul, 4 * p + 3)
                    if p == 0:
                        ready(b_tok)
                        ready(cb_masked, 1)
                        ready(dt_tok)
                    else:
                        ready(contrib_out, 4 * p - 1)
                    for c in range(TC):
                        last = pe.transpose(bank(3)[:, cols_of(c)], e4[:, cols_of(c)], ident[:])
                    last.then_inc(turned.sem, 1)
                    ready(proj_out, AT["i", p])
                    for c in range(TC):
                        last = pe.transpose(bank(4)[:, cols_of(c)], vf[:, cols_of(c)], ident[:])
                    last.then_inc(turned.sem, 1)
                    ready(hmul, 4 * p + 2)
                    for h in range(2):
                        hh = slice(HALF * h, HALF * h + HALF)
                        for c in range(TC):
                            last = mm(bank(5 + h)[:, cols_of(c)], e2[hh, cols_of(c)], e1[hh, cols_of(c)],
                                      start=True, stop=True)
                        last.then_inc(score.sem, 1)

                def hg_contribs(p):
                    ready(kd_tok, p)
                    ready(v_tok, 3 * p + 2)
                    ready(score_masked, 2 * p + 1)
                    for rr in range(4):
                        rows = slice(32 * rr, 32 * rr + 32)
                        for c in range(TC):
                            for h in range(2):
                                hh = slice(HALF * h, HALF * h + HALF)
                                last = mm(bank(3 + rr)[hh, cols_of(c)], kdt[rows, c, hh], vm[rows, c, :, hh],
                                          start=True, stop=True)
                        last.then_inc(contrib.sem, 1)

                def hg_outs(p):
                    ready(state, p)
                    ready(hmul, 4 * p + 1)
                    if p:
                        ready(o_out, 2 * p - 1)
                    for h in range(2):
                        hh = slice(HALF * h, HALF * h + HALF)
                        for c in range(TC):
                            mm(bank(7)[hh, cols_of(c)], vt[:, p % 2, c, hh], sm[:, p % 2, h, cols_of(c)],
                               start=c == 0, stop=False, skip_group_check=True)
                        for cc in range(NCC):
                            t = slice(cc * CH, cc * CH + CH)
                            last = mm(bank(7)[hh, t], ctr[hh, :, cc], e3[hh, p % 2, t],
                                      start=False, stop=cc == NCC - 1, skip_group_check=True)
                    last.then_inc(o_done.sem, 1)

                def ssd_turn(p):
                    ready(tanh_used, TANHS.index(("cv", p)))
                    ready(dt_tok)
                    if p == 0:
                        ready(contrib_out, 4 * NP - 1)
                    elif p in (2, 3):
                        ready(head_used, p - 2)
                    if p:
                        ready(xde_made, p - 1)
                        ready(seg, 2 * p - 1)
                    for c in range(TC):
                        last = pe.transpose(bank(3)[:, cols_of(c)], xs[:, p % 2, cols_of(c)], ident[:])
                    last.then_inc(x_tok.sem, 1)
                    for h in range(2):
                        k = 2 * p + h
                        mm(bank(4 + h), ident[0:8, k:k + 1].to_broadcast([8, P]), acb[:], start=True, stop=True)\
                            .then_inc(sums.sem, 1)

                def ssd_contribs(p):
                    gg = slice(HALF * (p // 2), HALF * (p // 2) + HALF)
                    ready(xde_made, p)
                    if p:
                        ready(s_state, p - 1)
                    for c in range(TC - 1):
                        last = mm(bank(6)[gg, cols_of(c)], bt[:, c, gg], xde[:, c, :], start=True, stop=True)
                    last.then_inc(s_contrib.sem, 1)

                def ssd_outs(p):
                    gg = slice(HALF * (p // 2), HALF * (p // 2) + HALF)
                    ready(s_state, p)
                    ready(lm_made, 2 * p + 1)
                    if p == 0:
                        ready(head_norm)
                    elif p == 3:
                        ready(group_read, 0)
                    else:
                        ready(y_gated, p - 1)
                    for h in range(2):
                        hh = slice(HALF * h, HALF * h + HALF)
                        for c in range(TC):
                            mm(bank(7)[hh, cols_of(c)], xdt[:, c, hh], lm[:, h, cols_of(c)],
                               start=c == 0, stop=False, skip_group_check=True)
                        for c in range(1, TC):
                            last = mm(bank(7)[hh, cols_of(c)], st[gg, c, hh], cx[gg, h, cols_of(c)],
                                      start=False, stop=c == TC - 1, skip_group_check=True)
                    last.then_inc(y_done.sem, 1)

                def head_sums():
                    ready(o_out, 2 * NP - 1)
                    for p in range(NP):
                        last = mm(bank(7)[0:8, :], headsum[:, 8 * p:8 * p + 8], km[:, p, :],
                                  start=p == 0, stop=p == NP - 1)
                    last.then_inc(head_sum.sem, 1)

                def head_spread(p, bk):
                    ready(head_norm)
                    ready(xde_made, p + 1 if p < 3 else 3)
                    for h in range(2):
                        k = 2 * p + h
                        last = mm(bank(bk)[HALF * h:HALF * h + HALF, :], ident[0:8, k:k + 1].to_broadcast([8, HALF]),
                                  rh[:], start=True, stop=True)
                    last.then_inc(head_rms.sem, 1)

                def group_sums(g, bk):
                    ready(y_sq, 2 * g + 1)
                    if g == 0:
                        ready(y_gated, 2)
                    mm(bank(bk), ones[:], sq[:], start=True, stop=False)
                    mm(bank(bk), ones[:], sqb[:], start=False, stop=True).then_inc(group_sum.sem, 1)

                for i, (n, k0, k1) in enumerate(PBLOCKS):
                    w = MIX0 + i
                    ready(split, w)
                    if k0 == 0:
                        ready(proj_out, n - 3)
                    for k in range(k0, k1):
                        if n == 0:
                            h_ready(1, k)
                        last = products(bank(n % 3), w % NS, k - k0, h_tile(k), k == 0, k == KD - 1)
                    last.then_inc(blk.sem, 1)
                    if k1 < KD:
                        continue
                    if n == 0:
                        norm_products(l, 1)
                    if n == 8:
                        common()
                    if n in (9, 11, 13, 15):
                        hg_turn((n - 9) // 2)
                    if n in (10, 12, 14, 16):
                        hg_contribs((n - 10) // 2)
                    if n in (11, 13, 15, 17):
                        hg_outs((n - 11) // 2)
                    if n in (20, 22, 24, 26):
                        if n == 26:
                            group_sums(0, 7)
                        ssd_outs((n - 20) // 2)
                    if n in (18, 20, 22, 24):
                        ssd_turn((n - 18) // 2)
                    if n in (19, 21, 23, 25):
                        ssd_contribs((n - 19) // 2)
                    if n == 19:
                        head_sums()
                    if n in (21, 23):
                        head_spread((n - 21) // 2, 3)
                    if n == 25:
                        head_spread(2, 3)
                        head_spread(3, 4)

                SOON, LATE = (0, 1, 4, 5, 6, 7), (2, 3)

                def out_products(m, ks):
                    w = OUT0 + m
                    for k in ks:
                        if m == 0:
                            if k < NP:
                                ready(ssd_low, k)
                            else:
                                ready(hg_low, k - NP)
                        moving = ((shi[:, k, :], slo[:, k, :]) if k < NP
                                  else (ohi[:, k - NP, :], olo[k - NP][:]))
                        last = products(bank(DOWN + m % 2), w % NS, k, moving, k == SOON[0], k == LATE[-1])
                    return last

                for m in (0, 1):
                    ready(split, OUT0 + m)
                    ready(x_tile, KD + m - 2)
                    out_products(m, SOON[:-1])
                    if m == 0:
                        group_sums(1, 6)
                for m in (0, 1):
                    out_products(m, SOON[-1:])
                    out_products(m, LATE).then_inc(blk.sem, 1)
                for m in range(2, KD):
                    ready(split, OUT0 + m)
                    ready(x_tile, KD + m - 2)
                    out_products(m, SOON)
                    out_products(m, LATE).then_inc(blk.sem, 1)
                ffn(1, FFN2)

            norm_products(DEPTH, 0)
            for m in range(KD):
                pe.wait_ge(out_made.sem, m + 1)
                for c in range(TC):
                    last = pe.transpose(bank(m)[:, c * P:(c + 1) * P], ont[:, m, c * P:(c + 1) * P], ident[:])
                last.then_inc(out_turned.sem, 1)


def kernel(**inputs):
    import concourse.bacc as bacc
    from concourse.bass_utils import run_bass_kernel_spmd

    a = {k: np.asarray(v) for k, v in inputs.items()}

    def tile_cols(v):
        return np.moveaxis(v.reshape(*v.shape[:-1], -1, P), -1, -2)

    def k_major(w, j0, n):
        w = w[:, :, j0:j0 + n]
        return w.reshape(w.shape[0], -1, P, n).transpose(0, 2, 1, 3)

    def col_tiles(w):
        d, k, n = w.shape
        return w.reshape(d, k // P, P, n // P, P).transpose(0, 3, 2, 1, 4).reshape(d, n // P, P, k)

    def up(gate, up_):
        t = np.stack([col_tiles(gate), col_tiles(up_)], axis=2)
        return np.ascontiguousarray(t.reshape(DEPTH, UP_BLOCKS, P, BW))

    def rows8(v):
        out = np.zeros((DEPTH, P, 1), np.float32)
        out[:, :8, 0] = v
        return out

    following = np.concatenate([a["ffn1_norm"][1:], a["final_norm"][None]])
    cols = np.concatenate([
        tile_cols(a["mix_norm"]), tile_cols(a["ffn2_norm"]), tile_cols(following),
        a["ssd_conv_w"].reshape(DEPTH, 4, 6, P).transpose(0, 3, 2, 1).reshape(DEPTH, P, 24),
        tile_cols(a["ssd_conv_b"]), tile_cols(a["ssd_norm_w"]),
        tile_cols(np.repeat(a["ssd_d"], HALF, axis=1)),
        np.tile(a["hg_norm_w"], (1, 2))[:, :, None],
        rows8(a["ssd_dt_bias"]), rows8(a["ssd_a_log"]),
    ], axis=2)
    w_in = a["w_in"]
    starts, at = {}, 0
    for name, width in (("z", 512), ("xs", 512), ("B", 128), ("C", 128), ("dt", 8), ("q", 512), ("f", 512),
                        ("i", 512), ("g", 512)):
        starts[name], at = at, at + width
    blocks = [k_major(w_in, starts[kind] + P * p, P).reshape(DEPTH, P, BW) for kind, p in PROJ if kind != "dt"]
    mix = np.concatenate([np.stack(blocks, axis=1), col_tiles(a["w_out"])], axis=1)
    arrays = {
        "x": a["x"], "cols": np.ascontiguousarray(cols.transpose(1, 0, 2)),
        "first_norm": np.ascontiguousarray(tile_cols(a["ffn1_norm"][0])),
        "logits": np.ascontiguousarray(tile_cols(a["hg_lb_logits"]).transpose(1, 0, 2)),
        "up1": up(a["ffn1_w_gate"], a["ffn1_w_up"]), "dn1": np.ascontiguousarray(col_tiles(a["ffn1_w_down"])),
        "mix": np.ascontiguousarray(mix), "dtw": np.ascontiguousarray(k_major(w_in, starts["dt"], 8)),
        "up2": up(a["ffn2_w_gate"], a["ffn2_w_up"]), "dn2": np.ascontiguousarray(col_tiles(a["ffn2_w_down"])),
    }
    nc = bacc.Bacc("TRN2", target_bir_lowering=False, num_devices=1)
    aps = [nc.dram_tensor(f"in_{k}", v.shape, mybir.dt.from_np(v.dtype), kind="ExternalInput").ap()
           for k, v in arrays.items()]
    out = nc.dram_tensor("out_0", a["x"].shape, F32, kind="ExternalOutput").ap()
    trunk_kernel(nc, *aps, out)
    r = run_bass_kernel_spmd(nc, [{f"in_{k}": v for k, v in arrays.items()}], core_ids=[0])
    return r.results[0]["out_0"]
```

```python
import numpy as np
import concourse.bass as bass
from concourse import mybir
from concourse.alu_op_type import AluOpType as ALU
from contextlib import ExitStack

F32 = mybir.dt.float32
F32R = mybir.dt.float32r
I32 = mybir.dt.int32
ACT = mybir.ActivationFunctionType
AX = mybir.AxisListType

P = 128
DEPTH = 2
T = 512
TC = T // P
D = 1024
KD = D // P
FF = 2816
NJ = FF // P
SSD_W = 512
GN = 128
NP = 4
HALF = 64
CH = 16
NCC = T // CH
CREF = CH // 2 - 1
EPS = 1e-6
BIG = 1e38
MAGIC = float(0x5F3759DF)

NS = 4
BW = KD * P
UP_BLOCKS = 2 * NJ
DN_PIECES = [(0, 8), (8, 15), (15, 22)]
DN_BLOCKS = KD * len(DN_PIECES)
PROJ = ([("f", 0), ("f", 1), ("B", 0), ("f", 2), ("dt", 0), ("f", 3), ("C", 0)]
        + [(k, p) for p in range(NP) for k in ("q", "i")]
        + [("g", 0)]
        + [(k, p) for p in range(NP) for k in ("xs", "z")]
        + [("g", 1), ("g", 2), ("g", 3)])
Q0, X0 = 7, 16
NPROJ = len(PROJ)
AT = {kp: n for n, kp in enumerate(PROJ)}
PBLOCKS = []
for _n, (_kind, _) in enumerate(PROJ):
    PBLOCKS += [(_n, 0, 4), (_n, 4, 8)] if _kind == "B" else [(_n, 0, 8)]
MIX0 = UP_BLOCKS + DN_BLOCKS
OUT0 = MIX0 + len(PBLOCKS)
FFN2 = OUT0 + KD
W = FFN2 + UP_BLOCKS + DN_BLOCKS
assert W % NS == 0 and MIX0 % NS == 0 and FFN2 % NS == 0
LAST_BLOCK = {n: MIX0 + i for i, (n, _, _) in enumerate(PBLOCKS)}

WN = 0
CW = WN + 3 * KD
CB = CW + 6 * 4
SN = CB + 6
DC = SN + NP
HN = DC + NP
DTB = HN + 1
ALOG = DTB + 1
NIN = ALOG + 1
LB = NIN
OLB = LB + NP
NEGA = OLB + NP
NCOL = NEGA + 1
CONV_B, CONV_C = 4, 5

TANHS = ([("cv", "B"), ("cv", "C")] + [("q", p) for p in range(NP)] + [("g", 0)]
         + [x for p in range(NP) for x in (("cv", p), ("z", p))] + [("g", 1), ("g", 2), ("g", 3)])
DVE_STEPS = 158
CONVS = ["B", "C", 0, 1, 2, 3]


class Event:

    def __init__(self, sem, per=0, before=0, credit=0):
        self.sem, self.per, self.first = sem, per, before + credit + 1

    def upto(self, l, k):
        return l * self.per + (k + self.first)


class Steps:

    def __init__(self, eng, sem):
        self.eng, self.sem, self.base, self.n = eng, sem, 0, 0

    def did(self, ins):
        ins.then_inc(self.sem, 1)
        self.n += 1

    def settle(self):
        self.eng.wait_ge(self.sem, self.base + self.n)


def trunk_kernel(nc, x_in, cols, first_norm, logits, up1, dn1, mix, dtw, up2, dn2, out):
    ctx = ExitStack()
    with ctx:
        def sb(name, shape, dt=F32, at=ctx):
            return at.enter_context(nc.sbuf_tensor(name, shape, dt))

        def ev(name, per=0, before=0, credit=0):
            return Event(ctx.enter_context(nc.semaphore(name)), per, before, credit)

        x = sb("x", [P, KD, T])
        hhi = sb("hhi", [P, KD, T], F32R)
        hlo = sb("hlo", [P, KD, T], F32R)
        raw = sb("raw", [P, NS, BW])
        whi = sb("whi", [P, NS, BW], F32R)
        wlo = sb("wlo", [P, NS, BW], F32R)
        r = sb("r", [P, T])
        t1 = sb("t1", [P, T])
        acc = sb("acc", [P, T])
        sq = sb("sq", [P, T])
        g2 = sb("g2", [P, 2, T])
        u2 = sb("u2", [P, 2, T])
        par = sb("par", [P, NCOL])
        par_all = sb("par_all", [P, DEPTH, NCOL])
        first = sb("first", [P, KD])
        lg = sb("lg", [P, DEPTH, NP])
        lt = sb("lt", [P, 3, NP])
        spare = sb("spare", [1, 1])
        ident = sb("ident", [P, P])
        ones = sb("ones", [P, P])
        causal = sb("causal", [P, P])
        block16 = sb("block16", [P, P])
        keep16 = sb("keep16", [P, T])
        rt = sb("rt", [P, TC])
        rht = sb("rht", [P, TC, 8])
        rgt = sb("rgt", [P, TC])
        ntn = sb("ntn", [P, 2, TC * 8])
        parity = sb("parity", [P, 2])
        par8 = sb("par8", [P, 2, 4])
        headsum = sb("headsum", [P, NP * 8])

        REGION = 27 * 1024 + 256 + 62 * 1024
        arena = sb("arena", [P, REGION // 4])
        base = nc.sbuf_base - REGION

        def place(name, shape, kib, dt=F32, start=0):
            assert start + kib * 1024 + 4 * int(np.prod(shape[1:])) <= REGION, name
            return nc.alloc_sbuf_tensor_at(name, shape, dt, offset=base + start + int(kib * 1024))

        ahi = place("ahi", [P, NJ, T], 0, F32R)
        alo = place("alo", [P, NJ, T], 44, F32R)
        stage = place("stage", [P, TC, D], 0)
        ont = place("ont", [P, KD, T], 16)
        b = place("b", [P, NP, T], 0)
        cf = place("cf", [P, T], 8)
        bt = place("bt", [P, TC, P], 10)
        cbm = place("cbm", [P, 2, TC, P], 12)
        acb = place("acb", [8, T], 16)
        dts = place("dts", [P, 2, TC, 8], 18)
        wend = place("wend", [P, TC, 8], 18.5)
        xr = place("xr", [P, 2, T + 3], 19)
        th = place("th", [P, 2, T], 23.25)
        S0 = 27 * 1024 + 256

        def put(name, shape, kib, dt=F32):
            return place(name, shape, kib, dt, S0)

        bf = put("bf", [P, T], 0)
        dtb = put("dtb", [8, T], 2)
        km = put("km", [P, NP, T], 4)
        e1 = put("e1", [P, T], 12)
        e2 = put("e2", [P, T], 14)
        e4 = put("e4", [P, T], 16)
        vf = put("vf", [P, T], 18)
        kdt = put("kdt", [P, TC, P], 20)
        vm = put("vm", [P, TC, 2, P], 22)
        vt = put("vt", [P, 2, TC, P], 26)
        e3 = put("e3", [P, 2, T], 30)
        sm = put("sm", [P, 2, 2, T], 34)
        dec = put("dec", [P, HALF, NCC + 1], 42)
        ctr = put("ctr", [P, HALF, NCC + 1], 50.25)
        xdt = put("xdt", [P, TC, P], 0)
        xde = put("xde", [P, TC, P], 2)
        gs = put("gs", [P, 2, T], 12)
        xs = put("xs", [P, 2, T], 16)
        zs = put("zs", [P, 2, T], 20)
        lm = put("lm", [P, 2, T], 24)
        cx = put("cx", [P, 2, T], 28)
        st = put("st", [P, TC, P], 32)
        y2 = put("y2", [P, 3, T], 34)
        sqb = put("sqb", [P, T], 58)
        shi = put("shi", [P, NP, T], 42, F32R)
        slo = put("slo", [P, NP, T], 50, F32R)
        ohi = put("ohi", [P, NP, T], 4, F32R)
        olo = [put(f"olo{p}", [P, T], kib, F32R) for p, kib in enumerate((40, 2, 60, 58))]
        eh = u2

        ps = ctx.enter_context(nc.psum_tensor("ps", [P, 8, T], F32))

        def bank(i):
            return ps[:, i, :]

        def in_tiles(ap):
            return ap.rearrange("p (c t) -> p c t", c=TC)

        DOWN, NORM, GROUP = 4, 6, (7, 6)

        loaded = ev("loaded")
        stored = ev("stored")
        consts = ev("consts")
        full = [ev(f"raw_full{s}") for s in range(NS)]
        high = ev("high", W)
        split = ev("split", W, credit=NS)
        blk = ev("blk", W, credit=NS)
        par_set = ev("par_set", 1)
        par_made = ev("par_made")
        lg_max = ev("lg_max")
        lg_exp = ev("lg_exp")
        x_turned = ev("x_turned")
        x_tile = ev("x_tile", 3 * KD, KD, 2)
        x_high = ev("x_high", 3 * KD, KD)
        x_low = ev("x_low", 3 * KD, KD)
        x_sq = ev("x_sq", 3 * KD, KD)
        x_sum = ev("x_sum", 3 * KD, KD)
        norm_sum = ev("norm_sum", 3)
        norm_rms = ev("norm_rms", 3)
        norm_spread = ev("norm_spread", 3)
        g_out = ev("g_out", 2 * NJ, credit=2)
        u_out = ev("u_out", 2 * NJ, credit=2)
        silu_g = ev("silu_g", 2 * NJ)
        hid = ev("hid", 2 * NJ)
        hid_high = ev("hid_high", 2 * NJ)
        hid_low = ev("hid_low", 2 * NJ)
        dve_step = ctx.enter_context(nc.semaphore("dve_step"))
        proj_out = ev("proj_out", NPROJ, credit=3)
        tanh = ev("tanh", len(TANHS))
        tanh_used = ev("tanh_used", len(TANHS), credit=2)
        f_exp = ev("f_exp", NP)
        f_gate = ev("f_gate", NP)
        f_log = ev("f_log", NP)
        f_sum = ev("f_sum", NP)
        dt_abs = ev("dt_abs", 1)
        dt_exp = ev("dt_exp", 1)
        dt_log = ev("dt_log", 1)
        dt_sum = ev("dt_sum", 1)
        conv = ev("conv", 6)
        conv_silu = ev("conv_silu", 6)
        b_turned = ev("b_turned", 1)
        b_tok = ev("b_tok", 1)
        cb = ev("cb", 2)
        cb_masked = ev("cb_masked", 2)
        dt_turned = ev("dt_turned", 1)
        dt_tok = ev("dt_tok", 1)
        dist = ev("dist", 2 * NP)
        hexp = ev("hexp", 4 * NP)
        hmul = ev("hmul", 4 * NP)
        turned = ev("turned", 2 * NP)
        score = ev("score", 2 * NP)
        score_masked = ev("score_masked", 2 * NP)
        kd_tok = ev("kd_tok", NP)
        v_tok = ev("v_tok", 3 * NP)
        contrib = ev("contrib", 4 * NP)
        contrib_out = ev("contrib_out", 4 * NP)
        decay = ev("decay", NP)
        state = ev("state", NP)
        o_done = ev("o_done", NP)
        o_out = ev("o_out", 2 * NP)
        head_sum = ev("head_sum", 1)
        head_norm = ev("head_norm", 1)
        head_spread = ev("head_spread", 2 * NP)
        head_used = ev("head_used", NP)
        hg_y = ev("hg_y", NP)
        hg_high = ev("hg_high", NP)
        hg_low = ev("hg_low", NP)
        x_tok = ev("x_tok", NP)
        sums = ev("sums", 2 * NP)
        sums_exp = ev("sums_exp", 2 * NP)
        last_sums = ev("last_sums", 1)
        to_end = ev("to_end", 1)
        to_end_exp = ev("to_end_exp", 1)
        seg = ev("seg", 2 * NP)
        seg_exp = ev("seg_exp", 2 * NP)
        xdt_made = ev("xdt_made", NP)
        xde_made = ev("xde_made", NP)
        lm_made = ev("lm_made", 2 * NP)
        cx_made = ev("cx_made", 2 * NP)
        s_contrib = ev("s_contrib", NP)
        s_state = ev("s_state", NP)
        y_done = ev("y_done", NP)
        y_gated = ev("y_gated", NP)
        y_sq = ev("y_sq", NP)
        group_sum = ev("group_sum", 2)
        group_norm = ev("group_norm", 2)
        group_spread = ev("group_spread", 2)
        ssd_y = ev("ssd_y", NP)
        ssd_high = ev("ssd_high", NP)
        ssd_low = ev("ssd_low", NP)
        out_made = ev("out_made")
        out_turned = ev("out_turned")
        out_tok = ev("out_tok")

        block = ctx.enter_context(nc.Block())

        @block.sync
        def _(sp):
            sp.dma_start(stage[:], x_in.rearrange("b (c p) d -> p (b c) d", p=P)).then_inc(loaded.sem, 16)
            sp.dma_start(par_all[:, :, 0:NIN], cols).then_inc(loaded.sem, 16)
            sp.dma_start(first[:], first_norm).then_inc(loaded.sem, 16)
            sp.dma_start(lg[:], logits).then_inc(loaded.sem, 16)
            with sp.Fori(0, DEPTH) as l:
                def load(w, q, dst, src):
                    sp.wait_ge(split.sem, split.upto(l, w - NS))
                    sp.dma_start(dst, src).then_inc(full[q].sem, 16)

                def ffn(wb, up, dn):
                    with sp.Fori(0, UP_BLOCKS // NS) as i:
                        for q in range(NS):
                            load(wb + NS * i + q, q, raw[:, q, :], up[l, NS * i + q])
                    for m in range(KD):
                        for s, (j0, j1) in enumerate(DN_PIECES):
                            w = wb + UP_BLOCKS + 3 * m + s
                            load(w, w % NS, raw[:, w % NS, 0:(j1 - j0) * P], dn[l, m, :, j0 * P:j1 * P])

                ffn(0, up1, dn1)
                for i, (n, k0, k1) in enumerate(PBLOCKS):
                    w = MIX0 + i
                    if PROJ[n][0] == "dt":
                        load(w, w % NS, raw[:, w % NS, :].rearrange("p (k m) -> p k m", k=KD)[:, :, 0:8],
                             dtw[l])
                    else:
                        load(w, w % NS, raw[:, w % NS, 0:(k1 - k0) * P],
                             mix[l, n - (n > AT["dt", 0]), :, k0 * P:k1 * P])
                for m in range(KD):
                    w = OUT0 + m
                    load(w, w % NS, raw[:, w % NS, :], mix[l, NPROJ - 1 + m])
                ffn(FFN2, up2, dn2)
            sp.wait_ge(out_tok.sem, KD)
            sp.dma_start(out.rearrange("b (c p) d -> p (b c) d", p=P), stage[:]).then_inc(stored.sem, 16)
            sp.wait_ge(stored.sem, 16)

        @block.gpsimd
        def _(pool):
            def made(ins, n):
                ins.then_inc(consts.sem, 1)
                pool.wait_ge(consts.sem, n)

            made(pool.memset(ident[:], 0.0), 1)
            made(pool.affine_select(out=ident[:], in_=ident[:], compare_op=ALU.not_equal, fill=1.0, base=0,
                                    pattern=[[-1, P]], channel_multiplier=1), 2)
            made(pool.memset(ones[:], 1.0), 3)
            made(pool.memset(causal[:], 1.0), 4)
            made(pool.affine_select(out=causal[:], in_=causal[:], compare_op=ALU.is_ge, fill=0.0, base=0,
                                    pattern=[[1, P]], channel_multiplier=-1), 5)
            made(pool.affine_select(out=block16[:].rearrange("p (c i) -> p c i", i=CH),
                                    in_=causal[:].rearrange("p (c i) -> p c i", i=CH),
                                    compare_op=ALU.is_ge, fill=0.0, base=0,
                                    pattern=[[-CH, P // CH], [0, CH]], channel_multiplier=1), 6)
            made(pool.memset(keep16[:], 1.0), 7)
            made(pool.memset(keep16[:, 0:T:CH], 0.0), 8)
            made(pool.memset(par8[:], 1.0), 9)
            made(pool.affine_select(out=par8[:], in_=par8[:], compare_op=ALU.is_ge, fill=0.0, base=0,
                                    pattern=[[-CH, 2], [-2 * CH, 4]], channel_multiplier=1), 10)
            made(pool.affine_select(out=par8[:], in_=par8[:], compare_op=ALU.is_ge, fill=0.0, base=CH - 1,
                                    pattern=[[CH, 2], [2 * CH, 4]], channel_multiplier=-1), 11)
            made(pool.memset(headsum[:], 0.0), 12)
            made(pool.memset(headsum[0:HALF, 0:31:10], 1.0), 13)
            made(pool.memset(headsum[HALF:P, 1:32:10], 1.0), 14)
            for q in range(NS):
                pool.sem_inc(split.sem, 1)
            with pool.Fori(0, DEPTH * W // NS) as i:
                for q in range(NS):
                    pool.wait_ge(high.sem, NS * i + (q + 1))
                    pool.tensor_tensor(wlo[:, q, :], raw[:, q, :], whi[:, q, :].bitcast(F32),
                                       ALU.subtract).then_inc(split.sem, 1)

        @block.scalar
        def _(act):
            act.wait_ge(lg_max.sem, 1)
            act.activation(lg[:], lg[:], ACT.Exp).then_inc(lg_exp.sem, 1)
            act.activation(par_all[:, :, NEGA:NEGA + 1], par_all[:, :, ALOG:ALOG + 1], ACT.Exp)\
               .then_inc(lg_exp.sem, 1)

            def residual(l, k, gain):
                m = k % KD
                act.wait_ge(x_tile.sem, x_tile.upto(l, k))
                act.activation(hhi[:, m, :], x[:, m, :], ACT.Copy, scale=gain).then_inc(x_high.sem, 1)
                if not (isinstance(l, int) and l == 0 and k == -KD):
                    act.wait_ge(x_sum.sem, x_sum.upto(l, k - 1))
                act.activation(sq[:], x[:, m, :], ACT.Square).then_inc(x_sq.sem, 1)

            for m in range(KD):
                residual(0, m - KD, first[:, m:m + 1])

            with act.Fori(0, DEPTH) as l:
                def hi(w, q=None):
                    q = w % NS if q is None else q
                    act.wait_ge(full[q].sem, 16 * ((w - q) // NS + l * (W // NS)) + 16)
                    act.wait_ge(blk.sem, blk.upto(l, w - NS))
                    act.activation(whi[:, q, :], raw[:, q, :], ACT.Copy).then_inc(high.sem, 1)

                def hi_i(wb, i, q):
                    act.wait_ge(full[q].sem, 16 * (wb // NS + 1) + 16 * i + l * (16 * W // NS))
                    act.wait_ge(blk.sem, blk.upto(l, wb + q - NS) + NS * i)
                    act.activation(whi[:, q, :], raw[:, q, :], ACT.Copy).then_inc(high.sem, 1)

                for q in range(NS):
                    hi(q)

                def ffn(c, wb, k0, gain0):
                    with act.Fori(0, NJ // 2) as i:
                        for jj in range(2):
                            k = NJ * c + jj
                            act.wait_ge(g_out.sem, g_out.upto(l, k) + 2 * i)
                            act.activation(g2[:, jj, :], g2[:, jj, :], ACT.Silu).then_inc(silu_g.sem, 1)
                            hi_i(wb + NS, i, 2 * jj)
                            act.wait_ge(hid.sem, hid.upto(l, k) + 2 * i)
                            act.activation(ahi[:, 2 * i + jj, :], u2[:, jj, :], ACT.Copy).then_inc(hid_high.sem, 1)
                            hi_i(wb + NS, i, 2 * jj + 1)
                    for m in range(KD):
                        for s in range(3):
                            w = wb + UP_BLOCKS + 3 * m + s
                            if w + NS < W:
                                hi(w + NS)
                        residual(l, k0 + m, par[:, gain0 + m:gain0 + m + 1])

                act.wait_ge(par_set.sem, par_set.upto(l, 0))
                ffn(0, 0, 0, WN)

                def ready(e, k=0):
                    act.wait_ge(e.sem, e.upto(l, k))

                def do(e, out, in_, f, **kw):
                    act.activation(out, in_, f, **kw).then_inc(e.sem, 1)

                def do_tanh(kind, src):
                    i = TANHS.index(kind)
                    ready(tanh_used, i - 2)
                    do(tanh, th[:, i % 2, :], src, ACT.Tanh)

                def conv_src(t):
                    return {"B": bf[:], "C": cf[:]}[t] if isinstance(t, str) else xs[:, t % 2, :]

                def conv_tanh(t):
                    ready(conv, CONVS.index(t))
                    do_tanh(("cv", t), conv_src(t))

                def plain_tanh(kind, p):
                    ready(proj_out, AT[kind, p])
                    do_tanh((kind, p), g2[:, 0, :])

                def hg_exps(p):
                    ready(dist, 2 * p)
                    do(hexp, e2[:], e1[:], ACT.Exp, scale=-1.0)
                    do(hexp, e1[:], e1[:], ACT.Exp)
                    if p >= 2:
                        ready(o_done, p - 2)
                    do(hexp, e3[:, p % 2, :], b[:, p, :], ACT.Exp)
                    ready(dist, 2 * p + 1)
                    do(hexp, e4[:], e4[:], ACT.Exp)

                def hg_copies(p):
                    ready(turned, 2 * p)
                    do(kd_tok, kdt[:].rearrange("p c n -> p (c n)"), bank(3), ACT.Copy)
                    ready(turned, 2 * p + 1)
                    if p >= 2:
                        ready(o_done, p - 2)
                    do(v_tok, vt[:, p % 2, :, :].rearrange("p c n -> p (c n)"), bank(4), ACT.Copy)
                    for j in range(2):
                        do(v_tok, vm[:, :, j, :], in_tiles(bank(4)), ACT.Copy, scale=parity[:, j:j + 1])

                def hg_contrib(p):
                    if p >= 1:
                        ready(state, p - 1)
                    else:
                        ready(f_sum, NP - 1)
                    do(decay, dec[:, :, 1:NCC + 1],
                       b[:, p, CH - 1:T:CH].unsqueeze(1).to_broadcast([P, HALF, NCC]), ACT.Exp)
                    for rr in range(4):
                        ready(contrib, 4 * p + rr)
                        do(contrib_out,
                           ctr[:, :, 1:NCC + 1].rearrange("p v (c r q) -> p r c q v", r=4, q=2)[:, rr],
                           bank(3 + rr).rearrange("p (c q v) -> p c q v", c=TC, q=2), ACT.Copy)

                def hg_out(p):
                    ready(o_done, p)
                    do(o_out, km[:, p, :], bank(7), ACT.Square)
                    do(o_out, b[:, p, :], bank(7), ACT.Copy)

                def ssd_exps(p):
                    for h in range(2):
                        k = 2 * p + h
                        ready(sums, k)
                        if p >= 1:
                            ready(s_state, p - 1)
                        do(sums_exp, eh[:, h, :], bank(4 + h), ACT.Exp)
                    for h in range(2):
                        k = 2 * p + h
                        ready(seg, k)
                        do(seg_exp, lm[:, h, :], lm[:, h, :], ACT.Exp)

                def ssd_sq(p):
                    ready(y_gated, p)
                    if p == 2:
                        ready(group_sum, 0)
                    do(y_sq, sqb[:] if p % 2 else sq[:], y2[:, p % 3, :], ACT.Square)

                def ssd_hi(p):
                    ready(ssd_y, p)
                    do(ssd_high, shi[:, p, :], y2[:, p % 3, :], ACT.Copy)

                def hg_hi(p):
                    ready(hg_y, p)
                    do(hg_high, ohi[:, p, :], b[:, p, :], ACT.Copy)

                for n, (kind, pr) in enumerate(PROJ):
                    for i, (nn, _, _) in enumerate(PBLOCKS):
                        if nn == n:
                            hi(MIX0 + i + NS)
                    if kind == "f":
                        ready(proj_out, n)
                        do(f_exp, km[:, pr, :], g2[:, pr % 2, :], ACT.Exp, scale=-1.0)
                    if kind == "dt":
                        ready(dt_abs)
                        do(dt_exp, acb[:], acb[:], ACT.Exp)
                    if kind == "B":
                        conv_tanh("B")
                    if kind == "C":
                        for p in range(NP):
                            ready(f_gate, p)
                            do(f_log, b[:, p, :], b[:, p, :], ACT.Ln)
                        ready(dt_exp)
                        do(dt_log, acb[:], acb[:], ACT.Ln, bias=1.0)
                        conv_tanh("C")
                    if n == Q0:
                        plain_tanh("q", 0)
                        hg_exps(0)
                    if n == Q0 + 1:
                        ready(b_turned)
                        do(b_tok, bt[:].rearrange("p c n -> p (c n)"), bank(3), ACT.Copy)
                    if n in (9, 11, 13):
                        p = (n - 9) // 2
                        plain_tanh("q", p + 1)
                        hg_copies(p)
                        hg_exps(p + 1)
                    if n == 10:
                        ready(to_end)
                        do(to_end_exp, wend[:], wend[:], ACT.Exp)
                    if n == 15:
                        plain_tanh("g", 0)
                        hg_copies(3)
                    if n in (10, 12, 14, 16):
                        hg_contrib((n - 10) // 2)
                    if n in (12, 14, 16):
                        hg_out((n - 12) // 2)
                    if kind == "xs":
                        conv_tanh(pr)
                    if kind == "z":
                        plain_tanh("z", pr)
                        if pr == 0:
                            hg_out(3)
                        ssd_exps(pr)
                        if pr:
                            ssd_sq(pr - 1)
                    if n == 20:
                        hg_hi(0)
                    if kind == "g" and pr:
                        plain_tanh("g", pr)
                        if pr == 2:
                            ssd_hi(0)
                            ssd_hi(1)
                        hg_hi(pr)
                        if pr == 2:
                            ssd_sq(3)
                ssd_hi(2)
                ssd_hi(3)
                for m in range(KD):
                    hi(OUT0 + m + NS)
                    residual(l, KD + m, par[:, WN + KD + m:WN + KD + m + 1])
                ffn(1, FFN2, 2 * KD, WN + 2 * KD)

        @block.vector
        def _(dve):
            own = Steps(dve, dve_step)
            did, settle = own.did, own.settle
            tt, ts, stt = dve.tensor_tensor, dve.tensor_scalar, dve.scalar_tensor_tensor

            def rsqrt(e, dst, src, scale):
                n = src.shape[1]
                ms, tmp = ntn[:, 0, 0:n], ntn[:, 1, 0:n]
                did(ts(ms, src, scale, EPS, ALU.mult, ALU.add))
                settle()
                did(ts(dst.bitcast(I32), ms.bitcast(I32), -0.5, MAGIC, ALU.mult, ALU.add))
                for step in range(3):
                    settle()
                    did(stt(tmp, dst, -0.5, dst, ALU.mult, ALU.mult))
                    settle()
                    did(tt(tmp, tmp, ms, ALU.mult))
                    settle()
                    ins = stt(dst, tmp, 1.5, dst, ALU.add, ALU.mult)
                    if step < 2:
                        did(ins)
                    else:
                        ins.then_inc(e.sem, 1)

            def residual(l, k, gain, update):
                m = k % KD
                update(m).then_inc(x_tile.sem, 1)
                dve.wait_ge(x_high.sem, x_high.upto(l, k))
                stt(hlo[:, m, :], x[:, m, :], gain, hhi[:, m, :].bitcast(F32), ALU.mult, ALU.subtract)\
                    .then_inc(x_low.sem, 1)
                dve.wait_ge(x_sq.sem, x_sq.upto(l, k))
                if m == 0:
                    dve.tensor_copy(acc[:], sq[:]).then_inc(x_sum.sem, 1)
                else:
                    dve.wait_ge(x_sum.sem, x_sum.upto(l, k - 1))
                    tt(acc[:], acc[:], sq[:], ALU.add).then_inc(x_sum.sem, 1)

            def norm(l, ph):
                dve.wait_ge(norm_sum.sem, norm_sum.upto(l, ph))
                rsqrt(norm_rms, rt[:], bank(NORM)[:, 0:TC], 1.0 / D)

            def norm_copy(l, ph):
                dve.wait_ge(norm_spread.sem, norm_spread.upto(l, ph))
                did(dve.tensor_copy(r[:], bank(NORM)))

            for e, n in ((g_out, 2), (u_out, 2), (proj_out, 3), (x_tile, 2), (tanh_used, 2)):
                for _ in range(n):
                    dve.sem_inc(e.sem, 1)

            dve.wait_ge(loaded.sem, 64)
            did(dve.tensor_copy(lt[:, 0, :], lg[:, 0, :]))
            for d in range(1, DEPTH):
                settle()
                did(tt(lt[:, 0, :], lt[:, 0, :], lg[:, d, :], ALU.max))
            settle()
            tt(lg[:], lg[:], lt[:, 0:1, :].to_broadcast([P, DEPTH, NP]), ALU.subtract).then_inc(lg_max.sem, 1)
            did(ts(par_all[:, :, CW:SN], par_all[:, :, CW:SN], 0.5, None, ALU.mult))
            dve.wait_ge(lg_exp.sem, 2)
            did(ts(par_all[:, :, NEGA:NEGA + 1], par_all[:, :, NEGA:NEGA + 1], -1.0, None, ALU.mult))
            did(dve.tensor_copy(lt[:, 0, :], lg[:, 0, :]))
            for d in range(1, DEPTH):
                settle()
                did(tt(lt[:, 0, :], lt[:, 0, :], lg[:, d, :], ALU.add))
            settle()
            did(dve.reciprocal(lt[:, 1, :], lt[:, 0, :]))
            settle()
            did(tt(lg[:], lg[:], lt[:, 1:2, :].to_broadcast([P, DEPTH, NP]), ALU.mult))
            settle()
            did(dve.tensor_copy(lt[:, 2, :], lg[:, 0, :]))
            for d in range(DEPTH):
                settle()
                if d:
                    did(tt(lt[:, 2, :], lt[:, 2, :], lg[:, d, :], ALU.add))
                    settle()
                did(tt(par_all[:, d, LB:LB + NP], lt[:, 2, :], lg[:, 0, :], ALU.subtract))
            settle()
            did(ts(par_all[:, :, OLB:OLB + NP], par_all[:, :, LB:LB + NP], -1.0, 1.0, ALU.mult, ALU.add))
            dve.wait_ge(consts.sem, 14)
            dve.reduce_sum(parity[:], par8[:], AX.X).then_inc(par_made.sem, 1)

            for m in range(KD):
                def turned_in(m):
                    dve.wait_ge(x_turned.sem, m + 1)
                    return dve.tensor_copy(x[:, m, :], bank(DOWN + m % 2))
                residual(0, m - KD, first[:, m:m + 1], turned_in)
            ahead = own.n

            with dve.Fori(0, DEPTH) as l:
                own.base, own.n = l * DVE_STEPS + ahead, 0
                dve.wait_ge(dve_step, own.base)
                dve.wait_ge(x_low.sem, x_low.upto(l, -1))
                dve.tensor_copy(par[:], par_all[:, l, :]).then_inc(par_set.sem, 1)
                dve.wait_ge(par_set.sem, par_set.upto(l, 0))

                def ready(e, k=0):
                    dve.wait_ge(e.sem, e.upto(l, k))

                def made(e, ins):
                    ins.then_inc(e.sem, 1)

                def alone():
                    settle()
                    did(dve.memset(spare[:], 0.0))

                def col(c):
                    return par[:, c:c + 1]

                def ffn(c, wb, k0, gain0):
                    norm(l, 2 * c)
                    norm_copy(l, 2 * c)
                    alone()
                    with dve.Fori(0, NJ // 2) as i:
                        for jj in range(2):
                            k = NJ * c + jj
                            dve.wait_ge(blk.sem, blk.upto(l, wb + 2 * jj) + NS * i)
                            made(g_out, tt(g2[:, jj, :], bank(jj), r[:], ALU.mult))
                            dve.wait_ge(blk.sem, blk.upto(l, wb + 2 * jj + 1) + NS * i)
                            made(u_out, tt(u2[:, jj, :], bank(2 + jj), r[:], ALU.mult))
                            dve.wait_ge(u_out.sem, u_out.upto(l, k) + 2 * i)
                            dve.wait_ge(silu_g.sem, silu_g.upto(l, k) + 2 * i)
                            made(hid, tt(u2[:, jj, :], g2[:, jj, :], u2[:, jj, :], ALU.mult))
                            dve.wait_ge(hid_high.sem, hid_high.upto(l, k) + 2 * i)
                            made(hid_low, tt(alo[:, 2 * i + jj, :], u2[:, jj, :],
                                             ahi[:, 2 * i + jj, :].bitcast(F32), ALU.subtract))
                    for m in range(KD):
                        def down(m):
                            ready(blk, wb + UP_BLOCKS + 3 * m + 2)
                            return stt(x[:, m, :], bank(DOWN + m % 2), 0.5, x[:, m, :], ALU.mult, ALU.add)
                        residual(l, k0 + m, col(gain0 + m), down)

                ffn(0, 0, 0, WN)

                norm(l, 1)

                def evac(n):
                    kind, p = PROJ[n]
                    ready(blk, LAST_BLOCK[n])
                    src = bank(n % 3)
                    if kind == "f":
                        made(proj_out, tt(g2[:, p % 2, :], src, r[:], ALU.mult))
                    elif kind == "dt":
                        made(proj_out, tt(dtb[:], src[0:8, :], r[0:8, :], ALU.mult))
                    elif kind in ("B", "C", "xs"):
                        made(proj_out, tt(xr[:, n % 2, 3:T + 3], src, r[:], ALU.mult))
                    elif kind == "i":
                        made(proj_out, tt(vf[:], src, r[:], ALU.mult))
                    else:
                        before = [t for t in TANHS[:TANHS.index((kind, p))] if t[0] != "cv"]
                        if before:
                            ready(tanh_used, TANHS.index(before[-1]))
                        made(proj_out, stt(g2[:, 0, :], src, 0.5, r[:], ALU.mult, ALU.mult))

                def silu(kind, half, dst, e=None):
                    i = TANHS.index(kind)
                    ready(tanh, i)
                    made(tanh_used, stt(dst, th[:, i % 2, :], 1.0, half, ALU.add, ALU.mult))

                def gate_f(p):
                    ready(f_exp, p)
                    did(ts(t1[:], km[:, p, :], BIG, 1.0, ALU.min, ALU.add))
                    settle()
                    did(dve.reciprocal(acc[:], t1[:]))
                    settle()
                    did(stt(km[:, p, :], km[:, p, :], BIG, acc[:], ALU.min, ALU.mult))
                    made(f_gate, ts(b[:, p, :], acc[:], col(OLB + p), col(LB + p), ALU.mult, ALU.add))

                def scan_f(p):
                    ready(f_log, p)
                    made(f_sum, dve.tensor_tensor_scan(b[:, p, :], keep16[:], b[:, p, :], 0.0,
                                                       ALU.mult, ALU.add))

                def dt_first():
                    ready(proj_out, AT["dt", 0])
                    did(ts(dtb[:], dtb[:], par[0:8, DTB:DTB + 1], None, ALU.add))
                    settle()
                    made(dt_abs, stt(acb[:], dtb[:], -1.0, dtb[:], ALU.mult, ALU.min))

                def dt_rest():
                    ready(dt_log)
                    did(stt(dtb[:], dtb[:], 0.0, acb[:], ALU.max, ALU.add))
                    settle()
                    did(ts(acb[:], dtb[:], par[0:8, NEGA:NEGA + 1], None, ALU.mult))
                    settle()
                    for c in range(TC):
                        a = acb[:, c * P:(c + 1) * P]
                        ins = dve.tensor_tensor_scan(a, ones[0:8, :], a, 0.0, ALU.mult, ALU.add)
                        if c < TC - 1:
                            did(ins)
                        else:
                            made(dt_sum, ins)

                def convolve(t, n):
                    dst = {"B": bf[:], "C": cf[:]}[t] if isinstance(t, str) else xs[:, t % 2, :]
                    i = {"B": CONV_B, "C": CONV_C}.get(t, t)
                    ready(proj_out, n)
                    did(ts(dst, xr[:, n % 2, 0:T], col(CW + 4 * i), col(CB + i), ALU.mult, ALU.add))
                    for k in range(1, 4):
                        settle()
                        ins = stt(dst, xr[:, n % 2, k:T + k], col(CW + 4 * i + k), dst, ALU.mult, ALU.add)
                        if k < 3:
                            did(ins)
                        else:
                            made(conv, ins)
                    ready(conv, CONVS.index(t))

                def conv_out(t):
                    dst = {"B": bf[:], "C": cf[:]}[t] if isinstance(t, str) else xs[:, t % 2, :]
                    silu(("cv", t), dst, dst)

                def hg_dist(p):
                    if p >= 1:
                        ready(score, 2 * p - 1)
                    ready(f_sum, p)
                    bb = b[:, p, :].rearrange("p (c i) -> p c i", i=CH)
                    made(dist, tt(e1[:].rearrange("p (c i) -> p c i", i=CH), bb,
                                  bb[:, :, CREF:CREF + 1].to_broadcast([P, NCC, CH]), ALU.subtract))
                    made(dist, tt(e4[:].rearrange("p (c i) -> p c i", i=CH),
                                  bb[:, :, CH - 1:CH].to_broadcast([P, NCC, CH]), bb, ALU.subtract))

                def hg_q(p):
                    ready(proj_out, AT["q", p])
                    silu(("q", p), g2[:, 0, :], g2[:, 1, :])
                    ready(tanh_used, TANHS.index(("q", p)))
                    ready(hexp, 4 * p + 1)
                    made(hmul, tt(e1[:], g2[:, 1, :], e1[:], ALU.mult))
                    ready(hexp, 4 * p + 2)
                    made(hmul, tt(e3[:, p % 2, :], g2[:, 1, :], e3[:, p % 2, :], ALU.mult))

                def hg_k(p):
                    made(hmul, stt(e2[:], km[:, p, :], col(OLB + p), e2[:], ALU.mult, ALU.mult))
                    ready(hexp, 4 * p + 3)
                    made(hmul, stt(e4[:], km[:, p, :], col(OLB + p), e4[:], ALU.mult, ALU.mult))

                def hg_mask(p):
                    if p >= 2:
                        ready(o_done, p - 2)
                    for h in range(2):
                        ready(score, 2 * p + h)
                        alone()
                        made(score_masked, dve.copy_predicated(
                            in_tiles(sm[:, p % 2, h, :]),
                            block16[:].bitcast(I32).unsqueeze(1).to_broadcast([P, TC, P]),
                            in_tiles(bank(5 + h))))

                def hg_scan(p):
                    ready(decay, p)
                    ready(contrib_out, 4 * p + 3)
                    made(state, dve.tensor_tensor_scan(
                        ctr[:].rearrange("p v c -> p (v c)"), dec[:].rearrange("p v c -> p (v c)"),
                        ctr[:].rearrange("p v c -> p (v c)"), 0.0, ALU.mult, ALU.add))

                def ssd_common():
                    for g in range(2):
                        ready(cb, g)
                        made(cb_masked, tt(cbm[:, g], in_tiles(bank(4 + g)),
                                           causal[:].unsqueeze(1).to_broadcast([P, TC, P]), ALU.mult))
                    ready(dt_turned)
                    made(dt_tok, dve.tensor_copy(dts[:].rearrange("p a c h -> p (a c h)"),
                                                 bank(6)[:, 0:2 * TC * 8]))

                def by_head(ap, p):
                    return ap[:, :, 2 * p:2 * p + 2].unsqueeze(3).to_broadcast([P, TC, 2, HALF])

                def ends():
                    ready(last_sums)
                    made(to_end, tt(wend[:], bank(7)[:, 0:TC * 8].rearrange("p (c h) -> p c h", c=TC), dts[:, 1],
                                    ALU.subtract))

                def end_weights():
                    ready(to_end_exp)
                    did(tt(wend[:], wend[:], dts[:, 0], ALU.mult))

                def ssd_main(p):
                    g = p // 2
                    gg = slice(HALF * g, HALF * g + HALF)
                    xtok = bank(3).rearrange("p (c h n) -> p c h n", c=TC, h=2)
                    ready(x_tok, p)
                    if p == 0:
                        settle()
                    made(xde_made, tt(xde[:].rearrange("p c (h n) -> p c h n", h=2), xtok,
                                      by_head(wend[:], p), ALU.mult))
                    if p:
                        ready(y_done, p - 1)
                    made(xdt_made, tt(xdt[:].rearrange("p c (h n) -> p c h n", h=2), xtok,
                                      by_head(dts[:, 0], p), ALU.mult))
                    for h in range(2):
                        k = 2 * p + h
                        ready(sums_exp, k)
                        for c in range(TC):
                            ins = ts(lm[:, h, c * P:(c + 1) * P], in_tiles(bank(4 + h))[:, c, :],
                                     dts[:, 1, c, k:k + 1], 0.0, ALU.subtract, ALU.min)
                            if c < TC - 1:
                                did(ins)
                            else:
                                made(seg, ins)
                    for h in range(2):
                        made(cx_made, tt(cx[gg, h, :], cf[gg, :], eh[gg, h, :], ALU.mult))
                    for h in range(2):
                        ready(seg_exp, 2 * p + h)
                        made(lm_made, tt(in_tiles(lm[:, h, :]), in_tiles(lm[:, h, :]), cbm[:, g], ALU.mult))

                def ssd_states(p):
                    g = p // 2
                    gg = slice(HALF * g, HALF * g + HALF)
                    ready(s_contrib, p)
                    did(dve.tensor_copy(st[gg, 1, :], bank(6)[gg, 0:P]))
                    for c in range(2, TC):
                        for h in range(2):
                            hh = slice(HALF * h, HALF * h + HALF)
                            if h == 0:
                                settle()
                            ins = stt(st[gg, c, hh], st[gg, c - 1, hh], eh[gg, h, c * P - P + P - 1:c * P - P + P],
                                      bank(6)[gg, (c - 1) * P + HALF * h:(c - 1) * P + HALF * h + HALF],
                                      ALU.mult, ALU.add)
                            if c == TC - 1 and h == 1:
                                made(s_state, ins)
                            else:
                                did(ins)

                def ssd_gate(p):
                    ready(y_done, p)
                    if p == 3:
                        ready(ssd_low, 0)
                    did(stt(y2[:, p % 3, :], xs[:, p % 2, :], col(DC + p), bank(7), ALU.mult, ALU.add))
                    settle()
                    made(y_gated, tt(y2[:, p % 3, :], y2[:, p % 3, :], zs[:, p % 2, :], ALU.mult))

                def group_rsqrt(g):
                    ready(group_sum, g)
                    rsqrt(group_norm, rgt[:], bank(GROUP[g])[:, 0:TC], 1.0 / (SSD_W // 2))

                def ssd_norm(p):
                    ready(group_spread, p // 2)
                    made(ssd_y, stt(y2[:, p % 3, :], y2[:, p % 3, :], col(SN + p), bank(7), ALU.mult, ALU.mult))

                def ssd_lo(p):
                    ready(ssd_high, p)
                    made(ssd_low, tt(slo[:, p, :], y2[:, p % 3, :], shi[:, p, :].bitcast(F32), ALU.subtract))

                def hg_norm(p, bk):
                    ready(head_spread, 2 * p + 1)
                    made(head_used, stt(b[:, p, :], b[:, p, :], col(HN), bank(bk), ALU.mult, ALU.mult))
                    ready(head_used, p)

                def hg_gate(p):
                    ready(tanh_used, TANHS.index(("g", p)))
                    made(hg_y, tt(b[:, p, :], b[:, p, :], gs[:, p % 2, :], ALU.mult))

                def hg_lo(p):
                    ready(hg_high, p)
                    if p == 3:
                        ready(group_sum, 1)
                    made(hg_low, tt(olo[p][:], b[:, p, :], ohi[:, p, :].bitcast(F32), ALU.subtract))

                did(dve.memset(xr[:, :, 0:3], 0.0))
                did(dve.memset(dec[:, :, 0:1], 0.0))
                did(dve.memset(ctr[:, :, 0:1], 0.0))
                norm_copy(l, 1)
                settle()
                for n, (kind, pr) in enumerate(PROJ):
                    evac(n)
                    if kind == "f":
                        gate_f(pr)
                    if kind == "dt":
                        dt_first()
                    if kind in ("B", "C"):
                        convolve(kind, n)
                    if kind == "B":
                        conv_out("B")
                    if kind == "C":
                        for p in range(NP):
                            scan_f(p)
                        dt_rest()
                        conv_out("C")
                    if n == Q0:
                        hg_dist(0)
                        hg_q(0)
                    if n == Q0 + 1:
                        hg_k(0)
                        ssd_common()
                        did(dve.memset(sm[:].rearrange("p a h t -> p (a h t)"), 0.0))
                    if n in (9, 11, 13):
                        p = (n - 9) // 2
                        if p == 0:
                            ends()
                        hg_mask(p)
                        hg_dist(p + 1)
                        hg_q(p + 1)
                    if n in (10, 12, 14):
                        p = (n - 10) // 2
                        hg_k(p + 1)
                        if p == 0:
                            end_weights()
                        hg_scan(p)
                    if n == 15:
                        hg_mask(3)
                        ready(proj_out, n)
                        silu(("g", 0), g2[:, 0, :], gs[:, 0, :])
                    if kind == "xs":
                        convolve(pr, n)
                        if pr == 0:
                            hg_scan(3)
                        conv_out(pr)
                        if pr:
                            ssd_states(pr - 1)
                        if pr == 1:
                            ready(head_sum)
                            rsqrt(head_norm, rht[:].rearrange("p c h -> p (c h)"), bank(7)[:, 0:TC * 8], 1.0 / HALF)
                        if pr == 2:
                            hg_norm(0, 3)
                            hg_gate(0)
                            hg_lo(0)
                        if pr == 3:
                            group_rsqrt(0)
                            hg_norm(1, 3)
                    if kind == "z":
                        ready(proj_out, n)
                        silu(("z", pr), g2[:, 0, :], zs[:, pr % 2, :])
                        if pr:
                            ssd_gate(pr - 1)
                        ssd_main(pr)
                    if kind == "g" and pr in (1, 2):
                        ready(proj_out, n)
                        silu(("g", pr), g2[:, 0, :], gs[:, pr % 2, :])
                        if pr == 1:
                            ssd_states(3)
                        hg_gate(pr)
                        if pr == 1:
                            hg_lo(1)
                            hg_norm(2, 3)
                            hg_norm(3, 4)
                            ssd_norm(0)
                            ssd_norm(1)
                        else:
                            ssd_lo(0)
                            ssd_lo(1)
                            hg_lo(2)
                            ssd_gate(3)
                group_rsqrt(1)
                silu(("g", 3), g2[:, 0, :], gs[:, 1, :])
                hg_gate(3)
                ssd_norm(2)
                ssd_norm(3)
                hg_lo(3)
                ssd_lo(2)
                ssd_lo(3)
                for m in range(KD):
                    def mixed(m):
                        ready(blk, OUT0 + m)
                        return stt(x[:, m, :], bank(DOWN + m % 2), 1.0, x[:, m, :], ALU.mult, ALU.add)
                    residual(l, KD + m, col(WN + KD + m), mixed)
                ffn(1, FFN2, 2 * KD, WN + 2 * KD)
                assert own.n == DVE_STEPS, own.n

            own.base, own.n = ahead + DEPTH * DVE_STEPS, 0
            norm(DEPTH, 0)
            norm_copy(DEPTH, 0)
            settle()
            for m in range(KD):
                stt(ont[:, m, :], x[:, m, :], par[:, WN + 2 * KD + m:WN + 2 * KD + m + 1], r[:],
                    ALU.mult, ALU.mult).then_inc(out_made.sem, 1)
            for m in range(KD):
                dve.wait_ge(out_turned.sem, m + 1)
                dve.tensor_copy(stage[:, :, m * P:(m + 1) * P], in_tiles(bank(m))).then_inc(out_tok.sem, 1)

        @block.tensor
        def _(pe):
            mm = pe.matmul
            for _ in range(NS):
                pe.sem_inc(blk.sem, 1)
            pe.wait_ge(consts.sem, 14)
            pe.wait_ge(loaded.sem, 64)
            for m in range(KD):
                pe.wait_ge(x_tile.sem, x_tile.upto(0, m - KD - 2))
                for c in range(TC):
                    last = pe.transpose(bank(DOWN + m % 2)[:, c * P:(c + 1) * P], stage[:, c, m * P:(m + 1) * P],
                                        ident[:])
                last.then_inc(x_turned.sem, 1)

            def products(dst, q, piece, moving, start, stop):
                s = slice(piece * P, piece * P + P)
                mh, ml = moving
                mm(dst, whi[:, q, s], mh, start=start, stop=False)
                mm(dst, whi[:, q, s], ml, start=False, stop=False)
                return mm(dst, wlo[:, q, s], mh, start=False, stop=stop)

            def norm_products(l, ph):
                pe.wait_ge(x_sum.sem, x_sum.upto(l, KD * ph - 1))
                for c in range(TC):
                    last = mm(bank(NORM)[:, c:c + 1], acc[:, c * P:(c + 1) * P], ones[:, 0:1],
                              start=True, stop=True)
                last.then_inc(norm_sum.sem, 1)

            def spread(e, dst, rms):
                for c in range(TC):
                    last = mm(dst[:, c * P:(c + 1) * P], rms(c), ident[:], start=True, stop=True)
                last.then_inc(e.sem, 1)

            def norm_spreads(l, ph):
                pe.wait_ge(norm_rms.sem, norm_rms.upto(l, ph))
                spread(norm_spread, bank(NORM), lambda c: rt[:, c:c + 1].to_broadcast([P, P]))

            def h_tile(k):
                return hhi[:, k, :], hlo[:, k, :]

            with pe.Fori(0, DEPTH) as l:
                def ready(e, k=0):
                    pe.wait_ge(e.sem, e.upto(l, k))

                def h_ready(ph, k):
                    if k in (0, KD - 1):
                        ready(x_low, KD * ph - KD + (KD - 2 if k == 0 else KD - 1))

                def ffn(c, wb):
                    ph = 2 * c

                    def up(i, peeled):
                        for jj in range(2):
                            for kind in range(2):
                                q = 2 * jj + kind
                                free = (g_out, u_out)[kind]
                                pe.wait_ge(free.sem, free.upto(l, NJ * c + jj - 2) + 2 * i)
                                pe.wait_ge(split.sem, split.upto(l, wb + q) + NS * i)
                                for k in range(KD):
                                    if peeled and q == 0:
                                        h_ready(ph, k)
                                    last = products(bank(2 * kind + jj), q, k, h_tile(k), k == 0, k == KD - 1)
                                last.then_inc(blk.sem, 1)
                                if peeled and q == 0:
                                    norm_products(l, ph)
                                if peeled and q == 1:
                                    norm_spreads(l, ph)

                    up(0, True)
                    with pe.Fori(1, NJ // 2) as i:
                        up(i, False)
                    with pe.Fori(0, 2) as i:
                        for mm4 in range(4):
                            pe.wait_ge(x_tile.sem, x_tile.upto(l, KD * ph + mm4 - 2) + 4 * i)
                            for s, (j0, j1) in enumerate(DN_PIECES):
                                w = wb + UP_BLOCKS + 3 * mm4 + s
                                ready(hid_low, NJ * c + j1 - 1)
                                pe.wait_ge(split.sem, split.upto(l, w) + 12 * i)
                                for j in range(j0, j1):
                                    last = products(bank(DOWN + mm4 % 2), w % NS, j - j0,
                                                    (ahi[:, j, :], alo[:, j, :]), j == 0, j == NJ - 1)
                                last.then_inc(blk.sem, 1)

                ffn(0, 0)

                def cols_of(c):
                    return slice(c * P, (c + 1) * P)

                def common():
                    ready(dt_sum)
                    ready(conv_silu_b, TANHS.index(("cv", "B")))
                    for c in range(TC):
                        last = pe.transpose(bank(3)[:, cols_of(c)], bf[:, cols_of(c)], ident[:])
                    last.then_inc(b_turned.sem, 1)
                    for a, src in enumerate((dtb, acb)):
                        for c in range(TC):
                            last = pe.transpose(bank(6)[:, a * 32 + c * 8:a * 32 + c * 8 + 8],
                                                src[:, cols_of(c)], ident[0:8, 0:8])
                    last.then_inc(dt_turned.sem, 1)
                    ready(conv_silu_b, TANHS.index(("cv", "C")))
                    for g in range(2):
                        gg = slice(HALF * g, HALF * g + HALF)
                        for c in range(TC):
                            last = mm(bank(4 + g)[:, cols_of(c)], bf[gg, cols_of(c)], cf[gg, cols_of(c)],
                                      start=True, stop=True)
                        last.then_inc(cb.sem, 1)

                conv_silu_b = tanh_used

                def chunk_ends():
                    ready(dt_tok)
                    mm(bank(7)[:, 0:TC * 8], ident[:, P - 1:P].to_broadcast([P, P]),
                       dts[:, 1].rearrange("p c h -> p (c h)"), start=True, stop=True).then_inc(last_sums.sem, 1)

                def hg_turn(p):
                    ready(hmul, 4 * p + 3)
                    if p == 0:
                        ready(b_tok)
                        ready(cb_masked, 1)
                        ready(dt_tok)
                    else:
                        ready(contrib_out, 4 * p - 1)
                    for c in range(TC):
                        last = pe.transpose(bank(3)[:, cols_of(c)], e4[:, cols_of(c)], ident[:])
                    last.then_inc(turned.sem, 1)
                    ready(proj_out, AT["i", p])
                    for c in range(TC):
                        last = pe.transpose(bank(4)[:, cols_of(c)], vf[:, cols_of(c)], ident[:])
                    last.then_inc(turned.sem, 1)
                    ready(hmul, 4 * p + 2)
                    for h in range(2):
                        hh = slice(HALF * h, HALF * h + HALF)
                        for c in range(TC):
                            last = mm(bank(5 + h)[:, cols_of(c)], e2[hh, cols_of(c)], e1[hh, cols_of(c)],
                                      start=True, stop=True)
                        last.then_inc(score.sem, 1)

                def hg_contribs(p):
                    ready(kd_tok, p)
                    ready(v_tok, 3 * p + 2)
                    ready(score_masked, 2 * p + 1)
                    for rr in range(4):
                        rows = slice(32 * rr, 32 * rr + 32)
                        for c in range(TC):
                            for h in range(2):
                                hh = slice(HALF * h, HALF * h + HALF)
                                last = mm(bank(3 + rr)[hh, cols_of(c)], kdt[rows, c, hh], vm[rows, c, :, hh],
                                          start=True, stop=True)
                        last.then_inc(contrib.sem, 1)

                def hg_outs(p):
                    ready(state, p)
                    ready(hmul, 4 * p + 1)
                    if p:
                        ready(o_out, 2 * p - 1)
                    else:
                        ready(to_end)
                    for h in range(2):
                        hh = slice(HALF * h, HALF * h + HALF)
                        for c in range(TC):
                            mm(bank(7)[hh, cols_of(c)], vt[:, p % 2, c, hh], sm[:, p % 2, h, cols_of(c)],
                               start=c == 0, stop=False, skip_group_check=True)
                        for cc in range(NCC):
                            t = slice(cc * CH, cc * CH + CH)
                            last = mm(bank(7)[hh, t], ctr[hh, :, cc], e3[hh, p % 2, t],
                                      start=False, stop=cc == NCC - 1, skip_group_check=True)
                    last.then_inc(o_done.sem, 1)

                def ssd_turn(p):
                    ready(tanh_used, TANHS.index(("cv", p)))
                    ready(dt_tok)
                    if p == 0:
                        ready(contrib_out, 4 * NP - 1)
                    elif p in (2, 3):
                        ready(head_used, p - 2)
                    if p:
                        ready(xde_made, p - 1)
                        ready(seg, 2 * p - 1)
                    for c in range(TC):
                        last = pe.transpose(bank(3)[:, cols_of(c)], xs[:, p % 2, cols_of(c)], ident[:])
                    last.then_inc(x_tok.sem, 1)
                    for h in range(2):
                        k = 2 * p + h
                        mm(bank(4 + h), ident[0:8, k:k + 1].to_broadcast([8, P]), acb[:], start=True, stop=True)\
                            .then_inc(sums.sem, 1)

                def ssd_contribs(p):
                    gg = slice(HALF * (p // 2), HALF * (p // 2) + HALF)
                    ready(xde_made, p)
                    if p:
                        ready(s_state, p - 1)
                    for c in range(TC - 1):
                        last = mm(bank(6)[gg, cols_of(c)], bt[:, c, gg], xde[:, c, :], start=True, stop=True)
                    last.then_inc(s_contrib.sem, 1)

                def ssd_outs(p):
                    gg = slice(HALF * (p // 2), HALF * (p // 2) + HALF)
                    ready(s_state, p)
                    ready(lm_made, 2 * p + 1)
                    if p == 0:
                        ready(head_norm)
                    elif p == 1:
                        ready(y_gated, 0)
                    elif p == 2:
                        ready(group_norm, 0)
                    else:
                        ready(ssd_y, 1)
                    for h in range(2):
                        hh = slice(HALF * h, HALF * h + HALF)
                        for c in range(TC):
                            mm(bank(7)[hh, cols_of(c)], xdt[:, c, hh], lm[:, h, cols_of(c)],
                               start=c == 0, stop=False, skip_group_check=True)
                        for c in range(1, TC):
                            last = mm(bank(7)[hh, cols_of(c)], st[gg, c, hh], cx[gg, h, cols_of(c)],
                                      start=False, stop=c == TC - 1, skip_group_check=True)
                    last.then_inc(y_done.sem, 1)

                def head_sums():
                    ready(o_out, 2 * NP - 1)
                    for c in range(TC):
                        for p in range(NP):
                            last = mm(bank(7)[:, 8 * c:8 * c + 8], km[:, p, cols_of(c)], headsum[:, 8 * p:8 * p + 8],
                                      start=p == 0, stop=p == NP - 1)
                    last.then_inc(head_sum.sem, 1)

                def head_spreads(p, bk):
                    ready(head_norm)
                    ready(xde_made, min(p + 1, 3))
                    ready(xdt_made, min(p + 1, 3))
                    ready(seg, 2 * min(p + 1, 3) + 1)
                    for h in range(2):
                        spread(head_spread, bank(bk)[HALF * h:HALF * h + HALF, :],
                               lambda c: rht[:, c, 2 * p + h:2 * p + h + 1].to_broadcast([P, HALF]))

                def group_sums(g):
                    ready(y_sq, 2 * g + 1)
                    for c in range(TC):
                        dst = bank(GROUP[g])[:, c:c + 1]
                        mm(dst, sq[:, cols_of(c)], ones[:, 0:1], start=True, stop=False)
                        last = mm(dst, sqb[:, cols_of(c)], ones[:, 0:1], start=False, stop=True)
                    last.then_inc(group_sum.sem, 1)

                def group_spreads(g):
                    ready(group_norm, g)
                    ready(y_gated, 2 + g)
                    spread(group_spread, bank(7), lambda c: rgt[:, c:c + 1].to_broadcast([P, P]))

                for i, (n, k0, k1) in enumerate(PBLOCKS):
                    w = MIX0 + i
                    ready(split, w)
                    if k0 == 0:
                        ready(proj_out, n - 3)
                    for k in range(k0, k1):
                        if n == 0:
                            h_ready(1, k)
                        last = products(bank(n % 3), w % NS, k - k0, h_tile(k), k == 0, k == KD - 1)
                    last.then_inc(blk.sem, 1)
                    if k1 < KD:
                        continue
                    if n == 0:
                        norm_products(l, 1)
                    if n == 1:
                        norm_spreads(l, 1)
                    if n == 8:
                        common()
                    if n == 9:
                        chunk_ends()
                    if n in (9, 11, 13, 15):
                        hg_turn((n - 9) // 2)
                    if n in (10, 12, 14, 16):
                        hg_contribs((n - 10) // 2)
                    if n in (11, 13, 15, 17):
                        hg_outs((n - 11) // 2)
                    if n in (19, 21, 23, 25):
                        ssd_outs((n - 19) // 2)
                    if n in (17, 19, 21, 23):
                        ssd_turn((n - 17) // 2)
                    if n in (18, 20, 22, 24):
                        ssd_contribs((n - 18) // 2)
                    if n == 18:
                        head_sums()
                    if n == 20:
                        head_spreads(0, 3)
                    if n == 22:
                        group_sums(0)
                        head_spreads(1, 3)
                    if n == 24:
                        head_spreads(2, 3)
                        head_spreads(3, 4)
                        group_spreads(0)

                SOON, LATE = (0, 1, 4, 5, 6), (7, 2, 3)

                def out_products(m, ks):
                    w = OUT0 + m
                    for k in ks:
                        if m == 0:
                            if k < NP:
                                ready(ssd_low, k)
                            else:
                                ready(hg_low, k - NP)
                        moving = ((shi[:, k, :], slo[:, k, :]) if k < NP
                                  else (ohi[:, k - NP, :], olo[k - NP][:]))
                        last = products(bank(DOWN + m % 2), w % NS, k, moving, k == SOON[0], k == LATE[-1])
                    return last

                group_sums(1)
                ready(head_used, 3)
                for m in (0, 1):
                    ready(split, OUT0 + m)
                    ready(x_tile, KD + m - 2)
                    out_products(m, SOON)
                    if m == 0:
                        group_spreads(1)
                for m in (0, 1):
                    out_products(m, LATE).then_inc(blk.sem, 1)
                for m in range(2, KD):
                    ready(split, OUT0 + m)
                    ready(x_tile, KD + m - 2)
                    out_products(m, SOON)
                    out_products(m, LATE).then_inc(blk.sem, 1)
                ffn(1, FFN2)

            norm_products(DEPTH, 0)
            norm_spreads(DEPTH, 0)
            for m in range(KD):
                pe.wait_ge(out_made.sem, m + 1)
                for c in range(TC):
                    last = pe.transpose(bank(m)[:, c * P:(c + 1) * P], ont[:, m, c * P:(c + 1) * P], ident[:])
                last.then_inc(out_turned.sem, 1)


def kernel(**inputs):
    import concourse.bacc as bacc
    from concourse.bass_utils import run_bass_kernel_spmd

    a = {k: np.asarray(v) for k, v in inputs.items()}

    def tile_cols(v):
        return np.moveaxis(v.reshape(*v.shape[:-1], -1, P), -1, -2)

    def k_major(w, j0, n):
        w = w[:, :, j0:j0 + n]
        return w.reshape(w.shape[0], -1, P, n).transpose(0, 2, 1, 3)

    def col_tiles(w):
        d, k, n = w.shape
        return w.reshape(d, k // P, P, n // P, P).transpose(0, 3, 2, 1, 4).reshape(d, n // P, P, k)

    def up(gate, up_):
        t = np.stack([col_tiles(gate), col_tiles(up_)], axis=2)
        return np.ascontiguousarray(t.reshape(DEPTH, UP_BLOCKS, P, BW))

    def rows8(v):
        out = np.zeros((DEPTH, P, 1), np.float32)
        out[:, :8, 0] = v
        return out

    following = np.concatenate([a["ffn1_norm"][1:], a["final_norm"][None]])
    cols = np.concatenate([
        tile_cols(a["mix_norm"]), tile_cols(a["ffn2_norm"]), tile_cols(following),
        a["ssd_conv_w"].reshape(DEPTH, 4, 6, P).transpose(0, 3, 2, 1).reshape(DEPTH, P, 24),
        tile_cols(a["ssd_conv_b"]), tile_cols(a["ssd_norm_w"]),
        tile_cols(np.repeat(a["ssd_d"], HALF, axis=1)),
        np.tile(a["hg_norm_w"], (1, 2))[:, :, None],
        rows8(a["ssd_dt_bias"]), rows8(a["ssd_a_log"]),
    ], axis=2)
    w_in = a["w_in"]
    starts, at = {}, 0
    for name, width in (("z", 512), ("xs", 512), ("B", 128), ("C", 128), ("dt", 8), ("q", 512), ("f", 512),
                        ("i", 512), ("g", 512)):
        starts[name], at = at, at + width
    blocks = [k_major(w_in, starts[kind] + P * p, P).reshape(DEPTH, P, BW) for kind, p in PROJ if kind != "dt"]
    mix = np.concatenate([np.stack(blocks, axis=1), col_tiles(a["w_out"])], axis=1)
    arrays = {
        "x": a["x"], "cols": np.ascontiguousarray(cols.transpose(1, 0, 2)),
        "first_norm": np.ascontiguousarray(tile_cols(a["ffn1_norm"][0])),
        "logits": np.ascontiguousarray(tile_cols(a["hg_lb_logits"]).transpose(1, 0, 2)),
        "up1": up(a["ffn1_w_gate"], a["ffn1_w_up"]), "dn1": np.ascontiguousarray(col_tiles(a["ffn1_w_down"])),
        "mix": np.ascontiguousarray(mix), "dtw": np.ascontiguousarray(k_major(w_in, starts["dt"], 8)),
        "up2": up(a["ffn2_w_gate"], a["ffn2_w_up"]), "dn2": np.ascontiguousarray(col_tiles(a["ffn2_w_down"])),
    }
    nc = bacc.Bacc("TRN2", target_bir_lowering=False, num_devices=1)
    aps = [nc.dram_tensor(f"in_{k}", v.shape, mybir.dt.from_np(v.dtype), kind="ExternalInput").ap()
           for k, v in arrays.items()]
    out = nc.dram_tensor("out_0", a["x"].shape, F32, kind="ExternalOutput").ap()
    trunk_kernel(nc, *aps, out)
    r = run_bass_kernel_spmd(nc, [{f"in_{k}": v for k, v in arrays.items()}], core_ids=[0])
    return r.results[0]["out_0"]
```

```python
import numpy as np
import concourse.bass as bass
from concourse import mybir
from concourse.alu_op_type import AluOpType as ALU
from contextlib import ExitStack

F32 = mybir.dt.float32
F32R = mybir.dt.float32r
I32 = mybir.dt.int32
ACT = mybir.ActivationFunctionType
AX = mybir.AxisListType

P = 128
DEPTH = 2
T = 512
TC = T // P
D = 1024
KD = D // P
FF = 2816
NJ = FF // P
SSD_W = 512
GN = 128
NP = 4
HALF = 64
CH = 16
CT = P // CH
CREF = CH // 2 - 1
EPS = 1e-6
BIG = 8e37
MAGIC = float(0x5F3759DF)

NS = 4
BW = KD * P
UP_BLOCKS = 2 * NJ
DN_PIECES = [(0, 8), (8, 15), (15, 22)]
DN_BLOCKS = KD * len(DN_PIECES)
PROJ = ([("f", 0), ("f", 1), ("B", 0), ("f", 2), ("dt", 0), ("f", 3), ("C", 0)]
        + [(k, p) for p in range(NP) for k in ("q", "i")]
        + [("g", 0)]
        + [(k, p) for p in range(NP) for k in ("xs", "z")]
        + [("g", 1), ("g", 2), ("g", 3)])
Q0, X0 = 7, 16
NPROJ = len(PROJ)
AT = {kp: n for n, kp in enumerate(PROJ)}
PBLOCKS = []
for _n, (_kind, _) in enumerate(PROJ):
    PBLOCKS += [(_n, 0, 4), (_n, 4, 8)] if _kind == "B" else [(_n, 0, 8)]
MIX0 = UP_BLOCKS + DN_BLOCKS
OUT0 = MIX0 + len(PBLOCKS)
FFN2 = OUT0 + KD
W = FFN2 + UP_BLOCKS + DN_BLOCKS
assert W % NS == 0 and MIX0 % NS == 0 and FFN2 % NS == 0
LAST_BLOCK = {n: MIX0 + i for i, (n, _, _) in enumerate(PBLOCKS)}

WN = 0
CW = WN + 3 * KD
CB = CW + 6 * 4
SN = CB + 6
DC = SN + NP
HN = DC + NP
DTB = HN + 1
ALOG = DTB + 1
NIN = ALOG + 1
LB = NIN
OLB = LB + NP
NEGA = OLB + NP
NCOL = NEGA + 1
CONV_B, CONV_C = 4, 5

LEADS = (0, 1, 3, 4)

OUT_PIECES = [(half, c) for half in range(2) for c in range(TC)]
OUT_BANKS = (0, 1, 2, 3, 4, 5, 7, 6)

SCORES_AT = ((), (), (0,), (1,), (2,), (3,), (4, 5), (6, 7))

TANHS = ([("cv", "B"), ("cv", "C")] + [("q", p) for p in range(NP)] + [("g", 0)]
         + [x for p in range(NP) for x in (("cv", p), ("z", p))] + [("g", 1), ("g", 2), ("g", 3)])
DVE_STEPS = 177
CONVS = ["B", "C", 0, 1, 2, 3]


class Event:

    def __init__(self, sem, per=0, before=0, credit=0):
        self.sem, self.per, self.first = sem, per, before + credit + 1

    def upto(self, l, k):
        return l * self.per + (k + self.first)


class Steps:

    def __init__(self, eng, sem):
        self.eng, self.sem, self.base, self.n = eng, sem, 0, 0

    def did(self, ins):
        ins.then_inc(self.sem, 1)
        self.n += 1

    def settle(self):
        self.eng.wait_ge(self.sem, self.base + self.n)


def trunk_kernel(nc, x_in, cols, first_norm, logits, lead, up1, dn1, mix, dtw, up2, dn2, out):
    ctx = ExitStack()
    with ctx:
        def sb(name, shape, dt=F32, at=ctx):
            return at.enter_context(nc.sbuf_tensor(name, shape, dt))

        def ev(name, per=0, before=0, credit=0):
            return Event(ctx.enter_context(nc.semaphore(name)), per, before, credit)

        x = sb("x", [P, KD, T])
        hhi = sb("hhi", [P, KD, T], F32R)
        hlo = sb("hlo", [P, KD, T], F32R)
        raw = sb("raw", [P, NS, BW])
        whi = sb("whi", [P, NS, BW], F32R)
        wlo = sb("wlo", [P, NS, BW], F32R)
        r = sb("r", [P, T])
        acb_lo = sb("acb_lo", [8, T], F32R)
        acc = sb("acc", [P, T])
        sq = sb("sq", [P, T])
        g2 = sb("g2", [P, 2, T])
        u2 = sb("u2", [P, 2, T])
        par = sb("par", [P, NCOL])
        par_all = sb("par_all", [P, DEPTH, NCOL])
        first = sb("first", [P, KD])
        lg = sb("lg", [P, DEPTH, NP])
        lt = sb("lt", [P, 3, NP])
        spare = sb("spare", [1, 1])
        ident = sb("ident", [P, P])
        identr = sb("identr", [P, P], F32R)
        ones = sb("ones", [P, P])
        causal = sb("causal", [P, P])
        keep16 = sb("keep16", [P, T])
        rt = sb("rt", [P, TC])
        rh = sb("rh", [P, TC * 8])
        rg = sb("rg", [P, TC])
        rt2 = sb("rt2", [P, 2, TC], F32R)
        rg2 = sb("rg2", [P, 2, TC], F32R)
        ntn = sb("ntn", [P, 2, TC * 8])
        headsum = sb("headsum", [P, NP * 8])

        REGION = 27 * 1024 + 256 + 62 * 1024
        arena = sb("arena", [P, REGION // 4])
        base = nc.sbuf_base - REGION

        def place(name, shape, kib, dt=F32, start=0):
            assert start + kib * 1024 + 4 * int(np.prod(shape[1:])) <= REGION, name
            return nc.alloc_sbuf_tensor_at(name, shape, dt, offset=base + start + int(kib * 1024))

        ahi = place("ahi", [P, NJ, T], 0, F32R)
        alo = place("alo", [P, NJ, T], 44, F32R)
        stage = place("stage", [P, TC, D], 0)
        b = place("b", [P, NP, T], 0)
        cf = place("cf", [P, T], 8)
        bt = place("bt", [P, TC, P], 10)
        cbm = place("cbm", [P, 2, TC, P], 12)
        acb = place("acb", [8, T], 16)
        dts = place("dts", [P, 2, TC, 8], 18)
        wend = place("wend", [P, TC, 8], 18.5)
        xr = place("xr", [P, T + 3], 19)
        acb_hi = place("acb_hi", [8, T], 21.125, F32R)
        th = place("th", [P, 2, T], 23.25)
        S0 = 27 * 1024 + 256

        def put(name, shape, kib, dt=F32):
            return place(name, shape, kib, dt, S0)

        bf = put("bf", [P, T], 0)
        dtb = put("dtb", [8, T], 2)
        km = put("km", [P, NP, T], 4)
        e1 = [put(f"e1_{i}", [P, T], kib) for i, kib in enumerate((12, 50))]
        e2 = [put(f"e2_{i}", [P, T], kib) for i, kib in enumerate((14, 52))]
        e4 = [put(f"e4_{i}", [P, T], kib) for i, kib in enumerate((16, 54))]
        t1 = put("t1", [P, T], 18)
        vf = put("vf", [P, T], 18)
        kdt = put("kdt", [P, TC, P], 20)
        w1 = [put(f"w1_{i}", [P, T], kib) for i, kib in enumerate((22, 56))]
        w2 = [put(f"w2_{i}", [P, T], kib) for i, kib in enumerate((24, 58))]
        vt = put("vt", [P, 2, TC, P], 26)
        qs = put("qs", [P, 2, T], 30)
        sm = put("sm", [P, 2, 2, T], 34)
        e3 = [put(f"e3_{i}", [P, T], kib) for i, kib in enumerate((42, 60))]
        ks = put("ks", [P, T], 44)
        hs = put("hs", [P, TC - 1, HALF], 46)
        dch, to_q, to_k, f1, f2 = (put(name, [P, NP * TC, CT], 47 + 0.5 * i)
                                   for i, name in enumerate(("dch", "to_q", "to_k", "f1", "f2")))
        dtile = put("dtile", [P, NP * TC], 49.5)
        xdt = put("xdt", [P, TC, P], 0)
        xde = put("xde", [P, TC, P], 2)
        gs = put("gs", [P, 2, T], 12)
        xs = put("xs", [P, 2, T], 16)
        zs = put("zs", [P, 2, T], 20)
        lm = put("lm", [P, 2, T], 24)
        cx = put("cx", [P, 2, T], 28)
        st = put("st", [P, TC, P], 32)
        y2 = put("y2", [P, 3, T], 34)
        sqb = put("sqb", [P, T], 58)
        shi = put("shi", [P, NP, T], 42, F32R)
        slo = put("slo", [P, NP, T], 50, F32R)
        ohi = put("ohi", [P, NP, T], 4, F32R)
        olo = [put(f"olo{p}", [P, T], kib, F32R) for p, kib in enumerate((40, 2, 60, 58))]
        eh = u2

        ps = ctx.enter_context(nc.psum_tensor("ps", [P, 8, T], F32))

        def bank(i):
            return ps[:, i, :]

        def in_tiles(ap):
            return ap.rearrange("p (c t) -> p c t", c=TC)

        DOWN, NORM = 4, 6
        GROUP0 = (TC - 1) * P

        loaded = ev("loaded")
        x_part = [ev(f"x_part{i}") for i in range(4)]
        stored = ev("stored")
        consts = ev("consts")
        full = [ev(f"raw_full{s}") for s in range(NS)]
        high = ev("high", W)
        split = ev("split", W)
        blk = ev("blk", W)
        par_set = ev("par_set", 1)
        lg_max = ev("lg_max")
        lg_exp = ev("lg_exp")
        x_turned = ev("x_turned")
        x_tile = ev("x_tile", 3 * KD, KD, 2)
        x_high = ev("x_high", 3 * KD, KD)
        x_low = ev("x_low", 3 * KD, KD)
        x_sq = ev("x_sq", 3 * KD, KD)
        x_sum = ev("x_sum", 3 * KD, KD)
        norm_sum = ev("norm_sum", 3)
        norm_rms = ev("norm_rms", 3)
        norm_spread = ev("norm_spread", 3)
        g_out = ev("g_out", 2 * NJ, credit=2)
        u_out = ev("u_out", 2 * NJ, credit=2)
        silu_g = ev("silu_g", 2 * NJ)
        hid = ev("hid", 2 * NJ)
        hid_high = ev("hid_high", 2 * NJ)
        hid_low = ev("hid_low", 2 * NJ)
        dve_step = ctx.enter_context(nc.semaphore("dve_step"))
        proj_out = ev("proj_out", NPROJ, credit=3)
        tanh = ev("tanh", len(TANHS))
        tanh_used = ev("tanh_used", len(TANHS), credit=2)
        f_exp = ev("f_exp", NP)
        f_gate = ev("f_gate", NP)
        f_log = ev("f_log", NP)
        f_sum = ev("f_sum", NP)
        dt_abs = ev("dt_abs", 1)
        dt_exp = ev("dt_exp", 1)
        dt_log = ev("dt_log", 1)
        dt_sum = ev("dt_sum", 1)
        acb_split = ev("acb_split", 1)
        conv = ev("conv", 6)
        conv_silu = ev("conv_silu", 6)
        b_turned = ev("b_turned", 1)
        b_tok = ev("b_tok", 1)
        cb = ev("cb", 2)
        cb_masked = ev("cb_masked", 2)
        dt_turned = ev("dt_turned", 1)
        dt_tok = ev("dt_tok", 1)
        dist = ev("dist", 2 * NP)
        hexp = ev("hexp", 4 * NP)
        hmul = ev("hmul", 4 * NP)
        turned = ev("turned", 2 * NP)
        score = ev("score", 2 * NP)
        score_masked = ev("score_masked", 2 * NP)
        kd_tok = ev("kd_tok", NP)
        v_tok = ev("v_tok", NP)
        contrib = ev("contrib", NP)
        decay = ev("decay", 1)
        level = ev("level", 6 * NP)
        cleared = ev("cleared", 1)
        state = ev("state", NP)
        o_done = ev("o_done", NP)
        o_out = ev("o_out", 2 * NP)
        head_sum = ev("head_sum", 1)
        head_norm = ev("head_norm", 1)
        head_spread = ev("head_spread", NP)
        head_used = ev("head_used", NP)
        hg_y = ev("hg_y", NP)
        hg_high = ev("hg_high", NP)
        hg_low = ev("hg_low", NP)
        x_tok = ev("x_tok", NP)
        sums = ev("sums", 2 * NP)
        sums_exp = ev("sums_exp", 2 * NP)
        last_sums = ev("last_sums", 1)
        to_end = ev("to_end", 1)
        to_end_exp = ev("to_end_exp", 1)
        seg = ev("seg", 2 * NP * TC)
        seg_exp = ev("seg_exp", 2 * NP)
        xdt_made = ev("xdt_made", NP)
        xde_made = ev("xde_made", NP)
        lm_made = ev("lm_made", 2 * NP)
        cx_made = ev("cx_made", 2 * NP)
        s_contrib = ev("s_contrib", NP)
        s_state = ev("s_state", NP)
        y_done = ev("y_done", NP)
        y_gated = ev("y_gated", NP)
        y_sq = ev("y_sq", NP)
        group_sum = ev("group_sum", 2)
        group_norm = ev("group_norm", 2)
        group_spread = ev("group_spread", 2)
        ssd_y = ev("ssd_y", NP)
        ssd_high = ev("ssd_high", NP)
        ssd_low = ev("ssd_low", NP)
        out_turned = ev("out_turned")
        out_act = ev("out_act")
        out_dve = ev("out_dve")

        block = ctx.enter_context(nc.Block())

        @block.sync
        def _(sp):
            sp.dma_start(par_all[:, :, 0:NIN], cols).then_inc(loaded.sem, 16)
            sp.dma_start(first[:], first_norm).then_inc(loaded.sem, 16)
            sp.dma_start(lg[:], logits).then_inc(loaded.sem, 16)
            for i in range(4):
                part = slice(i * D // 4, (i + 1) * D // 4)
                sp.dma_start(stage[:, :, part], x_in.rearrange("b (c p) d -> p (b c) d", p=P)[:, :, part])\
                    .then_inc(x_part[i].sem, 16)
                sp.dma_start(raw[:, i, :], lead[0, i]).then_inc(full[i].sem, 16)
            with sp.Fori(0, DEPTH) as l:
                def load(w, q, dst, src):
                    sp.wait_ge(split.sem, split.upto(l, w - NS))
                    sp.dma_start(dst, src).then_inc(full[q].sem, 16)

                def ffn(wb, up, dn, i0):
                    with sp.Fori(0, UP_BLOCKS // NS - i0) as i:
                        for q in range(NS):
                            load(wb + NS * i0 + NS * i + q, q, raw[:, q, :], up[l, NS * i + q])
                    for m in range(KD):
                        for s, (j0, j1) in enumerate(DN_PIECES):
                            w = wb + UP_BLOCKS + 3 * m + s
                            load(w, w % NS, raw[:, w % NS, 0:(j1 - j0) * P], dn[l, m, :, j0 * P:j1 * P])

                ffn(0, up1, dn1, 1)
                for i, (n, k0, k1) in enumerate(PBLOCKS):
                    w = MIX0 + i
                    if PROJ[n][0] == "dt":
                        load(w, w % NS, raw[:, w % NS, :].rearrange("p (k m) -> p k m", k=KD)[:, :, 0:8],
                             dtw[l])
                    else:
                        load(w, w % NS, raw[:, w % NS, 0:(k1 - k0) * P],
                             mix[l, n - (n > AT["dt", 0]), :, k0 * P:k1 * P])
                for m in range(KD):
                    w = OUT0 + m
                    load(w, w % NS, raw[:, w % NS, :], mix[l, NPROJ - 1 + m])
                ffn(FFN2, up2, dn2, 0)
                for q in range(NS):
                    load(W + q, q, raw[:, q, :], lead[l + 1, q])
            for i, (half, c) in enumerate(OUT_PIECES):
                made = out_dve if i % 2 else out_act
                sp.wait_ge(made.sem, i // 2 + 1)
                piece = slice(half * T, half * T + T)
                sp.dma_start(out.rearrange("b (c p) d -> p (b c) d", p=P)[:, c, piece], stage[:, c, piece])\
                    .then_inc(stored.sem, 16)
            sp.wait_ge(stored.sem, 16 * len(OUT_PIECES))

        @block.gpsimd
        def _(pool):
            def made(ins, n):
                ins.then_inc(consts.sem, 1)
                pool.wait_ge(consts.sem, n)

            made(pool.memset(ident[:], 0.0), 1)
            made(pool.affine_select(out=ident[:], in_=ident[:], compare_op=ALU.not_equal, fill=1.0, base=0,
                                    pattern=[[-1, P]], channel_multiplier=1), 2)
            made(pool.memset(ones[:], 1.0), 3)
            made(pool.memset(causal[:], 1.0), 4)
            made(pool.affine_select(out=causal[:], in_=causal[:], compare_op=ALU.is_ge, fill=0.0, base=0,
                                    pattern=[[1, P]], channel_multiplier=-1), 5)
            made(pool.memset(keep16[:], 1.0), 6)
            made(pool.memset(keep16[:, 0:T:CH], 0.0), 7)
            made(pool.memset(headsum[:], 0.0), 8)
            made(pool.memset(headsum[0:HALF, 0:31:10], 1.0), 9)
            made(pool.memset(headsum[HALF:P, 1:32:10], 1.0), 10)
            with pool.Fori(0, DEPTH * W // NS + 1) as i:
                for q in range(NS):
                    pool.wait_ge(high.sem, NS * i + (q + 1))
                    pool.tensor_tensor(wlo[:, q, :], raw[:, q, :], whi[:, q, :].bitcast(F32),
                                       ALU.subtract).then_inc(split.sem, 1)

        @block.scalar
        def _(act):
            act.wait_ge(lg_max.sem, 1)
            act.activation(lg[:], lg[:], ACT.Exp).then_inc(lg_exp.sem, 1)
            act.activation(par_all[:, :, NEGA:NEGA + 1], par_all[:, :, ALOG:ALOG + 1], ACT.Exp)\
               .then_inc(lg_exp.sem, 1)

            def residual(l, k, gain):
                m = k % KD
                act.wait_ge(x_tile.sem, x_tile.upto(l, k))
                act.activation(hhi[:, m, :], x[:, m, :], ACT.Copy, scale=gain).then_inc(x_high.sem, 1)
                if not (isinstance(l, int) and l == 0 and k == -KD):
                    act.wait_ge(x_sum.sem, x_sum.upto(l, k - 1))
                act.activation(sq[:], x[:, m, :], ACT.Square).then_inc(x_sq.sem, 1)

            for m in range(KD):
                residual(0, m - KD, first[:, m:m + 1])
                if m in LEADS:
                    q = LEADS.index(m)
                    act.wait_ge(full[q].sem, 16)
                    act.activation(whi[:, q, :], raw[:, q, :], ACT.Copy).then_inc(high.sem, 1)

            with act.Fori(0, DEPTH) as l:
                def hi(w, q=None):
                    q = w % NS if q is None else q
                    act.wait_ge(full[q].sem, 16 * ((w - q) // NS + l * (W // NS)) + 16)
                    act.wait_ge(blk.sem, blk.upto(l, w - NS))
                    act.activation(whi[:, q, :], raw[:, q, :], ACT.Copy).then_inc(high.sem, 1)

                def hi_i(wb, i, q):
                    act.wait_ge(full[q].sem, 16 * (wb // NS + 1) + 16 * i + l * (16 * W // NS))
                    act.wait_ge(blk.sem, blk.upto(l, wb + q - NS) + NS * i)
                    act.activation(whi[:, q, :], raw[:, q, :], ACT.Copy).then_inc(high.sem, 1)

                def ffn(c, wb, k0, gain0):
                    def hidden(i, first):
                        for jj in range(2):
                            k = NJ * c + jj
                            if first:
                                hi_i(wb + NS, i, 2 * jj)
                            act.wait_ge(g_out.sem, g_out.upto(l, k) + 2 * i)
                            act.activation(g2[:, jj, :], g2[:, jj, :], ACT.Silu).then_inc(silu_g.sem, 1)
                            if not first:
                                hi_i(wb + NS, i, 2 * jj)
                            act.wait_ge(hid.sem, hid.upto(l, k) + 2 * i)
                            act.activation(ahi[:, 2 * i + jj, :], u2[:, jj, :], ACT.Copy).then_inc(hid_high.sem, 1)
                            hi_i(wb + NS, i, 2 * jj + 1)

                    hidden(0, True)
                    with act.Fori(1, NJ // 2) as i:
                        hidden(i, False)
                    for m in range(KD):
                        w = wb + UP_BLOCKS + 3 * m
                        hi(w + NS)
                        hi(w + 1 + NS)
                        residual(l, k0 + m, par[:, gain0 + m:gain0 + m + 1])
                        hi(w + 2 + NS)

                act.wait_ge(par_set.sem, par_set.upto(l, 0))
                ffn(0, 0, 0, WN)

                def ready(e, k=0):
                    act.wait_ge(e.sem, e.upto(l, k))

                def do(e, out, in_, f, **kw):
                    act.activation(out, in_, f, **kw).then_inc(e.sem, 1)

                def do_tanh(kind, src):
                    i = TANHS.index(kind)
                    ready(tanh_used, i - 2)
                    do(tanh, th[:, i % 2, :], src, ACT.Tanh)

                def conv_src(t):
                    return {"B": bf[:], "C": cf[:]}[t] if isinstance(t, str) else xs[:, t % 2, :]

                def conv_tanh(t):
                    ready(conv, CONVS.index(t))
                    do_tanh(("cv", t), conv_src(t))

                def plain_tanh(kind, p):
                    ready(proj_out, AT[kind, p])
                    do_tanh((kind, p), g2[:, 0, :])

                def hg_exps(p):
                    ready(dist, 2 * p)
                    do(hexp, e2[p % 2][:], e1[p % 2][:], ACT.Exp, scale=-1.0)
                    do(hexp, e1[p % 2][:], e1[p % 2][:], ACT.Exp)
                    do(hexp, e3[p % 2][:], b[:, p, :], ACT.Exp)
                    ready(dist, 2 * p + 1)
                    do(hexp, e4[p % 2][:], e4[p % 2][:], ACT.Exp)

                def hg_copies(p):
                    ready(turned, 2 * p)
                    do(kd_tok, kdt[:, 0:TC - 1, :].rearrange("p c n -> p (c n)"), bank(3)[:, 0:T - P], ACT.Copy)
                    ready(turned, 2 * p + 1)
                    if p >= 2:
                        ready(o_done, p - 2)
                    do(v_tok, vt[:, p % 2, :, :].rearrange("p c n -> p (c n)"), bank(4), ACT.Copy)

                def hg_out(p):
                    ready(o_done, p)
                    do(o_out, km[:, p, :], bank(7), ACT.Square)
                    do(o_out, b[:, p, :], bank(7), ACT.Copy)

                def ssd_sq(p):
                    ready(y_gated, p)
                    if p == 2:
                        ready(group_sum, 0)
                    do(y_sq, sqb[:] if p % 2 else sq[:], y2[:, p % 3, :], ACT.Square)

                def ssd_exps(p):
                    for h in range(2):
                        k = 2 * p + h
                        ready(sums, k)
                        if p >= 1:
                            ready(s_state, p - 1)
                        do(sums_exp, eh[:, h, :], bank(4 + h), ACT.Exp)
                    if p:
                        ready(y_done, p - 1)
                    for h in range(2):
                        k = 2 * p + h
                        for c in range(TC):
                            do(seg, lm[:, h, c * P:(c + 1) * P], in_tiles(bank(4 + h))[:, c, :], ACT.Relu,
                               scale=-1.0, bias=dts[:, 1, c, k:k + 1])
                    for h in range(2):
                        k = 2 * p + h
                        ready(seg, TC * k + TC - 1)
                        do(seg_exp, lm[:, h, :], lm[:, h, :], ACT.Exp, scale=-1.0)
                    if p:
                        ssd_sq(p - 1)

                def ssd_hi(p):
                    ready(ssd_y, p)
                    do(ssd_high, shi[:, p, :], y2[:, p % 3, :], ACT.Copy)

                def hg_hi(p):
                    ready(hg_y, p)
                    do(hg_high, ohi[:, p, :], b[:, p, :], ACT.Copy)

                for n, (kind, pr) in enumerate(PROJ):
                    for i, (nn, _, _) in enumerate(PBLOCKS):
                        if nn == n:
                            hi(MIX0 + i + NS)
                    if kind == "f":
                        ready(proj_out, n)
                        do(f_exp, km[:, pr, :], g2[:, pr % 2, :], ACT.Exp, scale=-1.0)
                    if n == 2:
                        do(cleared, sm[:].rearrange("p a h t -> p (a h t)"),
                           keep16[:, 0:1].to_broadcast([P, 4 * T]), ACT.Copy)
                    if n == 5:
                        ready(dt_abs)
                        do(dt_exp, acb[:], acb[:], ACT.Exp)
                    if kind == "B":
                        conv_tanh("B")
                    if kind == "C":
                        for p in range(NP):
                            if p == NP - 1:
                                ready(dt_exp)
                                do(dt_log, acb[:], acb[:], ACT.Ln, bias=1.0)
                            ready(f_gate, p)
                            do(f_log, b[:, p, :], b[:, p, :], ACT.Ln)
                        conv_tanh("C")
                    if n == Q0:
                        ready(f_sum, NP - 1)
                        do(decay, dch[:].rearrange("p a j -> p (a j)"),
                           b[:].rearrange("p a t -> p (a t)")[:, CH - 1:NP * T:CH], ACT.Exp)
                        plain_tanh("q", 0)
                        hg_exps(0)
                    if n == Q0 + 1:
                        ready(b_turned)
                        do(b_tok, bt[:].rearrange("p c n -> p (c n)"), bank(3), ACT.Copy)
                    if n in (9, 11, 13):
                        p = (n - 9) // 2
                        plain_tanh("q", p + 1)
                        hg_copies(p)
                        hg_exps(p + 1)
                    if n == 10:
                        ready(to_end)
                        do(to_end_exp, wend[:], wend[:], ACT.Exp)
                    if n == 15:
                        plain_tanh("g", 0)
                        hg_copies(3)
                    if n in (12, 14, 16):
                        hg_out((n - 12) // 2)
                    if kind == "xs":
                        conv_tanh(pr)
                    if kind == "z":
                        plain_tanh("z", pr)
                        if pr == 0:
                            hg_out(3)
                        ssd_exps(pr)
                    if n == 20:
                        hg_hi(0)
                    if kind == "g" and pr:
                        plain_tanh("g", pr)
                        if pr == 2:
                            ssd_hi(0)
                            ssd_hi(1)
                        hg_hi(pr)
                        if pr == 2:
                            ssd_sq(3)
                ssd_hi(2)
                ssd_hi(3)
                for m in range(KD):
                    hi(OUT0 + m + NS)
                    residual(l, KD + m, par[:, WN + KD + m:WN + KD + m + 1])
                ffn(1, FFN2, 2 * KD, WN + 2 * KD)

            act.wait_ge(norm_rms.sem, norm_rms.upto(DEPTH, 0))
            for i, (half, c) in enumerate(OUT_PIECES):
                if i % 2 == 0:
                    act.wait_ge(out_turned.sem, i + 1)
                    act.activation(stage[:, c, half * T:half * T + T], bank(OUT_BANKS[i]), ACT.Copy,
                                   scale=rt[:, c:c + 1]).then_inc(out_act.sem, 1)

        @block.vector
        def _(dve):
            own = Steps(dve, dve_step)
            did, settle = own.did, own.settle
            tt, ts, stt = dve.tensor_tensor, dve.tensor_scalar, dve.scalar_tensor_tensor

            def rsqrt(e, rms, parts, src, scale):
                n, dst = src.shape[1], rms[:]
                ms, tmp = ntn[:, 0, 0:n], ntn[:, 1, 0:n]
                did(ts(ms, src, scale, EPS, ALU.mult, ALU.add))
                settle()
                did(ts(dst.bitcast(I32), ms.bitcast(I32), -0.5, MAGIC, ALU.mult, ALU.add))
                for step in range(3):
                    settle()
                    did(stt(tmp, dst, -0.5, dst, ALU.mult, ALU.mult))
                    settle()
                    did(tt(tmp, tmp, ms, ALU.mult))
                    settle()
                    ins = stt(dst, tmp, 1.5, dst, ALU.add, ALU.mult)
                    if step < 2 or parts is not None:
                        did(ins)
                    else:
                        ins.then_inc(e.sem, 1)
                if parts is None:
                    return
                settle()
                did(dve.tensor_copy(parts[:, 0, :], dst))
                settle()
                tt(parts[:, 1, :], dst, parts[:, 0, :].bitcast(F32), ALU.subtract).then_inc(e.sem, 1)

            def residual(l, k, gain, update):
                update(k % KD).then_inc(x_tile.sem, 1)
                low_and_sum(l, k, gain)

            def low_and_sum(l, k, gain):
                m = k % KD
                dve.wait_ge(x_high.sem, x_high.upto(l, k))
                stt(hlo[:, m, :], x[:, m, :], gain, hhi[:, m, :].bitcast(F32), ALU.mult, ALU.subtract)\
                    .then_inc(x_low.sem, 1)
                dve.wait_ge(x_sq.sem, x_sq.upto(l, k))
                if m == 0:
                    dve.tensor_copy(acc[:], sq[:]).then_inc(x_sum.sem, 1)
                else:
                    dve.wait_ge(x_sum.sem, x_sum.upto(l, k - 1))
                    tt(acc[:], acc[:], sq[:], ALU.add).then_inc(x_sum.sem, 1)

            def norm(l, ph):
                dve.wait_ge(norm_sum.sem, norm_sum.upto(l, ph))
                rsqrt(norm_rms, rt, rt2, bank(NORM)[:, 0:TC], 1.0 / D)

            def norm_copy(l, ph):
                dve.wait_ge(norm_spread.sem, norm_spread.upto(l, ph))
                did(dve.tensor_copy(r[:], bank(NORM)))

            for e, n in ((g_out, 2), (u_out, 2), (proj_out, 3), (x_tile, 2), (tanh_used, 2)):
                for _ in range(n):
                    dve.sem_inc(e.sem, 1)

            dve.wait_ge(loaded.sem, 48)
            did(dve.tensor_copy(lt[:, 0, :], lg[:, 0, :]))
            for d in range(1, DEPTH):
                settle()
                did(tt(lt[:, 0, :], lt[:, 0, :], lg[:, d, :], ALU.max))
            settle()
            tt(lg[:], lg[:], lt[:, 0:1, :].to_broadcast([P, DEPTH, NP]), ALU.subtract).then_inc(lg_max.sem, 1)
            did(ts(par_all[:, :, CW:SN], par_all[:, :, CW:SN], 0.5, None, ALU.mult))
            dve.wait_ge(lg_exp.sem, 2)
            did(ts(par_all[:, :, NEGA:NEGA + 1], par_all[:, :, NEGA:NEGA + 1], -1.0, None, ALU.mult))
            did(dve.tensor_copy(lt[:, 0, :], lg[:, 0, :]))
            for d in range(1, DEPTH):
                settle()
                did(tt(lt[:, 0, :], lt[:, 0, :], lg[:, d, :], ALU.add))
            settle()
            did(dve.reciprocal(lt[:, 1, :], lt[:, 0, :]))
            settle()
            did(tt(lg[:], lg[:], lt[:, 1:2, :].to_broadcast([P, DEPTH, NP]), ALU.mult))
            settle()
            did(dve.tensor_copy(lt[:, 2, :], lg[:, 0, :]))
            for d in range(DEPTH):
                settle()
                if d:
                    did(tt(lt[:, 2, :], lt[:, 2, :], lg[:, d, :], ALU.add))
                    settle()
                did(tt(par_all[:, d, LB:LB + NP], lt[:, 2, :], lg[:, 0, :], ALU.subtract))
            settle()
            did(ts(par_all[:, :, OLB:OLB + NP], par_all[:, :, LB:LB + NP], -1.0, 1.0, ALU.mult, ALU.add))
            dve.wait_ge(consts.sem, 10)

            def turned_in(m):
                dve.wait_ge(x_turned.sem, m + 1)
                dve.tensor_copy(x[:, m, :], bank(DOWN + m % 4)).then_inc(x_tile.sem, 1)

            turned_in(0)
            for m in range(KD):
                if m + 1 < KD:
                    turned_in(m + 1)
                low_and_sum(0, m - KD, first[:, m:m + 1])
            did(dve.tensor_copy(identr[:], ident[:]))
            ahead = own.n

            with dve.Fori(0, DEPTH) as l:
                own.base, own.n = l * DVE_STEPS + ahead, 0
                dve.wait_ge(dve_step, own.base)
                dve.wait_ge(x_low.sem, x_low.upto(l, -1))
                dve.tensor_copy(par[:], par_all[:, l, :]).then_inc(par_set.sem, 1)
                dve.wait_ge(par_set.sem, par_set.upto(l, 0))

                def ready(e, k=0):
                    dve.wait_ge(e.sem, e.upto(l, k))

                def made(e, ins):
                    ins.then_inc(e.sem, 1)

                def alone():
                    settle()
                    did(dve.memset(spare[:], 0.0))

                def col(c):
                    return par[:, c:c + 1]

                def ffn(c, wb, k0, gain0):
                    norm(l, 2 * c)
                    norm_copy(l, 2 * c)
                    alone()
                    with dve.Fori(0, NJ // 2) as i:
                        for jj in range(2):
                            k = NJ * c + jj
                            dve.wait_ge(blk.sem, blk.upto(l, wb + 2 * jj) + NS * i)
                            made(g_out, tt(g2[:, jj, :], bank(jj), r[:], ALU.mult))
                            dve.wait_ge(blk.sem, blk.upto(l, wb + 2 * jj + 1) + NS * i)
                            made(u_out, tt(u2[:, jj, :], bank(2 + jj), r[:], ALU.mult))
                            dve.wait_ge(u_out.sem, u_out.upto(l, k) + 2 * i)
                            dve.wait_ge(silu_g.sem, silu_g.upto(l, k) + 2 * i)
                            made(hid, tt(u2[:, jj, :], g2[:, jj, :], u2[:, jj, :], ALU.mult))
                            dve.wait_ge(hid_high.sem, hid_high.upto(l, k) + 2 * i)
                            made(hid_low, tt(alo[:, 2 * i + jj, :], u2[:, jj, :],
                                             ahi[:, 2 * i + jj, :].bitcast(F32), ALU.subtract))
                    for m in range(KD):
                        def down(m):
                            ready(blk, wb + UP_BLOCKS + 3 * m + 2)
                            return stt(x[:, m, :], bank(DOWN + m % 2), 0.5, x[:, m, :], ALU.mult, ALU.add)
                        residual(l, k0 + m, col(gain0 + m), down)

                ffn(0, 0, 0, WN)

                norm(l, 1)

                def evac(n):
                    kind, p = PROJ[n]
                    ready(blk, LAST_BLOCK[n])
                    src = bank(n % 3)
                    if kind == "f":
                        made(proj_out, tt(g2[:, p % 2, :], src, r[:], ALU.mult))
                    elif kind == "dt":
                        made(proj_out, tt(dtb[:], src[0:8, :], r[0:8, :], ALU.mult))
                    elif kind in ("B", "C", "xs"):
                        made(proj_out, tt(xr[:, 3:T + 3], src, r[:], ALU.mult))
                    elif kind == "i":
                        made(proj_out, tt(vf[:], src, r[:], ALU.mult))
                    else:
                        before = [t for t in TANHS[:TANHS.index((kind, p))] if t[0] != "cv"]
                        if before:
                            ready(tanh_used, TANHS.index(before[-1]))
                        made(proj_out, stt(g2[:, 0, :], src, 0.5, r[:], ALU.mult, ALU.mult))

                def silu(kind, half, dst, e=None):
                    i = TANHS.index(kind)
                    ready(tanh, i)
                    made(tanh_used, stt(dst, th[:, i % 2, :], 1.0, half, ALU.add, ALU.mult))

                def gate_f(p):
                    ready(f_exp, p)
                    did(ts(t1[:], km[:, p, :], BIG, 1.0, ALU.min, ALU.add))
                    settle()
                    did(dve.reciprocal(acc[:], t1[:]))
                    settle()
                    did(stt(km[:, p, :], km[:, p, :], BIG, acc[:], ALU.min, ALU.mult))
                    made(f_gate, ts(b[:, p, :], acc[:], col(OLB + p), col(LB + p), ALU.mult, ALU.add))

                def scan_f(p):
                    ready(f_log, p)
                    made(f_sum, dve.tensor_tensor_scan(b[:, p, :], keep16[:], b[:, p, :], 0.0,
                                                       ALU.mult, ALU.add))

                def dt_first():
                    ready(proj_out, AT["dt", 0])
                    did(ts(dtb[:], dtb[:], par[0:8, DTB:DTB + 1], None, ALU.add))
                    settle()
                    made(dt_abs, stt(acb[:], dtb[:], -1.0, dtb[:], ALU.mult, ALU.min))

                def dt_rest():
                    ready(dt_log)
                    did(stt(dtb[:], dtb[:], 0.0, acb[:], ALU.max, ALU.add))
                    settle()
                    did(ts(acb[:], dtb[:], par[0:8, NEGA:NEGA + 1], None, ALU.mult))
                    settle()
                    for c in range(TC):
                        a = acb[:, c * P:(c + 1) * P]
                        ins = dve.tensor_tensor_scan(a, ones[0:8, :], a, 0.0, ALU.mult, ALU.add)
                        if c < TC - 1:
                            did(ins)
                        else:
                            made(dt_sum, ins)

                def convolve(t, n):
                    dst = {"B": bf[:], "C": cf[:]}[t] if isinstance(t, str) else xs[:, t % 2, :]
                    i = {"B": CONV_B, "C": CONV_C}.get(t, t)
                    ready(proj_out, n)
                    did(ts(dst, xr[:, 0:T], col(CW + 4 * i), col(CB + i), ALU.mult, ALU.add))
                    for k in range(1, 4):
                        settle()
                        ins = stt(dst, xr[:, k:T + k], col(CW + 4 * i + k), dst, ALU.mult, ALU.add)
                        if k < 3:
                            did(ins)
                        else:
                            made(conv, ins)
                    ready(conv, CONVS.index(t))

                def conv_out(t):
                    dst = {"B": bf[:], "C": cf[:]}[t] if isinstance(t, str) else xs[:, t % 2, :]
                    silu(("cv", t), dst, dst)

                def hg_dist(p):
                    if p >= 2:
                        ready(score, 2 * p - 3)
                    ready(f_sum, p)
                    bb = b[:, p, :].rearrange("p (c i) -> p c i", i=CH)
                    made(dist, tt(e1[p % 2][:].rearrange("p (c i) -> p c i", i=CH), bb,
                                  bb[:, :, CREF:CREF + 1].to_broadcast([P, T // CH, CH]), ALU.subtract))
                    made(dist, tt(e4[p % 2][:].rearrange("p (c i) -> p c i", i=CH),
                                  bb[:, :, CH - 1:CH].to_broadcast([P, T // CH, CH]), bb, ALU.subtract))

                def hg_q(p):
                    ready(proj_out, AT["q", p])
                    silu(("q", p), g2[:, 0, :], g2[:, 1, :])
                    ready(tanh_used, TANHS.index(("q", p)))
                    ready(hexp, 4 * p + 1)
                    made(hmul, tt(e1[p % 2][:], g2[:, 1, :], e1[p % 2][:], ALU.mult))
                    ready(hexp, 4 * p + 2)
                    made(hmul, tt(e3[p % 2][:], g2[:, 1, :], e3[p % 2][:], ALU.mult))

                def hg_k(p):
                    made(hmul, stt(e2[p % 2][:], km[:, p, :], col(OLB + p), e2[p % 2][:], ALU.mult, ALU.mult))
                    ready(hexp, 4 * p + 3)
                    made(hmul, stt(e4[p % 2][:], km[:, p, :], col(OLB + p), e4[p % 2][:], ALU.mult, ALU.mult))

                def hg_tables():
                    ready(decay)
                    did(dve.tensor_copy(f2[:, :, 0:CT:4], dch[:, :, 1:CT:4]))
                    did(dve.tensor_copy(f2[:, :, 3:CT:4], dch[:, :, 2:CT:4]))
                    for j in range(1, CT):
                        did(tt(to_q[:, :, j], to_q[:, :, j - 1], dch[:, :, j - 1], ALU.mult))
                        did(tt(to_k[:, :, CT - 1 - j], to_k[:, :, CT - j], dch[:, :, CT - j], ALU.mult))
                        if j < CT // 2:
                            m = CT // 2 + j
                            did(tt(f1[:, :, m], f1[:, :, m - 1], dch[:, :, m - 1], ALU.mult))
                            m = CT // 2 - 1 - j
                            did(tt(f1[:, :, m], f1[:, :, m + 1], dch[:, :, m + 1], ALU.mult))
                        settle()
                    did(tt(dtile[:], to_q[:, :, CT - 1], dch[:, :, CT - 1], ALU.mult))

                def hg_levels(p):
                    ready(hmul, 4 * p + 3)
                    settle()
                    if p:
                        ready(turned, 2 * p - 2)
                    if p >= 2:
                        ready(o_done, p - 2)

                    def by_chunk(ap, j=CT):
                        return ap.rearrange("p (c j i) -> p c j i", j=j, i=CH)

                    def times(dst, src, table, cs, js, j=CT):
                        f = table[:, TC * p:TC * p + TC, :]
                        if j != CT:
                            f = f.rearrange("p c (g j) -> p (c g) j", j=j)
                        f = f[:, cs, js]
                        made(level, tt(by_chunk(dst, j)[:, cs, js, :], by_chunk(src, j)[:, cs, js, :],
                                       f.unsqueeze(3).to_broadcast([*f.shape, CH]), ALU.mult))

                    times(ks[:], e4[p % 2][:], to_k, slice(0, TC - 1), slice(0, CT))
                    times(w1[p % 2][:], e4[p % 2][:], f1, slice(0, TC), slice(0, CT // 2))
                    times(w1[p % 2][:], e3[p % 2][:], f1, slice(0, TC), slice(CT // 2, CT))
                    times(w2[p % 2][:], e4[p % 2][:], f2, slice(0, 2 * TC), slice(0, 2), 4)
                    times(w2[p % 2][:], e3[p % 2][:], f2, slice(0, 2 * TC), slice(2, 4), 4)
                    times(qs[:, p % 2, :], e3[p % 2][:], to_q, slice(1, TC), slice(0, CT))

                def hg_mask(p):
                    if p >= 2:
                        ready(o_done, p - 2)
                    for h in range(2):
                        ready(score, 2 * p + h)
                        alone()
                        made(score_masked, dve.copy_predicated(
                            in_tiles(sm[:, p % 2, h, :]),
                            causal[:].bitcast(I32).unsqueeze(1).to_broadcast([P, TC, P]),
                            in_tiles(bank(5 + h))))

                def hg_states(p):
                    ready(contrib, p)
                    did(dve.tensor_copy(hs[:, 0, :], bank(3)[:, 0:HALF]))
                    for c in range(1, TC - 1):
                        settle()
                        ins = stt(hs[:, c, :], hs[:, c - 1, :], dtile[:, TC * p + c:TC * p + c + 1],
                                  bank(3)[:, HALF * c:HALF * c + HALF], ALU.mult, ALU.add)
                        if c < TC - 2:
                            did(ins)
                        else:
                            made(state, ins)

                def dt_out():
                    ready(dt_turned)
                    made(dt_tok, dve.tensor_copy(dts[:].rearrange("p a c h -> p (a c h)"),
                                                 bank(4)[:, 0:2 * TC * 8]))

                def cb_mask():
                    for g in range(2):
                        ready(cb, g)
                        made(cb_masked, tt(cbm[:, g], in_tiles(bank(5 + g)),
                                           causal[:].unsqueeze(1).to_broadcast([P, TC, P]), ALU.mult))

                def by_head(ap, p):
                    return ap[:, :, 2 * p:2 * p + 2].unsqueeze(3).to_broadcast([P, TC, 2, HALF])

                def ends():
                    ready(last_sums)
                    made(to_end, tt(wend[:], bank(7)[:, 0:TC * 8].rearrange("p (c h) -> p c h", c=TC), dts[:, 1],
                                    ALU.subtract))

                def end_weights():
                    ready(to_end_exp)
                    did(tt(wend[:], wend[:], dts[:, 0], ALU.mult))

                def ssd_main(p):
                    g = p // 2
                    gg = slice(HALF * g, HALF * g + HALF)
                    xtok = bank(3).rearrange("p (c h n) -> p c h n", c=TC, h=2)
                    ready(x_tok, p)
                    if p == 0:
                        settle()
                    made(xde_made, tt(xde[:].rearrange("p c (h n) -> p c h n", h=2), xtok,
                                      by_head(wend[:], p), ALU.mult))
                    if p:
                        ready(y_done, p - 1)
                    made(xdt_made, tt(xdt[:].rearrange("p c (h n) -> p c h n", h=2), xtok,
                                      by_head(dts[:, 0], p), ALU.mult))
                    for h in range(2):
                        ready(sums_exp, 2 * p + h)
                        made(cx_made, tt(cx[gg, h, :], cf[gg, :], eh[gg, h, :], ALU.mult))
                    for h in range(2):
                        ready(seg_exp, 2 * p + h)
                        made(lm_made, tt(in_tiles(lm[:, h, :]), in_tiles(lm[:, h, :]), cbm[:, g], ALU.mult))

                def ssd_states(p):
                    g = p // 2
                    gg = slice(HALF * g, HALF * g + HALF)
                    ready(s_contrib, p)
                    did(dve.tensor_copy(st[gg, 1, :], bank(6)[gg, 0:P]))
                    for c in range(2, TC):
                        for h in range(2):
                            hh = slice(HALF * h, HALF * h + HALF)
                            if h == 0:
                                settle()
                            ins = stt(st[gg, c, hh], st[gg, c - 1, hh], eh[gg, h, c * P - P + P - 1:c * P - P + P],
                                      bank(6)[gg, (c - 1) * P + HALF * h:(c - 1) * P + HALF * h + HALF],
                                      ALU.mult, ALU.add)
                            if c == TC - 1 and h == 1:
                                made(s_state, ins)
                            else:
                                did(ins)

                def ssd_gate(p):
                    ready(y_done, p)
                    if p == 3:
                        ready(ssd_low, 0)
                    did(stt(y2[:, p % 3, :], xs[:, p % 2, :], col(DC + p), bank(7), ALU.mult, ALU.add))
                    settle()
                    made(y_gated, tt(y2[:, p % 3, :], y2[:, p % 3, :], zs[:, p % 2, :], ALU.mult))

                def group_rsqrt(g):
                    ready(group_sum, g)
                    rsqrt(group_norm, rg, rg2, bank(6)[:, GROUP0:GROUP0 + TC], 1.0 / (SSD_W // 2))

                def ssd_norm(p):
                    ready(group_spread, p // 2)
                    made(ssd_y, stt(y2[:, p % 3, :], y2[:, p % 3, :], col(SN + p), bank(7), ALU.mult, ALU.mult))

                def ssd_lo(p):
                    ready(ssd_high, p)
                    made(ssd_low, tt(slo[:, p, :], y2[:, p % 3, :], shi[:, p, :].bitcast(F32), ALU.subtract))

                def hg_norm(p, bk):
                    ready(head_spread, p)
                    made(head_used, stt(b[:, p, :], b[:, p, :], col(HN), bank(bk), ALU.mult, ALU.mult))
                    ready(head_used, p)

                def hg_gate(p):
                    ready(tanh_used, TANHS.index(("g", p)))
                    made(hg_y, tt(b[:, p, :], b[:, p, :], gs[:, p % 2, :], ALU.mult))

                def hg_lo(p):
                    ready(hg_high, p)
                    if p == 3:
                        ready(group_sum, 1)
                    made(hg_low, tt(olo[p][:], b[:, p, :], ohi[:, p, :].bitcast(F32), ALU.subtract))

                did(dve.memset(xr[:, 0:3], 0.0))
                for t in (to_q, to_k, f1, f2):
                    did(dve.memset(t[:].rearrange("p a j -> p (a j)"), 1.0))
                norm_copy(l, 1)
                settle()
                for n, (kind, pr) in enumerate(PROJ):
                    evac(n)
                    if n == 10:
                        ready(cleared)
                    if n == 5:
                        dt_first()
                    if n in (1, 2, 4, 5):
                        gate_f((1, 2, 4, 5).index(n))
                    if kind in ("B", "C"):
                        convolve(kind, n)
                    if n == 3:
                        conv_out("B")
                    if kind == "C":
                        dt_rest()
                        conv_out("C")
                        for p in range(NP):
                            scan_f(p)
                    if n == Q0:
                        hg_dist(0)
                        hg_q(0)
                    if n == Q0 + 1:
                        dt_out()
                        hg_k(0)
                        hg_tables()
                        hg_levels(0)
                        cb_mask()
                        did(dve.tensor_copy(acb_hi[:], acb[:]))
                        settle()
                        made(acb_split, tt(acb_lo[:], acb[:], acb_hi[:].bitcast(F32), ALU.subtract))
                    if n in (9, 11, 13):
                        p = (n - 9) // 2
                        if p == 0:
                            ends()
                        hg_dist(p + 1)
                        hg_q(p + 1)
                    if n in (10, 12, 14):
                        p = (n - 10) // 2
                        if p == 0:
                            end_weights()
                        hg_mask(p)
                        hg_states(p)
                        hg_k(p + 1)
                        hg_levels(p + 1)
                    if n == 15:
                        ready(proj_out, n)
                        silu(("g", 0), g2[:, 0, :], gs[:, 0, :])
                    if kind == "xs":
                        if pr == 0:
                            hg_mask(3)
                            hg_states(3)
                        convolve(pr, n)
                        conv_out(pr)
                        if pr:
                            ssd_states(pr - 1)
                        if pr == 1:
                            ready(head_sum)
                            rsqrt(head_norm, rh, None, bank(7)[:, 0:TC * 8], 1.0 / HALF)
                        if pr == 2:
                            hg_norm(0, 3)
                            hg_gate(0)
                            hg_lo(0)
                        if pr == 3:
                            hg_norm(1, 3)
                            group_rsqrt(0)
                    if kind == "z":
                        ready(proj_out, n)
                        silu(("z", pr), g2[:, 0, :], zs[:, pr % 2, :])
                        if pr:
                            ssd_gate(pr - 1)
                        ssd_main(pr)
                    if kind == "g" and pr in (1, 2):
                        ready(proj_out, n)
                        silu(("g", pr), g2[:, 0, :], gs[:, pr % 2, :])
                        if pr == 1:
                            ssd_states(3)
                        hg_gate(pr)
                        if pr == 1:
                            ssd_norm(0)
                            ssd_norm(1)
                            hg_norm(2, 3)
                            hg_norm(3, 4)
                            hg_lo(1)
                        else:
                            ssd_lo(0)
                            ssd_lo(1)
                            hg_lo(2)
                            ssd_gate(3)
                group_rsqrt(1)
                silu(("g", 3), g2[:, 0, :], gs[:, 1, :])
                hg_gate(3)
                ssd_norm(2)
                ssd_norm(3)
                hg_lo(3)
                ssd_lo(2)
                ssd_lo(3)
                for m in range(KD):
                    def mixed(m):
                        ready(blk, OUT0 + m)
                        return stt(x[:, m, :], bank(DOWN + m % 2), 1.0, x[:, m, :], ALU.mult, ALU.add)
                    residual(l, KD + m, col(WN + KD + m), mixed)
                ffn(1, FFN2, 2 * KD, WN + 2 * KD)
                assert own.n == DVE_STEPS, own.n

            own.base, own.n = ahead + DEPTH * DVE_STEPS, 0
            dve.wait_ge(norm_sum.sem, norm_sum.upto(DEPTH, 0))
            rsqrt(norm_rms, rt, None, bank(NORM)[:, 0:TC], 1.0 / D)
            dve.wait_ge(norm_rms.sem, norm_rms.upto(DEPTH, 0))
            for i, (half, c) in enumerate(OUT_PIECES):
                if i % 2:
                    dve.wait_ge(out_turned.sem, i + 1)
                    dve.tensor_scalar(stage[:, c, half * T:half * T + T], bank(OUT_BANKS[i]), rt[:, c:c + 1], None,
                                      ALU.mult).then_inc(out_dve.sem, 1)

        @block.tensor
        def _(pe):
            mm = pe.matmul
            pe.wait_ge(consts.sem, 10)
            for m in range(KD):
                pe.wait_ge(x_part[m // 2].sem, 16)
                if m >= 4:
                    pe.wait_ge(x_tile.sem, x_tile.upto(0, m - KD - 4))
                for c in range(TC):
                    last = pe.transpose(bank(DOWN + m % 4)[:, c * P:(c + 1) * P], stage[:, c, m * P:(m + 1) * P],
                                        ident[:])
                last.then_inc(x_turned.sem, 1)

            def products(dst, q, piece, moving, start, stop):
                s = slice(piece * P, piece * P + P)
                mh, ml = moving
                mm(dst, whi[:, q, s], mh, start=start, stop=False)
                mm(dst, whi[:, q, s], ml, start=False, stop=False)
                return mm(dst, wlo[:, q, s], mh, start=False, stop=stop)

            def norm_products(l, ph):
                pe.wait_ge(x_sum.sem, x_sum.upto(l, KD * ph - 1))
                for c in range(TC):
                    last = mm(bank(NORM)[:, c:c + 1], acc[:, c * P:(c + 1) * P], ones[:, 0:1],
                              start=True, stop=True)
                last.then_inc(norm_sum.sem, 1)

            def spread(e, dst, parts):
                for c in range(TC):
                    for part in range(2):
                        last = mm(dst[:, c * P:(c + 1) * P], parts[:, part, c:c + 1].to_broadcast([P, P]), identr[:],
                                  start=part == 0, stop=part == 1)
                last.then_inc(e.sem, 1)

            def norm_spreads(l, ph):
                pe.wait_ge(norm_rms.sem, norm_rms.upto(l, ph))
                spread(norm_spread, bank(NORM), rt2)

            def h_tile(k):
                return hhi[:, k, :], hlo[:, k, :]

            with pe.Fori(0, DEPTH) as l:
                def ready(e, k=0):
                    pe.wait_ge(e.sem, e.upto(l, k))

                def norm_steps(ph, n, k):
                    if n == 0 and k in (0, KD - 1):
                        ready(x_low, KD * ph - KD + (KD - 2 if k == 0 else KD - 1))
                    if (n, k) == (0, 5):
                        norm_products(l, ph)
                    if (n, k) == (1, 3):
                        norm_spreads(l, ph)

                def ffn(c, wb):
                    ph = 2 * c

                    def begin(i, q):
                        jj, kind = q // 2, q % 2
                        free = (g_out, u_out)[kind]
                        pe.wait_ge(free.sem, free.upto(l, NJ * c + jj - 2) + 2 * i)
                        pe.wait_ge(split.sem, split.upto(l, wb + q) + NS * i)

                    def tile_products(q, k):
                        return products(bank(2 * (q % 2) + q // 2), q, k, h_tile(k), k == 0, k == KD - 1)

                    def up_staggered():
                        for step in range(KD + NS - 1):
                            for q in range(NS):
                                k = step - q
                                if k == 0:
                                    begin(0, q)
                                if q == 0 and k < KD:
                                    ready(x_low, KD * ph - KD + k)
                                if 0 <= k < KD:
                                    last = tile_products(q, k)
                                if k == KD - 1:
                                    last.then_inc(blk.sem, 1)
                            if step == KD - 2:
                                norm_products(l, ph)
                            if step == KD:
                                norm_spreads(l, ph)

                    def up(i, peeled):
                        for q in range(NS):
                            begin(i, q)
                            for k in range(KD):
                                if peeled:
                                    norm_steps(ph, q, k)
                                last = tile_products(q, k)
                            last.then_inc(blk.sem, 1)

                    if c == 0:
                        up_staggered()
                    else:
                        up(0, True)
                    with pe.Fori(1, NJ // 2) as i:
                        up(i, False)
                    with pe.Fori(0, 2) as i:
                        for mm4 in range(4):
                            pe.wait_ge(x_tile.sem, x_tile.upto(l, KD * ph + mm4 - 2) + 4 * i)
                            for s, (j0, j1) in enumerate(DN_PIECES):
                                w = wb + UP_BLOCKS + 3 * mm4 + s
                                ready(hid_low, NJ * c + j1 - 1)
                                pe.wait_ge(split.sem, split.upto(l, w) + 12 * i)
                                for j in range(j0, j1):
                                    last = products(bank(DOWN + mm4 % 2), w % NS, j - j0,
                                                    (ahi[:, j, :], alo[:, j, :]), j == 0, j == NJ - 1)
                                last.then_inc(blk.sem, 1)

                ffn(0, 0)

                def cols_of(c):
                    return slice(c * P, (c + 1) * P)

                def common():
                    ready(dt_sum)
                    ready(tanh_used, TANHS.index(("cv", "B")))
                    for c in range(TC):
                        last = pe.transpose(bank(3)[:, cols_of(c)], bf[:, cols_of(c)], ident[:])
                    last.then_inc(b_turned.sem, 1)
                    for a, src in enumerate((dtb, acb)):
                        for c in range(TC):
                            last = pe.transpose(bank(4)[:, a * 32 + c * 8:a * 32 + c * 8 + 8],
                                                src[:, cols_of(c)], ident[0:8, 0:8])
                    last.then_inc(dt_turned.sem, 1)
                    ready(tanh_used, TANHS.index(("cv", "C")))
                    for g in range(2):
                        gg = slice(HALF * g, HALF * g + HALF)
                        for c in range(TC):
                            last = mm(bank(5 + g)[:, cols_of(c)], bf[gg, cols_of(c)], cf[gg, cols_of(c)],
                                      start=True, stop=True)
                        last.then_inc(cb.sem, 1)

                def chunk_ends():
                    ready(dt_tok)
                    mm(bank(7)[:, 0:TC * 8], ident[:, P - 1:P].to_broadcast([P, P]),
                       dts[:, 1].rearrange("p c h -> p (c h)"), start=True, stop=True).then_inc(last_sums.sem, 1)

                def hg_turn(p):
                    ready(level, 6 * p)
                    if p == 0:
                        ready(b_tok)
                        ready(dt_tok)
                    else:
                        ready(state, p - 1)
                    for c in range(TC - 1):
                        last = pe.transpose(bank(3)[:, cols_of(c)], ks[:, cols_of(c)], ident[:])
                    last.then_inc(turned.sem, 1)
                    ready(proj_out, AT["i", p])
                    for c in range(TC):
                        last = pe.transpose(bank(4)[:, cols_of(c)], vf[:, cols_of(c)], ident[:])
                    last.then_inc(turned.sem, 1)

                def hg_scores(p, k):
                    h, c = k // TC, k % TC
                    hh = slice(HALF * h, HALF * h + HALF)
                    if k == 0:
                        ready(level, 6 * p + 4)
                        if p:
                            ready(score_masked, 2 * p - 1)
                        else:
                            ready(cb_masked, 1)

                    def scores(s0, t0, n, keys, queries):
                        c0 = c * P
                        return mm(bank(5 + h)[s0:s0 + n, c0 + t0:c0 + t0 + n],
                                  keys[p % 2][hh, c0 + s0:c0 + s0 + n], queries[p % 2][hh, c0 + t0:c0 + t0 + n],
                                  start=True, stop=True)

                    scores(0, 0, P, e2, e1)
                    for s0 in range(0, P, 2 * CH):
                        scores(s0, s0 + CH, CH, e4, e3)
                    for s0 in range(0, P, 4 * CH):
                        scores(s0, s0 + 2 * CH, 2 * CH, w2, w2)
                    last = scores(0, 4 * CH, 4 * CH, w1, w1)
                    if c == TC - 1:
                        last.then_inc(score.sem, 1)

                def hg_contribs(p):
                    ready(kd_tok, p)
                    ready(v_tok, p)
                    for c in range(TC - 1):
                        for h in range(2):
                            hh = slice(HALF * h, HALF * h + HALF)
                            last = mm(bank(3)[hh, HALF * c:HALF * c + HALF], kdt[:, c, hh], vt[:, p % 2, c, hh],
                                      start=True, stop=True)
                    last.then_inc(contrib.sem, 1)

                def hg_outs(p, k):
                    h, c = k // TC, k % TC
                    hh = slice(HALF * h, HALF * h + HALF)
                    if k == 0:
                        ready(state, p)
                        ready(score_masked, 2 * p + 1)
                        ready(level, 6 * p + 5)
                        if p:
                            ready(o_out, 2 * p - 1)
                        else:
                            ready(to_end)
                    last = mm(bank(7)[hh, cols_of(c)], vt[:, p % 2, c, hh], sm[:, p % 2, h, cols_of(c)],
                              start=c == 0, stop=False, skip_group_check=True)
                    if c:
                        last = mm(bank(7)[hh, cols_of(c)], hs[hh, c - 1, :], qs[hh, p % 2, cols_of(c)],
                                  start=False, stop=c == TC - 1, skip_group_check=True)
                    if k == 2 * TC - 1:
                        last.then_inc(o_done.sem, 1)

                def ssd_turn(p):
                    ready(tanh_used, TANHS.index(("cv", p)))
                    ready(dt_tok)
                    if p == 0:
                        ready(state, NP - 1)
                        ready(score_masked, 2 * NP - 1)
                        ready(acb_split)
                    elif p in (2, 3):
                        ready(head_used, p - 2)
                    if p:
                        ready(xde_made, p - 1)
                        ready(seg, TC * 2 * p - 1)
                    for c in range(TC):
                        last = pe.transpose(bank(3)[:, cols_of(c)], xs[:, p % 2, cols_of(c)], ident[:])
                    last.then_inc(x_tok.sem, 1)
                    for h in range(2):
                        k = 2 * p + h
                        pick = identr[0:8, k:k + 1].to_broadcast([8, P])
                        mm(bank(4 + h), pick, acb_hi[:], start=True, stop=False)
                        mm(bank(4 + h), pick, acb_lo[:], start=False, stop=True).then_inc(sums.sem, 1)

                def ssd_contribs(p):
                    gg = slice(HALF * (p // 2), HALF * (p // 2) + HALF)
                    ready(xde_made, p)
                    if p:
                        ready(s_state, p - 1)
                    if p == 3:
                        ready(group_norm, 0)
                    for c in range(TC - 1):
                        last = mm(bank(6)[gg, cols_of(c)], bt[:, c, gg], xde[:, c, :], start=True, stop=True)
                    last.then_inc(s_contrib.sem, 1)

                def ssd_outs(p):
                    gg = slice(HALF * (p // 2), HALF * (p // 2) + HALF)
                    ready(s_state, p)
                    ready(lm_made, 2 * p + 1)
                    if p == 0:
                        ready(head_norm)
                    elif p < 3:
                        ready(y_gated, p - 1)
                    else:
                        ready(ssd_y, 1)
                    for h in range(2):
                        hh = slice(HALF * h, HALF * h + HALF)
                        for c in range(TC):
                            mm(bank(7)[hh, cols_of(c)], xdt[:, c, hh], lm[:, h, cols_of(c)],
                               start=c == 0, stop=False, skip_group_check=True)
                        for c in range(1, TC):
                            last = mm(bank(7)[hh, cols_of(c)], st[gg, c, hh], cx[gg, h, cols_of(c)],
                                      start=False, stop=c == TC - 1, skip_group_check=True)
                    last.then_inc(y_done.sem, 1)

                def head_sums():
                    ready(o_out, 2 * NP - 1)
                    for c in range(TC):
                        for p in range(NP):
                            last = mm(bank(7)[:, 8 * c:8 * c + 8], km[:, p, cols_of(c)], headsum[:, 8 * p:8 * p + 8],
                                      start=p == 0, stop=p == NP - 1)
                    last.then_inc(head_sum.sem, 1)

                def head_spreads(p, bk):
                    ready(head_norm)
                    ready(xde_made, min(p + 1, 3))
                    ready(xdt_made, min(p + 1, 3))
                    ready(seg, TC * 2 * (min(p + 1, 3) + 1) - 1)
                    for h in range(2):
                        for c in range(TC):
                            k = 8 * c + 2 * p + h
                            last = mm(bank(bk)[HALF * h:HALF * h + HALF, cols_of(c)],
                                      rh[:, k:k + 1].to_broadcast([P, HALF]), ident[:], start=True, stop=True)
                    last.then_inc(head_spread.sem, 1)

                def group_sums(g):
                    ready(y_sq, 2 * g + 1)
                    ready(s_state, 2 * g + 1)
                    for c in range(TC):
                        dst = bank(6)[:, GROUP0 + c:GROUP0 + c + 1]
                        mm(dst, sq[:, cols_of(c)], ones[:, 0:1], start=True, stop=False)
                        last = mm(dst, sqb[:, cols_of(c)], ones[:, 0:1], start=False, stop=True)
                    last.then_inc(group_sum.sem, 1)

                def group_spreads(g):
                    ready(group_norm, g)
                    ready(y_gated, 2 + g)
                    spread(group_spread, bank(7), rg2)

                for i, (n, k0, k1) in enumerate(PBLOCKS):
                    w = MIX0 + i
                    ready(split, w)
                    if k0 == 0:
                        ready(proj_out, n - 3)
                    for k in range(k0, k1):
                        norm_steps(1, n, k)
                        last = products(bank(n % 3), w % NS, k - k0, h_tile(k), k == 0, k == KD - 1)
                        if k == k1 - 1:
                            last.then_inc(blk.sem, 1)
                        if n in (10, 12, 14, 16):
                            for i in SCORES_AT[k]:
                                hg_scores((n - 10) // 2, i)
                        if n in (11, 13, 15, 17) and k >= 4:
                            hg_outs((n - 11) // 2, 2 * (k - 4))
                            hg_outs((n - 11) // 2, 2 * (k - 4) + 1)
                    if k1 < KD:
                        continue
                    if n == 8:
                        common()
                    if n == 9:
                        chunk_ends()
                    if n in (9, 11, 13, 15):
                        hg_turn((n - 9) // 2)
                    if n in (10, 12, 14, 16):
                        hg_contribs((n - 10) // 2)
                    if n in (19, 21, 23, 25):
                        ssd_outs((n - 19) // 2)
                    if n in (17, 19, 21, 23):
                        ssd_turn((n - 17) // 2)
                    if n == 22:
                        group_sums(0)
                    if n in (18, 20, 22, 24):
                        ssd_contribs((n - 18) // 2)
                    if n == 18:
                        head_sums()
                    if n == 20:
                        head_spreads(0, 3)
                    if n == 22:
                        head_spreads(1, 3)
                    if n == 24:
                        head_spreads(2, 3)
                        head_spreads(3, 4)
                        group_spreads(0)

                SOON, LATE = (0, 1, 4, 5, 6), (7, 2, 3)

                def out_products(m, ks):
                    w = OUT0 + m
                    for k in ks:
                        if m == 0:
                            if k < NP:
                                ready(ssd_low, k)
                            else:
                                ready(hg_low, k - NP)
                        moving = ((shi[:, k, :], slo[:, k, :]) if k < NP
                                  else (ohi[:, k - NP, :], olo[k - NP][:]))
                        last = products(bank(DOWN + m % 2), w % NS, k, moving, k == SOON[0], k == LATE[-1])
                    return last

                group_sums(1)
                ready(head_used, 3)
                for m in (0, 1):
                    ready(split, OUT0 + m)
                    ready(x_tile, KD + m - 2)
                    out_products(m, SOON)
                    if m == 0:
                        group_spreads(1)
                for m in (0, 1):
                    out_products(m, LATE).then_inc(blk.sem, 1)
                for m in range(2, KD):
                    ready(split, OUT0 + m)
                    ready(x_tile, KD + m - 2)
                    out_products(m, SOON)
                    out_products(m, LATE).then_inc(blk.sem, 1)
                ffn(1, FFN2)

            for i, (half, c) in enumerate(OUT_PIECES):
                if i in (0, TC):
                    pe.wait_ge(x_low.sem, x_low.upto(DEPTH, half * KD // 2 - KD // 2 - 1))
                if i == TC:
                    norm_products(DEPTH, 0)
                if OUT_BANKS[i] == NORM:
                    pe.wait_ge(norm_rms.sem, norm_rms.upto(DEPTH, 0))
                for j in range(KD // 2):
                    m = half * (KD // 2) + j
                    dst = bank(OUT_BANKS[i])[:, j * P:(j + 1) * P]
                    mm(dst, hhi[:, m, c * P:(c + 1) * P], identr[:], start=True, stop=False)
                    last = mm(dst, hlo[:, m, c * P:(c + 1) * P], identr[:], start=False, stop=True)
                last.then_inc(out_turned.sem, 1)


def kernel(**inputs):
    import concourse.bacc as bacc
    from concourse.bass_utils import run_bass_kernel_spmd

    a = {k: np.asarray(v) for k, v in inputs.items()}

    def tile_cols(v):
        return np.moveaxis(v.reshape(*v.shape[:-1], -1, P), -1, -2)

    def k_major(w, j0, n):
        w = w[:, :, j0:j0 + n]
        return w.reshape(w.shape[0], -1, P, n).transpose(0, 2, 1, 3)

    def col_tiles(w):
        d, k, n = w.shape
        return w.reshape(d, k // P, P, n // P, P).transpose(0, 3, 2, 1, 4).reshape(d, n // P, P, k)

    def up(gate, up_):
        t = np.stack([col_tiles(gate), col_tiles(up_)], axis=2)
        return np.ascontiguousarray(t.reshape(DEPTH, UP_BLOCKS, P, BW))

    def rows8(v):
        out = np.zeros((DEPTH, P, 1), np.float32)
        out[:, :8, 0] = v
        return out

    following = np.concatenate([a["ffn1_norm"][1:], a["final_norm"][None]])
    cols = np.concatenate([
        tile_cols(a["mix_norm"]), tile_cols(a["ffn2_norm"]), tile_cols(following),
        a["ssd_conv_w"].reshape(DEPTH, 4, 6, P).transpose(0, 3, 2, 1).reshape(DEPTH, P, 24),
        tile_cols(a["ssd_conv_b"]), tile_cols(a["ssd_norm_w"]),
        tile_cols(np.repeat(a["ssd_d"], HALF, axis=1)),
        np.tile(a["hg_norm_w"], (1, 2))[:, :, None],
        rows8(a["ssd_dt_bias"]), rows8(a["ssd_a_log"]),
    ], axis=2)
    w_in = a["w_in"]
    starts, at = {}, 0
    for name, width in (("z", 512), ("xs", 512), ("B", 128), ("C", 128), ("dt", 8), ("q", 512), ("f", 512),
                        ("i", 512), ("g", 512)):
        starts[name], at = at, at + width
    blocks = [k_major(w_in, starts[kind] + P * p, P).reshape(DEPTH, P, BW) for kind, p in PROJ if kind != "dt"]
    up1 = up(a["ffn1_w_gate"], a["ffn1_w_up"])
    mix = np.concatenate([np.stack(blocks, axis=1), col_tiles(a["w_out"])], axis=1)
    arrays = {
        "x": a["x"], "cols": np.ascontiguousarray(cols.transpose(1, 0, 2)),
        "first_norm": np.ascontiguousarray(tile_cols(a["ffn1_norm"][0])),
        "logits": np.ascontiguousarray(tile_cols(a["hg_lb_logits"]).transpose(1, 0, 2)),
        "lead": np.concatenate([up1[:, :NS], up1[-1:, :NS]]), "up1": np.ascontiguousarray(up1[:, NS:]), "dn1": np.ascontiguousarray(col_tiles(a["ffn1_w_down"])),
        "mix": np.ascontiguousarray(mix), "dtw": np.ascontiguousarray(k_major(w_in, starts["dt"], 8)),
        "up2": up(a["ffn2_w_gate"], a["ffn2_w_up"]), "dn2": np.ascontiguousarray(col_tiles(a["ffn2_w_down"])),
    }
    nc = bacc.Bacc("TRN2", target_bir_lowering=False, num_devices=1)
    aps = [nc.dram_tensor(f"in_{k}", v.shape, mybir.dt.from_np(v.dtype), kind="ExternalInput").ap()
           for k, v in arrays.items()]
    out = nc.dram_tensor("out_0", a["x"].shape, F32, kind="ExternalOutput").ap()
    trunk_kernel(nc, *aps, out)
    r = run_bass_kernel_spmd(nc, [{f"in_{k}": v for k, v in arrays.items()}], core_ids=[0])
    return r.results[0]["out_0"]
```
